# Optimizing a Trainium2 kernel written in Bass

```python
import jax, jax.numpy as jnp
from jax import lax
import numpy as np

D_MODEL = 1024
BATCH = 1
SEQ = 1024
DEPTH = 1
DEC_BATCH = 8
DEC_SEQ = 1
PAST_LEN = 2048
PAGE_SIZE = 128

MIX_WIDTH = D_MODEL
MLA_WIDTH = D_MODEL // 2
GLA_WIDTH = MIX_WIDTH - MLA_WIDTH
MLA_HEADS = 4
MLA_V = MLA_WIDTH // MLA_HEADS
MLA_NOPE = 128
MLA_ROPE = 64
Q_RANK = (3 * D_MODEL) // 8
KV_RANK = D_MODEL // 4
MLA_SCALE = (MLA_NOPE + MLA_ROPE) ** -0.5
ROPE_THETA = 10000.0
Q_BLOCK = 128
GLA_HEADS = 4
GLA_DV = GLA_WIDTH // GLA_HEADS
GLA_DK = GLA_DV // 2
GATE_RANK = 16
GATE_TAU = 16.0
GLA_CHUNK = 64
D_FF = 4 * D_MODEL
ALPHA = (2.0 * DEPTH) ** 0.25
BETA = (8.0 * DEPTH) ** -0.25
EPS = 1e-5
IN_SIZES = (Q_RANK, KV_RANK, MLA_ROPE, GLA_HEADS * GLA_DK, GLA_HEADS * GLA_DK,
            GLA_WIDTH, GATE_RANK, GLA_WIDTH)
IN_COLS = sum(IN_SIZES)

kernel_name = 'hymba_mla_gla_deepnorm_decode_step'

def rms_norm(x, g):
    xf = x.astype(jnp.float32)
    return (xf * lax.rsqrt(jnp.mean(xf * xf, -1, keepdims=True) + EPS) * g).astype(x.dtype)

def layer_norm(x, g, b):
    xf = x.astype(jnp.float32)
    mu = jnp.mean(xf, -1, keepdims=True)
    var = jnp.mean(jnp.square(xf - mu), -1, keepdims=True)
    return ((xf - mu) * lax.rsqrt(var + EPS) * g + b).astype(x.dtype)

def rope_tables(pos):
    inv = ROPE_THETA ** (-jnp.arange(0, MLA_ROPE, 2, dtype=jnp.float32) / MLA_ROPE)
    ang = pos.astype(jnp.float32)[:, None] * inv[None, :]
    return jnp.cos(ang), jnp.sin(ang)

def apply_rope(x, cos, sin):
    half = MLA_ROPE // 2
    x1, x2 = x[..., :half], x[..., half:]
    return jnp.concatenate([x1 * cos - x2 * sin, x2 * cos + x1 * sin], -1).astype(x.dtype)

def mixer_inputs(x, pos, w_in, q_norm, w_uq, kv_norm, w_uk, w_gate2, b_gate):
    B, T, _ = x.shape
    idx = np.cumsum(IN_SIZES)[:-1].tolist()
    cq, ckv, kr, gq, gk, gv, gr, gg = jnp.split(x @ w_in, idx, axis=-1)
    cos, sin = rope_tables(pos)
    q = (rms_norm(cq, q_norm) @ w_uq).reshape(B, T, MLA_HEADS, MLA_NOPE + MLA_ROPE)
    q_nope, q_rope = q[..., :MLA_NOPE], q[..., MLA_NOPE:]
    q_rope = apply_rope(q_rope, cos[:, None, :], sin[:, None, :])
    k_rope = apply_rope(kr, cos, sin)
    ckv = rms_norm(ckv, kv_norm)
    q_lat = jnp.einsum('bthn,rhn->bthr', q_nope, w_uk)
    gla_q = gq.reshape(B, T, GLA_HEADS, GLA_DK) * (GLA_DK ** -0.5)
    gla_k = gk.reshape(B, T, GLA_HEADS, GLA_DK)
    gla_v = gv.reshape(B, T, GLA_HEADS, GLA_DV)
    loga = jax.nn.log_sigmoid((gr @ w_gate2 + b_gate).astype(jnp.float32)) / GATE_TAU
    loga = loga.reshape(B, T, GLA_HEADS, GLA_DK)
    return q_lat, q_rope, ckv, k_rope, gla_q, gla_k, gla_v, loga, gg

def mla_prompt(q_lat, q_rope, ckv, krope):
    B, T = ckv.shape[:2]
    key_pos = jnp.arange(T)

    def block(i):
        start = i * Q_BLOCK
        qs = lax.dynamic_slice_in_dim(q_lat, start, Q_BLOCK, axis=1)
        qr = lax.dynamic_slice_in_dim(q_rope, start, Q_BLOCK, axis=1)
        s = (jnp.einsum('bqhr,bkr->bhqk', qs, ckv)
             + jnp.einsum('bqhe,bke->bhqk', qr, krope)).astype(jnp.float32) * MLA_SCALE
        qpos = start + jnp.arange(Q_BLOCK)
        s = jnp.where(key_pos[None, :] <= qpos[:, None], s, -jnp.inf)
        p = jax.nn.softmax(s, axis=-1).astype(ckv.dtype)
        return jnp.einsum('bhqk,bkr->bqhr', p, ckv)

    o = lax.map(block, jnp.arange(T // Q_BLOCK))
    return jnp.moveaxis(o, 0, 1).reshape(B, T, MLA_HEADS, KV_RANK)

def mla_sample(q_lat, q_rope, c_past, kr_past, c_new, kr_new):
    T = c_new.shape[1]
    s_past = jnp.einsum('bthr,bsr->bhts', q_lat, c_past) + jnp.einsum('bthe,bse->bhts', q_rope, kr_past)
    s_new = jnp.einsum('bthr,bur->bhtu', q_lat, c_new) + jnp.einsum('bthe,bue->bhtu', q_rope, kr_new)
    tri = jnp.arange(T)[:, None] >= jnp.arange(T)[None, :]
    s_new = jnp.where(tri, s_new.astype(jnp.float32), -jnp.inf)
    s = jnp.concatenate([s_past.astype(jnp.float32), s_new], -1) * MLA_SCALE
    p = jax.nn.softmax(s, axis=-1).astype(c_new.dtype)
    P = c_past.shape[1]
    return (jnp.einsum('bhts,bsr->bthr', p[..., :P], c_past)
            + jnp.einsum('bhtu,bur->bthr', p[..., P:], c_new))

def gla_prompt(q, k, v, loga):
    B, T = q.shape[:2]
    N = T // GLA_CHUNK

    def chunks(a):
        return a.reshape(B, N, GLA_CHUNK, a.shape[2], a.shape[3]).transpose(0, 3, 1, 2, 4).astype(jnp.float32)

    qf, kf, vf, g = chunks(q), chunks(k), chunks(v), chunks(loga)
    b = jnp.cumsum(g, axis=3)
    b_last = b[..., -1:, :]
    q_t = qf * jnp.exp(b)
    k_t = kf * jnp.exp(-b)
    k_h = kf * jnp.exp(b_last - b)
    tri = jnp.arange(GLA_CHUNK)[:, None] >= jnp.arange(GLA_CHUNK)[None, :]
    A = jnp.where(tri, jnp.einsum('bhnid,bhnjd->bhnij', q_t, k_t), 0.0)
    o_intra = jnp.einsum('bhnij,bhnjv->bhniv', A, vf)
    kv_chunk = jnp.einsum('bhnjd,bhnjv->bhndv', k_h, vf)
    decay = jnp.exp(b_last[..., 0, :])

    def step(S, inp):
        dec, kv = inp
        return dec[..., None] * S + kv, S

    S0 = jnp.zeros((B, GLA_HEADS, GLA_DK, GLA_DV), jnp.float32)
    S_fin, S_prev = lax.scan(step, S0, (jnp.moveaxis(decay, 2, 0), jnp.moveaxis(kv_chunk, 2, 0)))
    S_prev = jnp.moveaxis(S_prev, 0, 2)
    o = o_intra + jnp.einsum('bhnid,bhndv->bhniv', q_t, S_prev)
    o = o.transpose(0, 2, 3, 1, 4).reshape(B, T, GLA_HEADS, GLA_DV)
    return o, S_fin

def gla_recurrent(S0, q, k, v, loga):
    xs = tuple(jnp.moveaxis(a.astype(jnp.float32), 1, 0) for a in (q, k, v, loga))

    def step(S, inp):
        qt, kt, vt, gt = inp
        S = jnp.exp(gt)[..., None] * S + kt[..., :, None] * vt[..., None, :]
        return S, jnp.einsum('bhd,bhdv->bhv', qt, S)

    S_fin, o = lax.scan(step, S0.astype(jnp.float32), xs)
    return jnp.moveaxis(o, 0, 1), S_fin

def mixer_output(o_lat, gla_o, gg, w_uv, gla_norm, w_out, dtype):
    B, T = gg.shape[:2]
    mla = jnp.einsum('bthr,rhv->bthv', o_lat, w_uv).reshape(B, T, MLA_WIDTH)
    gla = rms_norm(gla_o.astype(dtype), gla_norm) * jax.nn.silu(gg.reshape(B, T, GLA_HEADS, GLA_DV))
    return jnp.concatenate([mla, gla.reshape(B, T, GLA_WIDTH)], -1) @ w_out

def post_block(x, mix, ln1_g, ln1_b, w1, w2, ln2_g, ln2_b):
    x = layer_norm(ALPHA * x + mix, ln1_g, ln1_b)
    h = jnp.square(jax.nn.relu(x @ w1)) @ w2
    return layer_norm(ALPHA * x + h, ln2_g, ln2_b)

def setup_inputs(seed: int = 0) -> dict:
    key = jax.random.key(seed)
    ks = jax.random.split(key, 24)
    n_pages = PAST_LEN // PAGE_SIZE
    n_used = DEC_BATCH * n_pages
    n_phys = n_used + n_used // 4
    nrm = jax.random.normal
    f32 = jnp.float32
    L = DEPTH
    page_table = jax.random.permutation(ks[5], n_phys)[:n_used].reshape(DEC_BATCH, n_pages).astype(jnp.int32)
    return {
        'x_prompt': nrm(ks[0], (BATCH, SEQ, D_MODEL), f32),
        'x_sample': nrm(ks[1], (DEC_BATCH, DEC_SEQ, D_MODEL), f32),
        'cache_ckv': nrm(ks[2], (L, n_phys, PAGE_SIZE, KV_RANK), f32),
        'cache_krope': nrm(ks[3], (L, n_phys, PAGE_SIZE, MLA_ROPE), f32),
        'state_gla': 0.5 * nrm(ks[4], (L, DEC_BATCH, GLA_HEADS, GLA_DK, GLA_DV), f32),
        'page_table': page_table,
        'w_in': nrm(ks[6], (L, D_MODEL, IN_COLS), f32) * D_MODEL ** -0.5,
        'mla_q_norm': 1.0 + 0.02 * nrm(ks[7], (L, Q_RANK), f32),
        'mla_w_uq': nrm(ks[8], (L, Q_RANK, MLA_HEADS * (MLA_NOPE + MLA_ROPE)), f32) * Q_RANK ** -0.5,
        'mla_kv_norm': 1.0 + 0.02 * nrm(ks[9], (L, KV_RANK), f32),
        'mla_w_uk': nrm(ks[10], (L, KV_RANK, MLA_HEADS, MLA_NOPE), f32) * KV_RANK ** -0.5,
        'mla_w_uv': nrm(ks[11], (L, KV_RANK, MLA_HEADS, MLA_V), f32) * (BETA * KV_RANK ** -0.5),
        'gla_w_gate2': nrm(ks[12], (L, GATE_RANK, GLA_HEADS * GLA_DK), f32) * GATE_RANK ** -0.5,
        'gla_b_gate': 0.1 * nrm(ks[13], (L, GLA_HEADS * GLA_DK), f32),
        'gla_norm': 1.0 + 0.02 * nrm(ks[14], (L, GLA_DV), f32),
        'w_out': nrm(ks[15], (L, MIX_WIDTH, D_MODEL), f32) * (BETA * MIX_WIDTH ** -0.5),
        'ln1_g': 1.0 + 0.02 * nrm(ks[16], (L, D_MODEL), f32),
        'ln1_b': 0.02 * nrm(ks[17], (L, D_MODEL), f32),
        'mlp_w1': nrm(ks[18], (L, D_MODEL, D_FF), f32) * (BETA * D_MODEL ** -0.5),
        'mlp_w2': nrm(ks[19], (L, D_FF, D_MODEL), f32) * (BETA * D_FF ** -0.5),
        'ln2_g': 1.0 + 0.02 * nrm(ks[20], (L, D_MODEL), f32),
        'ln2_b': 0.02 * nrm(ks[21], (L, D_MODEL), f32),
    }

def reference(x_prompt, x_sample, cache_ckv, cache_krope, state_gla, page_table,
              w_in, mla_q_norm, mla_w_uq, mla_kv_norm, mla_w_uk, mla_w_uv,
              gla_w_gate2, gla_b_gate, gla_norm, w_out, ln1_g, ln1_b,
              mlp_w1, mlp_w2, ln2_g, ln2_b):
    DB, T_new = x_sample.shape[:2]
    pos_p = jnp.arange(x_prompt.shape[1], dtype=jnp.int32)
    pos_s = PAST_LEN + jnp.arange(T_new, dtype=jnp.int32)
    xp, xs = x_prompt, x_sample
    ckv_p_l, kr_p_l, S_p_l, ckv_s_l, kr_s_l, S_s_l = [], [], [], [], [], []
    for l in range(DEPTH):
        proj = (w_in[l], mla_q_norm[l], mla_w_uq[l], mla_kv_norm[l], mla_w_uk[l],
                gla_w_gate2[l], gla_b_gate[l])
        q_lat, q_rope, ckv, krope, gq, gk, gv, ga, gg = mixer_inputs(xp, pos_p, *proj)
        o_lat = mla_prompt(q_lat, q_rope, ckv, krope)
        gla_o, S_p = gla_prompt(gq, gk, gv, ga)
        mix = mixer_output(o_lat, gla_o, gg, mla_w_uv[l], gla_norm[l], w_out[l], xp.dtype)
        xp = post_block(xp, mix, ln1_g[l], ln1_b[l], mlp_w1[l], mlp_w2[l], ln2_g[l], ln2_b[l])
        ckv_p_l.append(ckv)
        kr_p_l.append(krope)
        S_p_l.append(S_p.astype(state_gla.dtype))
        q_lat, q_rope, ckv, krope, gq, gk, gv, ga, gg = mixer_inputs(xs, pos_s, *proj)
        c_past = cache_ckv[l][page_table].reshape(DB, -1, KV_RANK)
        kr_past = cache_krope[l][page_table].reshape(DB, -1, MLA_ROPE)
        o_lat = mla_sample(q_lat, q_rope, c_past, kr_past, ckv, krope)
        gla_o, S_s = gla_recurrent(state_gla[l], gq, gk, gv, ga)
        mix = mixer_output(o_lat, gla_o, gg, mla_w_uv[l], gla_norm[l], w_out[l], xs.dtype)
        xs = post_block(xs, mix, ln1_g[l], ln1_b[l], mlp_w1[l], mlp_w2[l], ln2_g[l], ln2_b[l])
        ckv_s_l.append(ckv)
        kr_s_l.append(krope)
        S_s_l.append(S_s.astype(state_gla.dtype))
    return (xp, xs, jnp.stack(ckv_p_l), jnp.stack(kr_p_l), jnp.stack(S_p_l),
            jnp.stack(ckv_s_l), jnp.stack(kr_s_l), jnp.stack(S_s_l))


_drawn_inputs = setup_inputs


def setup_inputs(seed=0):
    import zlib

    import numpy as np

    out = dict(_drawn_inputs(seed))
    spreads = {}
    factors = {'cache_ckv': 7.721,
     'cache_krope': 8.0,
     'mla_q_norm': 8.0,
     'mla_w_uk': 2.968,
     'gla_norm': 25.905,
     'ln1_g': 7.692,
     'ln1_b': 7.842,
     'ln2_g': 8.718,
     'ln2_b': 8.11}
    for name, (base, spread) in spreads.items():
        noise = np.random.default_rng([zlib.crc32(name.encode()), seed]).standard_normal(out[name].shape)
        drawn = base * np.exp(spread * noise) if base else spread * noise
        out[name] = __import__('jax').numpy.asarray(drawn.astype(out[name].dtype))
    for name, factor in factors.items():
        out[name] = (out[name] * factor).astype(out[name].dtype)
    return out
```

```python
from contextlib import ExitStack

import concourse.bass as bass
from concourse import mybir

ALU = mybir.AluOpType
ACT = mybir.ActivationFunctionType
AX = mybir.AxisListType
F32 = mybir.dt.float32
F32R = mybir.dt.float32r
U32 = mybir.dt.uint32
I32 = mybir.dt.int32

P = 128
D = 1024
TP, NB = 1024, 8
T = TP + NB
BLK = T // 3
KD = D // P
TT = TP // P + 1
QR, KVR, ROPE, NOPE = 384, 256, 64, 128
HEADS, DK, DV, GR = 4, 64, 128, 16
CH = 64
NCH = TP // CH
PAST, PAGE = 2048, 128
PAGES = PAST // PAGE
N_PHYS = NB * PAGES + NB * PAGES // 4
DFF = 4096
ALPHA = 2.0 ** 0.25
EPS = 1e-5
SCALE = (NOPE + ROPE) ** -0.5
NEG = -1.0e30

OFF = dict(cq=0, ckv=384, kr=640, gq=704, gk=960, gv=1216, gr=1728, gg=1744)
TILES = [("krgr", None)]
TILES += [("gq", OFF["gq"] + P * i) for i in range(2)] + [("gk", OFF["gk"] + P * i) for i in range(2)]
TILES += [("gv", OFF["gv"] + P * i) for i in range(4)] + [("gg", OFF["gg"] + P * i) for i in range(4)]
TILES += [("ckv", OFF["ckv"] + P * i) for i in range(2)] + [("cq", OFF["cq"] + P * i) for i in range(3)]
NT = len(TILES)
ROW_GQ, ROW_GK, ROW_GV, ROW_GG, ROW_CKV, ROW_CQ = 1, 3, 5, 9, 13, 15

CONST_COLS = {}
_at = 0
for _n, _w in (("ident", P), ("swap", P), ("tri16", P), ("chunkmask", P), ("causal", P), ("spread", 4 * P),
               ("ones", P), ("dup", P), ("swapdup", P), ("sumkq", 4), ("diagh", 4)):
    CONST_COLS[_n] = (_at, _w)
    _at += _w
CONST_W = _at


def tok(t):
    return (t * P, P) if t < TP // P else (TP, NB)


def hymba_step(nc, a, out, scratch):
    with ExitStack() as ctx:
        def sem(name):
            return ctx.enter_context(nc.semaphore(name))

        def sb(at, name, shape, dt=F32):
            assert at % 8 == 0, name
            with nc.sbuf_tensor(name + "_below", [P, at], F32):
                with nc.sbuf_tensor(name, shape, dt) as t:
                    return t

        psum = ctx.enter_context(nc.psum_tensor("psum", [P, 8, 512], F32))

        consts = sb(8, "consts", [P, CONST_W])
        cols = sb(8 + CONST_W, "cols", [P, 24])
        smp = sb(8 + CONST_W + 24, "decode_cols", [P, 72])
        pt = sb(8 + CONST_W + 96, "page_table", [1, NB * PAGES], I32)
        PERSIST = 8 + CONST_W + 96 + NB * PAGES
        mixT = sb(PERSIST, "mixT", [P, KD, T])
        AREA = PERSIST + KD * T

        def const(name, rows=P):
            c, w = CONST_COLS[name]
            return consts[0:rows, c:c + w]

        ident = const("ident")
        QN, KVN, GN, L1G, L1B = 0, 3, 5, 6, 14

        s_const = sem("const_loaded")

        at = AREA
        xTh = sb(at, "xTh", [P, KD, T], F32R); at += KD * T
        xTl = sb(at, "xTl", [P, KD, T], F32R); at += KD * T
        xnat = sb(at, "xnat", [P, 2, D]); at += 2 * D
        w1raw = sb(at, "win_raw", [P, 3, KD, P]); at += 3 * D
        winh = sb(at, "win_hi", [P, 2, KD, P], F32R); at += 2 * D
        winl = sb(at, "win_lo", [P, 2, KD, P], F32R); at += 2 * D
        pstage = sb(at, "proj_stage", [P, 3, T]); at += 3 * T
        GLA_IN = at

        x_loaded = [sem(f"x_loaded{i}") for i in range(2)]
        xt_done, xh_done, xl_done = sem("xt_transposed"), sem("xT_hi"), sem("xT_lo")
        win_loaded = [sem(f"win_loaded{i}") for i in range(3)]
        winh_done, winl_done = sem("win_hi_done"), sem("win_lo_done")
        proj_mm, proj_out = sem("proj_multiplied"), sem("proj_evacuated")
        proj_stored = [sem(f"proj_stored{i}") for i in range(3)]

        def stored(eng, m):
            eng.wait_ge(proj_stored[m % 3], 16 * (m // 3 + 1))

        GATE_FROM = 4

        def sp_project(sp):
            sp.dma_start(consts[:], a["consts"]).then_inc(s_const, 16)
            sp.dma_start(cols[:], a["cols"]).then_inc(s_const, 16)

            def load_w(m):
                if m >= 3:
                    sp.wait_ge(winl_done, m - 2)
                kind, c0 = TILES[m]
                w = a["w_in"].rearrange("l (k p) n -> p (l k) n", p=P)
                if kind == "krgr":
                    sp.dma_start(w1raw[:, m % 3, :, 0:ROPE], w[:, :, OFF["kr"]:OFF["kr"] + ROPE]).then_inc(win_loaded[m % 3], 16)
                    sp.dma_start(w1raw[:, m % 3, :, ROPE:ROPE + GR], w[:, :, OFF["gr"]:OFF["gr"] + GR]).then_inc(win_loaded[m % 3], 16)
                else:
                    sp.dma_start(w1raw[:, m % 3, :, :], w[:, :, c0:c0 + P]).then_inc(win_loaded[m % 3], 16)

            for t in range(TT):
                if t >= 2:
                    sp.wait_ge(xt_done, t - 1)
                n = tok(t)[1]
                src = a["x_prompt"][0, t * P:(t + 1) * P, :] if t < 8 else a["x_sample"].rearrange("b s d -> (b s) d")
                sp.dma_start(xnat[0:n, t % 2, :], src).then_inc(x_loaded[t % 2], 16)
                if 1 <= t <= 3:
                    load_w(t - 1)
            for m in range(3, NT + 3):
                if m < NT:
                    load_w(m)
                j = m - 3
                rows = ROPE + GR if j == 0 else P
                sp.wait_ge(proj_out, j + 1)
                sp.dma_start(scratch[j, 0:rows, :], pstage[0:rows, j % 3, :]).then_inc(proj_stored[j % 3], 16)
                if j >= 1:
                    sp_gla_in(sp, j - 1)

        def xt_bank(t, n):
            return psum[:, 2 * (t % 3):2 * (t % 3) + 2, :].rearrange("p b (k c) -> p (b k) c", c=P)[:, :, 0:n]

        def pe_project(pe):
            pe.wait_ge(s_const, 32)
            for t in range(TT):
                n = tok(t)[1]
                pe.wait_ge(x_loaded[t % 2], 16 * (t // 2 + 1))
                if t >= 3:
                    pe.wait_ge(xl_done, t - 2)
                for k in range(KD):
                    mm = pe.transpose(xt_bank(t, n)[:, k, :], xnat[0:n, t % 2, k * P:(k + 1) * P], ident[0:n, 0:n])
                mm.then_inc(xt_done, 1)
            pe.wait_ge(xl_done, TT)
            for m in range(NT):
                if 0 <= m - GATE_FROM < TT:
                    pe_gate(pe, m - GATE_FROM)
                M = ROPE + GR if m == 0 else P
                pe.wait_ge(winl_done, m + 1)
                if m >= 2:
                    pe.wait_ge(proj_out, m - 1)
                for b in range(3):
                    for k in range(KD):
                        for i, (w, x) in enumerate(((winh, xTh), (winh, xTl), (winl, xTh))):
                            mm = pe.matmul(psum[0:M, 3 * (m % 2) + b, 0:BLK], w[:, m % 2, k, 0:M],
                                           x[:, k, b * BLK:(b + 1) * BLK], start=(k == 0 and i == 0),
                                           stop=(k == KD - 1 and i == 2))
                mm.then_inc(proj_mm, 1)

        def act_project(act):
            for t in range(TT):
                c0, n = tok(t)
                act.wait_ge(xt_done, t + 1)
                act.activation(xTh[:, :, c0:c0 + n], xt_bank(t, n), ACT.Copy).then_inc(xh_done, 1)
                if t in (2, 3):
                    split_hi(act, t - 2)
            for m in range(NT):
                if 2 <= m + 1 < NT:
                    split_hi(act, m + 1)
                if m == GATE_FROM + TT + 1:
                    act_gate(act)
                M = ROPE + GR if m == 0 else P
                act.wait_ge(proj_mm, m + 1)
                if m >= 3:
                    act.wait_ge(proj_stored[m % 3], 16 * (m // 3))
                act.activation(pstage[0:M, m % 3, :].rearrange("p (b c) -> p b c", b=3),
                               psum[0:M, 3 * (m % 2):3 * (m % 2) + 3, 0:BLK], ACT.Copy).then_inc(proj_out, 1)

        def split_hi(act, m):
            M = ROPE + GR if m == 0 else P
            act.wait_ge(win_loaded[m % 3], 16 * (m // 3 + 1) + (16 if m % 3 == 0 else 0))
            if m >= 2:
                act.wait_ge(proj_mm, m - 1)
            act.activation(winh[:, m % 2, :, 0:M], w1raw[:, m % 3, :, 0:M], ACT.Copy).then_inc(winh_done, 1)

        def dve_project(dve):
            def split_lo(m):
                M = ROPE + GR if m == 0 else P
                dve.wait_ge(winh_done, m + 1)
                dve.tensor_tensor(winl[:, m % 2, :, 0:M], w1raw[:, m % 3, :, 0:M], winh[:, m % 2, :, 0:M].bitcast(F32),
                                  ALU.subtract).then_inc(winl_done, 1)

            for t in range(TT):
                c0, n = tok(t)
                dve.wait_ge(xh_done, t + 1)
                dve.tensor_tensor(xTl[:, :, c0:c0 + n], xt_bank(t, n), xTh[:, :, c0:c0 + n].bitcast(F32),
                                  ALU.subtract).then_inc(xl_done, 1)
                if t in (2, 3):
                    split_lo(t - 2)
            for m in range(2, NT):
                split_lo(m)
                if m == GATE_FROM + TT + 2:
                    dve_gate(dve, TT)
                if 0 <= m - GATE_FROM - 1 < TT:
                    dve_gate(dve, m - GATE_FROM - 1)

        G_TASKS = [(("z", t), 1) for t in range(TT)]
        G_TASKS += [(("cum", f, h), 1) for f in range(2) for h in range(2)] + [(("cums",), 1)]
        G_TASKS += [(("v", t), 1) for t in range(TT)]
        G_TASKS += [(("kh", i), 1) for i in range(4)] + [(("vb", b), 1) for b in range(NB)]
        G_TASKS += [(("kv", n), 1) for n in range(NCH)] + [(("A", 0), 1)]
        for t in range(TT):
            G_TASKS += [(("A", t + 1), 1)] * (t + 1 < 8) + [(("O", t), 1)]
        G_TASKS += [(("oT", t), 1) for t in range(TT)]
        G_AT = {key: i for i, (key, _) in enumerate(G_TASKS)}
        g_full = sem("gla_bank_full")
        g_free = [sem(f"gla_bank_free{i}") for i in range(2)]

        def g_bank(key):
            return psum[:, 6 + G_AT[key] % 2, :]

        def g_begin(pe, key):
            i = G_AT[key]
            reads = sum(r for j, (_, r) in enumerate(G_TASKS[:i]) if j % 2 == i % 2)
            if reads:
                pe.wait_ge(g_free[i % 2], reads)

        def g_wait(eng, key):
            eng.wait_ge(g_full, G_AT[key] + 1)

        def g_read(eng, *keys):
            for key in keys:
                i = G_AT[key]
                eng.wait_ge(g_free[i % 2], sum(r for j, (_, r) in enumerate(G_TASKS[:i + 1]) if j % 2 == i % 2))

        def g_done(ins, key):
            ins.then_inc(g_free[G_AT[key] % 2], 1)

        at = GLA_IN
        gqk = sb(at, "gqk", [P, 4, T]); at += 4 * T
        gvT = sb(at, "gvT", [P, 4, T])
        state = sb(at, "state", [P, NB, 2, DV])
        vk = sb(at + NB * 2 * DV, "vk", [P, NB, 2, DV]); at += 4 * T
        grT = sb(at, "grT", [32, T]); at += T
        w2g = sb(at, "w_gate2", [32, 256]); at += 256
        ggT = sb(at, "ggT", [P, 4, T])
        loga = sb(at, "loga", [P, TT, 256]); zabs = sb(at + TT * 256, "zabs", [P, TT, 256]); at += 2 * TT * 256
        assert at <= 53200
        at = AREA
        gout = sb(at, "gla_out", [P, TT, 512]); at += TT * 512
        gv = sb(at, "gv", [P, TT, 512]); at += TT * 512
        eb = sb(at, "exp_b", [P, 2, T]); at += 2 * T
        kt = sb(at, "k_tilde", [P, 2, TP]); at += 2 * TP
        khT = sb(at, "k_hat_T", [P, 2, TP]); at += 2 * TP
        kh = sb(at, "k_hat", [P, 8, 256]); at += 8 * 256
        hist = sb(at, "state_hist", [P, NCH + 1, 2, DV]); at += (NCH + 1) * 2 * DV
        qt = sb(at, "q_tilde", [P, 2, 2, TP]); at += 4 * T
        am = sb(at, "a_masked", [P, 2, 4, P]); at += 8 * P
        blast = sb(at, "b_last", [P, 2, NCH]); at += 2 * NCH
        gss = sb(at, "gla_sumsq", [P, 4 * TT]); at += 40
        grs = sb(at, "gla_rstd", [P, 4 * TT]); at += 40
        gtmp = sb(at, "gla_tmp", [P, 4 * TT]); at += 40
        qz = sb(at, "q_diag", [P, 2, 2, NB, NB]); at += 4 * NB * NB
        gjunk = sb(at, "square_out", [P, P]); at += P
        assert at <= GLA_IN

        gr_ones, gin_loaded, gst_loaded = sem("gate_ones"), [sem(f"gla_in{i}") for i in range(4)], sem("state_loaded")
        abs_done, ln_done, lg_done, silu_e = sem("abs_done"), sem("ln_done"), sem("loga_done"), sem("silu_exp")
        exb_done, sub_done, qk_done, seen_done = sem("exp_b_done"), sem("b_differences"), sem("gla_qk"), sem("exp_hat")
        hist_done, gss_set, gss_done = sem("state_steps"), sem("sumsq_preset"), sem("sumsq_done")
        st_done, grv_done, gry_done = sem("state_new"), sem("gla_var"), sem("gla_lnexp")
        gon_done, silu_done, gst_stored = sem("gla_normed"), sem("silu_done"), sem("gla_stored")
        dve_step, act_step = sem("dve_step"), sem("act_step")
        steps = {"dve": 0, "act": 0}

        def dlink(dve, ins):
            steps["dve"] += 1
            ins.then_inc(dve_step, 1)
            dve.wait_ge(dve_step, steps["dve"])

        def alink(act, ins):
            steps["act"] += 1
            ins.then_inc(act_step, 1)
            act.wait_ge(act_step, steps["act"])

        def sp_gla_in(sp, j):
            if j == 0:
                stored(sp, 0)
                sp.wait_ge(gr_ones, 1)
                sp.dma_start(grT[0:GR, :], scratch[0, ROPE:ROPE + GR, :]).then_inc(gin_loaded[0], 16)
                sp.dma_start(w2g[0:GR, :], a["w_gate2"][0]).then_inc(gin_loaded[0], 16)
                sp.dma_start(w2g[GR:GR + 1, :], a["b_gate"]).then_inc(gin_loaded[0], 16)
            elif j == ROW_GK + 1:
                stored(sp, j), stored(sp, j - 1), stored(sp, j - 2)
                sp.dma_start(gqk[:], scratch[ROW_GQ:ROW_GQ + 4].rearrange("m p t -> p m t")).then_inc(gin_loaded[1], 16)
            elif j == ROW_GV + 3:
                stored(sp, j), stored(sp, j - 1), stored(sp, j - 2)
                sp.dma_start(gvT[:], scratch[ROW_GV:ROW_GV + 4].rearrange("m p t -> p m t")).then_inc(gin_loaded[2], 16)

        def sp_gla(sp):
            g_wait(sp, ("cums",))
            sp.dma_start(ggT[:], scratch[ROW_GG:ROW_GG + 4].rearrange("m p t -> p m t")).then_inc(gin_loaded[3], 16)
            g_wait(sp, ("v", TT - 1))
            for f in range(2):
                sp.dma_start(state[:, :, f, :], a["state_gla"][0].rearrange("b (f h) d v -> f (h d) b v", f=2)[f]).then_inc(gst_loaded, 16)
            g_read(sp, ("kv", NCH - 1))
            sp.dma_start(out["gla_prompt"][0, 0].rearrange("(f h) d v -> (h d) f v", f=2), hist[:, NCH, :, :]).then_inc(gst_stored, 16)
            sp.wait_ge(st_done, 1)
            for f in range(2):
                sp.dma_start(out["gla_sample"][0].rearrange("b (f h) d v -> f (h d) b v", f=2)[f], state[:, :, f, :]).then_inc(gst_stored, 16)

        def half(hh):
            return slice(DK * hh, DK * hh + DK)

        def pe_gate(pe, t):
            c0, n = tok(t)
            key = ("z", t)
            if t == 0:
                pe.wait_ge(gin_loaded[0], 48)
            g_begin(pe, key)
            pe.matmul(g_bank(key)[0:n, 0:256], grT[0:GR + 1, c0:c0 + n], w2g[0:GR + 1, :], start=True, stop=True).then_inc(g_full, 1)

        def pe_gla(pe):
            pe.wait_ge(lg_done, 2)
            for f in range(2):
                for h in range(2):
                    key = ("cum", f, h)
                    g_begin(pe, key)
                    for i in range(4):
                        t = 4 * h + i
                        mm = pe.matmul(g_bank(key)[:, i * P:(i + 1) * P], loga[:, t, f * P:(f + 1) * P], const("tri16"),
                                       start=True, stop=True)
                    mm.then_inc(g_full, 1)
            key = ("cums",)
            g_begin(pe, key)
            for f in range(2):
                mm = pe.matmul(g_bank(key)[:, f * NB:(f + 1) * NB], loga[0:NB, TT - 1, f * P:(f + 1) * P], ident[0:NB, 0:NB],
                               start=True, stop=True)
            mm.then_inc(g_full, 1)
            for t in range(TT):
                c0, n = tok(t)
                key = ("v", t)
                if t == 0:
                    pe.wait_ge(gin_loaded[2], 16)
                g_begin(pe, key)
                for h in range(HEADS):
                    mm = pe.transpose(g_bank(key)[0:n, h * P:(h + 1) * P], gvT[:, h, c0:c0 + n], ident)
                mm.then_inc(g_full, 1)
            for i in range(4):
                key = ("kh", i)
                if i == 0:
                    pe.wait_ge(qk_done, 2)
                g_begin(pe, key)
                for j in range(2):
                    for f in range(2):
                        t = 2 * i + j
                        mm = pe.transpose(g_bank(key)[:, (2 * j + f) * P:(2 * j + f + 1) * P], khT[:, f, t * P:(t + 1) * P], ident)
                mm.then_inc(g_full, 1)
            g_read(pe, ("v", TT - 1), ("v", TT - 2))
            for b in range(NB):
                key = ("vb", b)
                g_begin(pe, key)
                pe.matmul(g_bank(key), ident[0:NB, b:b + 1].broadcast_to([NB, P]), gv[0:NB, TT - 1, :], start=True, stop=True).then_inc(g_full, 1)
            for n in range(NCH):
                key = ("kv", n)
                if n % 4 == 0:
                    g_read(pe, ("kh", n // 4))
                g_begin(pe, key)
                r = slice(CH * (n % 2), CH * (n % 2) + CH)
                for f in range(2):
                    mm = pe.matmul(g_bank(key)[:, f * 256:(f + 1) * 256], kh[r, n // 2, f * P:(f + 1) * P],
                                   gv[r, n // 2, f * 256:(f + 1) * 256], start=True, stop=True)
                mm.then_inc(g_full, 1)

            def inner(t):
                key = ("A", t)
                g_begin(pe, key)
                for h in range(HEADS):
                    f = h // 2
                    mm = pe.matmul(g_bank(key)[:, h * P:(h + 1) * P], kt[:, f, t * P:(t + 1) * P], qt[:, f, h % 2, t * P:(t + 1) * P],
                                   start=True, stop=True)
                mm.then_inc(g_full, 1)

            pe.wait_ge(qk_done, 6)
            inner(0)
            g_read(pe, ("kv", NCH - 2), ("kv", NCH - 1))
            for t in range(TT):
                if t + 1 < 8:
                    inner(t + 1)
                key = ("O", t)
                if t < 8:
                    g_read(pe, ("A", t))
                else:
                    pe.wait_ge(st_done, 2)
                g_begin(pe, key)
                o = g_bank(key)
                for h in range(HEADS):
                    f = h // 2
                    if t < 8:
                        pe.matmul(o[:, h * P:(h + 1) * P], am[:, t % 2, h, :], gv[:, t, h * P:(h + 1) * P], start=True, stop=True,
                                  skip_group_check=True)
                        for c in range(2):
                            q0 = t * P + CH * c
                            mm = pe.matmul(o[CH * c:CH * c + CH, h * P:(h + 1) * P], qt[:, f, h % 2, q0:q0 + CH], hist[:, 2 * t + c, f, :],
                                           start=False, stop=True, skip_group_check=True)
                    else:
                        for b in range(NB):
                            mm = pe.matmul(o[0:NB, h * P:(h + 1) * P], qz[:, f, h % 2, b, :], state[:, b, f, :], start=(b == 0), stop=(b == NB - 1))
                mm.then_inc(g_full, 1)
            pe.wait_ge(gon_done, 1)
            for t in range(TT):
                c0, n = tok(t)
                key = ("oT", t)
                g_begin(pe, key)
                for h in range(HEADS):
                    mm = pe.transpose(g_bank(key)[:, h * P:h * P + n], gout[0:n, t, h * P:(h + 1) * P], ident[0:n, 0:n])
                mm.then_inc(g_full, 1)

        def act_gate(act):
            g_read(act, ("z", TT - 1), ("z", TT - 2))
            for n, ts in ((P, slice(0, 8)), (NB, slice(8, 9))):
                alink(act, act.activation(zabs[0:n, ts, :], loga[0:n, ts, :], ACT.Abs))
                alink(act, act.activation(zabs[0:n, ts, :], zabs[0:n, ts, :], ACT.Exp, scale=-1.0))
                act.activation(zabs[0:n, ts, :], zabs[0:n, ts, :], ACT.Ln, bias=1.0).then_inc(ln_done, 1)

        def act_gla(act):
            for f in range(2):
                for h in range(2):
                    key = ("cum", f, h)
                    g_wait(act, key)
                    c = slice(512 * h, 512 * h + 512)
                    act.activation(eb[:, f, c], g_bank(key), ACT.Exp)
                    act.activation(kt[:, f, c], g_bank(key), ACT.Exp, scale=-1.0).then_inc(exb_done, 1)
            key = ("cums",)
            g_wait(act, key)
            g_done(act.activation(eb[:, :, TP:T], g_bank(key)[:, 0:2 * NB].rearrange("p (f b) -> p f b", f=2), ACT.Exp,
                                  scale=1.0 / 16.0), key)
            for t in range(TT):
                n = tok(t)[1]
                g_wait(act, ("v", t))
                ins = act.activation(gv[0:n, t, :], g_bank(("v", t))[0:n, :], ACT.Copy)
                g_done(ins, ("v", t))
            for f in range(2):
                act.wait_ge(sub_done, 2 * f + 2)
                act.activation(khT[:, f, :], khT[:, f, :], ACT.Exp).then_inc(seen_done, 1)
            for i in range(4):
                key = ("kh", i)
                g_wait(act, key)
                g_done(act.activation(kh[:, 2 * i:2 * i + 2, :], g_bank(key).rearrange("p (t c) -> p t c", t=2), ACT.Copy), key)
            act.wait_ge(gin_loaded[3], 16)
            act.activation(ggT[:], ggT[:], ACT.Silu).then_inc(silu_e, 1)
            act.wait_ge(gss_set, 1)
            for t in range(TT):
                n = tok(t)[1]
                key = ("O", t)
                g_read(act, key)
                for h in range(HEADS):
                    alink(act, act.activation(gjunk[0:n, :], gout[0:n, t, h * P:(h + 1) * P], ACT.Square,
                                              accum_out=gss[0:n, 4 * t + h:4 * t + h + 1]))
            act.sem_inc(gss_done, 1)
            act.wait_ge(grv_done, 1)
            alink(act, act.activation(grs[:], gtmp[:], ACT.Ln))
            act.activation(grs[:], grs[:], ACT.Exp, scale=-0.5).then_inc(gry_done, 1)

        def dve_gla_early(dve):
            dve.memset(grT[:], 1.0).then_inc(gr_ones, 1)

        def dve_gate(dve, t):
            if t < TT:
                n = tok(t)[1]
                key = ("z", t)
                g_wait(dve, key)
                g_done(dve.tensor_copy(loga[0:n, t, :], g_bank(key)[0:n, 0:256]), key)
                return
            g_read(dve, ("z", TT - 1), ("z", TT - 2))
            for i, (n, ts) in enumerate(((P, slice(0, 8)), (NB, slice(8, 9)))):
                dve.wait_ge(ln_done, i + 1)
                dve.scalar_tensor_tensor(loga[0:n, ts, :], loga[0:n, ts, :], 0.0, zabs[0:n, ts, :], ALU.min, ALU.subtract).then_inc(lg_done, 1)

        def dve_gla(dve):
            dve.wait_ge(proj_mm, NT)
            for m in range(NT - 3, NT):
                stored(dve, m)
            dlink(dve, dve.memset(hist[:, 0], 0.0))
            dlink(dve, dve.memset(qz[:], 0.0))
            dlink(dve, dve.memset(am[:], 0.0))
            dve.memset(gss[:], 1.0).then_inc(gss_set, 1)
            dlink(dve, dve.memset(qt[:], 0.0))
            for f in range(2):
                for h in range(2):
                    key = ("cum", f, h)
                    dve.wait_ge(exb_done, 2 * f + h + 1)
                    b3 = g_bank(key).rearrange("p (n c) -> p n c", c=CH)
                    dlink(dve, dve.tensor_copy(blast[:, f, 8 * h:8 * h + 8], b3[:, :, CH - 1]))
                    ins = dve.tensor_tensor(khT[:, f, 512 * h:512 * h + 512].rearrange("p (n c) -> p n c", c=CH),
                                            blast[:, f, 8 * h:8 * h + 8].unsqueeze(2).broadcast_to([P, 8, CH]), b3, ALU.subtract)
                    g_done(ins, key)
                    g_read(dve, key)
                    dve.sem_inc(sub_done, 1)
            dve.wait_ge(gin_loaded[1], 16)
            for f in range(2):
                dve.wait_ge(seen_done, f + 1)
                dve.tensor_tensor(khT[:, f, :], khT[:, f, :], gqk[:, 2 + f, 0:TP], ALU.mult).then_inc(qk_done, 1)
            g_read(dve, ("cums",), ("cum", 1, 1))
            for f in range(2):
                dve.tensor_tensor(kt[:, f, :], kt[:, f, :], gqk[:, 2 + f, 0:TP], ALU.mult).then_inc(qk_done, 1)
                for hh in range(2):
                    r = half(hh)
                    dve.tensor_scalar(qz[r, f, hh].rearrange("p b c -> p (b c)")[:, 0:NB * NB:NB + 1], gqk[r, f, TP:T], DK ** -0.5, None, ALU.mult)
                    ins = dve.scalar_tensor_tensor(qt[r, f, hh], gqk[r, f, 0:TP], DK ** -0.5, eb[r, f, 0:TP], ALU.mult, ALU.mult)
                ins.then_inc(qk_done, 1)
            dve.wait_ge(gst_loaded, 32)
            dlink(dve, dve.tensor_tensor(state[:], state[:],
                                         eb[:, :, TP:T].rearrange("p f b -> p b f").unsqueeze(3).broadcast_to([P, NB, 2, DV]), ALU.mult))
            for b in range(NB):
                key = ("vb", b)
                g_wait(dve, key)
                vb = g_bank(key).rearrange("p (f h v) -> p f h v", f=2, h=2)
                for hh in range(2):
                    r = half(hh)
                    ins = dve.tensor_tensor(vk[r, b], vb[r, :, hh, :],
                                            gqk[r, 2:4, TP + b:TP + b + 1].broadcast_to([DK, 2, DV]), ALU.mult)
                g_done(ins, key)
            g_read(dve, ("vb", NB - 1), ("vb", NB - 2))
            dve.tensor_tensor(state[:], state[:], vk[:], ALU.add).then_inc(st_done, 1)
            dve.wait_ge(st_done, 1)
            dve.sem_inc(st_done, 1)
            for n in range(NCH):
                key = ("kv", n)
                g_wait(dve, key)
                if n >= 1:
                    g_read(dve, ("kv", n - 1))
                for i in range(4):
                    f, hh = i // 2, i % 2
                    r = half(hh)
                    ins = dve.scalar_tensor_tensor(hist[r, n + 1, f, :], hist[r, n, f, :], eb[r, f, CH * n + CH - 1:CH * n + CH],
                                                   g_bank(key)[r, f * 256 + hh * DV:f * 256 + hh * DV + DV], ALU.mult, ALU.add)
                g_done(ins, key)

            def mask_a(t):
                key = ("A", t)
                g_wait(dve, key)
                if t >= 2:
                    g_wait(dve, ("O", t - 2))
                for h in range(HEADS):
                    ins = dve.copy_predicated(am[:, t % 2, h, :], const("chunkmask").bitcast(U32), g_bank(key)[:, h * P:(h + 1) * P])
                g_done(ins, key)

            mask_a(0)
            for t in range(TT):
                n = tok(t)[1]
                if t + 1 < 8:
                    mask_a(t + 1)
                key = ("O", t)
                g_wait(dve, key)
                g_done(dve.tensor_copy(gout[0:n, t, :], g_bank(key)[0:n, :]), key)
            g_read(dve, ("O", TT - 1), ("O", TT - 2))
            dve.wait_ge(gss_done, 1)
            dve.tensor_scalar(gtmp[:], gss[:], 1.0 / DV, EPS, ALU.mult, ALU.add).then_inc(grv_done, 1)
            dve.wait_ge(gry_done, 1)
            newton(dve, grs[:], gtmp[:], gss[:])
            dve.tensor_tensor(gout[:, 0:8].rearrange("p t (h v) -> p (t h) v", h=4), gout[:, 0:8].rearrange("p t (h v) -> p (t h) v", h=4),
                              grs[:, 0:32].unsqueeze(2).broadcast_to([P, 32, DV]), ALU.mult)
            dve.tensor_tensor(gout[0:NB, 8].rearrange("p (h v) -> p h v", h=4), gout[0:NB, 8].rearrange("p (h v) -> p h v", h=4),
                              grs[0:NB, 32:36].unsqueeze(2).broadcast_to([NB, 4, DV]), ALU.mult).then_inc(gon_done, 1)
            dve.wait_ge(silu_e, 1)
            for t in range(TT):
                c0, n = tok(t)
                key = ("oT", t)
                g_wait(dve, key)
                g_done(dve.scalar_tensor_tensor(mixT[:, 4:8, c0:c0 + n], g_bank(key).rearrange("p (h c) -> p h c", h=4)[:, :, 0:n],
                                                cols[:, GN:GN + 1], ggT[:, :, c0:c0 + n], ALU.mult, ALU.mult), key)

        def newton(dve, y, v, tmp):
            dlink(dve, dve.tensor_tensor(tmp, y, y, ALU.mult))
            dlink(dve, dve.tensor_tensor(tmp, tmp, v, ALU.mult))
            dlink(dve, dve.tensor_scalar(tmp, tmp, -0.5, 1.5, ALU.mult, ALU.add))
            dlink(dve, dve.tensor_tensor(y, y, tmp, ALU.mult))

        class Banks:

            def __init__(self, name, banks, keys, after=None):
                self.banks, self.at, B = banks, {k: i for i, k in enumerate(keys)}, len(banks)
                assert len(self.at) == len(keys)
                if after is None:
                    self.full_sem, self.full0 = sem(name + "_full"), 0
                    self.free_sem, self.free0 = [sem(f"{name}_free{b}") for b in banks], [0] * B
                else:
                    n = len(after.at)
                    self.full_sem, self.full0 = after.full_sem, after.full0 + n
                    self.free_sem, self.free0 = after.free_sem, [f + (n - q + B - 1) // B for q, f in enumerate(after.free0)]

            def of(self, key):
                return psum[:, self.banks[self.at[key] % len(self.banks)], :]

            def begin(self, pe, key):
                q = self.at[key] % len(self.banks)
                n = self.free0[q] + self.at[key] // len(self.banks)
                if n:
                    pe.wait_ge(self.free_sem[q], n)

            def full(self, ins):
                ins.then_inc(self.full_sem, 1)

            def wait(self, eng, key):
                eng.wait_ge(self.full_sem, self.full0 + self.at[key] + 1)

            def free(self, ins, key):
                ins.then_inc(self.free_sem[self.at[key] % len(self.banks)], 1)

            def read(self, eng, key):
                q = self.at[key] % len(self.banks)
                eng.wait_ge(self.free_sem[q], self.free0[q] + self.at[key] // len(self.banks) + 1)

        at = AREA
        cqh, cql = (sb(at + i * 3 * T, f"cq_{n}", [P, 3, T], F32R) for i, n in enumerate(("hi", "lo"))); at += 6 * T
        ckh, ckl = (sb(at + i * 2 * T, f"ckv_{n}", [P, 2, T], F32R) for i, n in enumerate(("hi", "lo"))); at += 4 * T
        krh, krl = (sb(at + i * T, f"krope_{n}", [P, T], F32R) for i, n in enumerate(("hi", "lo"))); at += 2 * T
        qrh, qrl = (sb(at + i * 2 * T, f"qrope_{n}", [P, 2, T], F32R) for i, n in enumerate(("hi", "lo"))); at += 4 * T
        V_AT = at
        vh, vl = (sb(at + i * 4096, f"v_{n}", [P, 8, 512], F32R) for i, n in enumerate(("hi", "lo"))); at += 8192
        LOOP_AT = at
        pth, ptl = (sb(at + i * 4096, f"pT_{n}", [P, 8, 512], F32R) for i, n in enumerate(("hi", "lo"))); at += 8192
        prow = sb(at, "p_rows", [P, 2, TP]); at += 2 * TP
        qh, ql = (sb(at + i * T, f"q_{n}", [P, T], F32R) for i, n in enumerate(("hi", "lo"))); at += 2 * T
        knh, knl = (sb(at + i * TP, f"kn_{n}", [P, TP], F32R) for i, n in enumerate(("hi", "lo"))); at += 2 * TP
        LOOP_END = at
        wqh, wql = (sb(at + i * 640, f"whead_{n}", [P, 5, P], F32R) for i, n in enumerate(("hi", "lo"))); at += 1280
        wqraw = sb(at, "whead_raw", [P, 5, P]); at += 640
        wuvh, wuvl = (sb(at + i * 1024, f"wuv_{n}", [P, 2, 512], F32R) for i, n in enumerate(("hi", "lo"))); at += 2048
        stat = sb(at, "softmax_stats", [P, 4, 8]); at += 32
        MLA_END = at
        at = LOOP_AT
        cqraw = sb(at, "cq_raw", [P, 3, T]); at += 3 * T
        ckraw = sb(at, "ckv_raw", [P, 2, T]); at += 2 * T
        krraw = sb(at, "krope_raw", [P, T]); at += T
        rope = sb(at, "rope_tables", [P, 2, T]); at += 2 * T
        sq = sb(at, "squares", [P, 2, T])
        xr = sb(at, "q_rope_in", [P, 2, T]); at += 2 * T
        rst = sb(at, "rstd_rows", [P, T]); at += T
        var = sb(at, "var_rows", [P, T]); at += T
        ntmp = sb(at, "newton_tmp", [P, T]); at += T
        assert at <= LOOP_END
        at = V_AT
        uvraw = sb(at, "wuv_raw", [P, 2, 512]); at += 1024
        wrraw = sb(at, "wqrope_raw", [P, 2, 3, P]); at += 768
        wrh, wrl = (sb(at + i * 768, f"wqrope_{n}", [P, 2, 3, P], F32R) for i, n in enumerate(("hi", "lo"))); at += 1536
        tout = sb(at, "latent_rows", [P, TT, KVR + ROPE]); at += 2880
        assert at <= LOOP_AT

        M_TASKS = [("sqc", b) for b in range(3)] + [("sqq", b) for b in range(3)]
        M_TASKS += [("krd", b) for b in range(3)] + [("krs", b) for b in range(3)]
        M_TASKS += [("tok", t) for t in range(TT)]
        for pr in range(2):
            M_TASKS += [("qr", pr, b) for b in range(3)] + [("qs", pr, b) for b in range(3)]
        M_TASKS += [("v", t) for t in range(8)]
        mb = Banks("mla_setup_bank", list(range(6)), M_TASKS)
        min_loaded = [sem(f"mla_in{i}") for i in range(6)]
        sq_done, mv_done, mr_done, my_done = sem("squares_done"), sem("mla_var"), sem("mla_lnexp"), sem("mla_scaled")
        mh_done, ml_done, rows_done, rows_stored = sem("mla_hi"), sem("mla_lo"), sem("latent_rows_done"), sem("latent_stored")
        kr_done, qx_done, qrope_done = sem("krope_done"), sem("qrope_in"), sem("qrope_done")
        SPLITS = ["wr", "uv", "ck", "cq", "kr", "q0", "q1"] + [f"v{t}" for t in range(8)]

        def split_src(name):
            if name == "wr":
                return wrh[:], wrl[:], wrraw[:]
            if name == "uv":
                return wuvh[:], wuvl[:], uvraw[:]
            if name == "ck":
                return ckh[:], ckl[:], ckraw[:]
            if name == "cq":
                return cqh[:], cql[:], cqraw[:]
            if name == "kr":
                return krh[:], krl[:], krraw[:]
            if name[0] == "q":
                i = int(name[1])
                return qrh[:, i], qrl[:, i], xr[:, i]
            t = int(name[1])
            return vh[:, t], vl[:, t], mb.of(("v", t))

        def hi_of(act, name):
            h, _, s = split_src(name)
            act.activation(h, s, ACT.Copy).then_inc(mh_done, 1)

        def lo_of(dve, name):
            h, l, s = split_src(name)
            dve.wait_ge(mh_done, SPLITS.index(name) + 1)
            ins = dve.tensor_tensor(l, s, h.bitcast(F32), ALU.subtract)
            if name[0] == "v":
                mb.free(ins, ("v", int(name[1])))
            else:
                ins.then_inc(ml_done, 1)

        def split(eng, name):
            eng.wait_ge(ml_done, SPLITS.index(name) + 1)

        def passes(pe, o, pairs, stop=True, start=True):
            n = 3 * len(pairs)
            for i, (w, x) in enumerate((w, x) for (wh, wl), (xh, xl) in pairs for w, x in ((wh, xh), (wh, xl), (wl, xh))):
                mm = pe.matmul(o, w, x, start=(start and i == 0), stop=(stop and i == n - 1))
            return mm

        def sp_mla_in(sp):
            g_read(sp, ("oT", TT - 1), ("oT", TT - 2))
            sp.dma_start(ckraw[:], scratch[ROW_CKV:ROW_CKV + 2].rearrange("m p t -> p m t")).then_inc(min_loaded[0], 16)
            sp.dma_start(cqraw[:], scratch[ROW_CQ:ROW_CQ + 3].rearrange("m p t -> p m t")).then_inc(min_loaded[1], 16)
            sp.dma_start(krraw[0:ROPE, :], scratch[0, 0:ROPE, :]).then_inc(min_loaded[2], 16)
            sp.dma_start(rope[:], a["rope"].rearrange("p (c t) -> p c t", c=2)).then_inc(min_loaded[3], 16)
            uq = a["w_uq"].rearrange("l (k p) (g h c) -> p (l k) g h c", p=P, g=2, h=2)
            for pr in range(2):
                for hh in range(2):
                    sp.dma_start(wrraw[:, pr, :, ROPE * hh:ROPE * hh + ROPE], uq[:, :, pr, hh, NOPE:]).then_inc(min_loaded[4], 16)
            sp.dma_start(uvraw[:], a["w_uv"].rearrange("l (k p) h n -> p (l k) (h n)", p=P)).then_inc(min_loaded[5], 16)
            load_head(sp, 0)
            sp.wait_ge(rows_done, 1)
            for t0, n, o1, o2 in ((0, P, out["ckv_prompt"], out["krope_prompt"]), (8, NB, out["ckv_sample"], out["krope_sample"])):
                ts = slice(0, 8) if t0 == 0 else slice(8, 9)
                for o, c in ((o1, slice(0, KVR)), (o2, slice(KVR, KVR + ROPE))):
                    dst = o[0, 0].rearrange("(t p) c -> p t c", p=P) if t0 == 0 else o[0].rearrange("b t c -> b t c")
                    sp.dma_start(dst, tout[0:n, ts, c]).then_inc(rows_stored, 16)

        wh_loaded, wh_hi, wh_lo = sem("whead_loaded"), sem("whead_hi"), sem("whead_lo")

        def load_head(sp, h):
            if h >= 1:
                sp.wait_ge(wh_lo, h)
            uq = a["w_uq"].rearrange("l (k p) (h c) -> p (l k) h c", p=P, h=HEADS)
            sp.dma_start(wqraw[:, 0:3, :], uq[:, :, h, 0:NOPE]).then_inc(wh_loaded, 16)
            sp.dma_start(wqraw[:, 3:5, :], a["w_uk"].rearrange("l (k p) h n -> p (l k) h n", p=P)[:, :, h, :]).then_inc(wh_loaded, 16)

        def pe_mla_in(pe):
            g_read(pe, ("oT", TT - 1), ("oT", TT - 2))
            for j, (name, nk) in enumerate((("sqc", 2), ("sqq", 3))):
                for b in range(3):
                    mb.begin(pe, (name, b))
                for k in range(nk):
                    pe.wait_ge(sq_done, 2 * j + k + 1)
                    for b in range(3):
                        mm = pe.matmul(mb.of((name, b))[:, 0:BLK], const("ones"), sq[:, (2 * j + k) % 2, b * BLK:(b + 1) * BLK],
                                       start=(k == 0), stop=(k == nk - 1))
                        if k == nk - 1:
                            mb.full(mm)
                        elif b == 2:
                            mm.then_inc(sq_read, 1)
            pe.wait_ge(min_loaded[2], 16)
            for name, c in (("krd", "dup"), ("krs", "swapdup")):
                for b in range(3):
                    mb.begin(pe, (name, b))
                    mb.full(pe.matmul(mb.of((name, b))[:, 0:BLK], const(c)[0:ROPE, :],
                                      krraw[0:ROPE, b * BLK:(b + 1) * BLK], start=True, stop=True))
            pe.wait_ge(kr_done, 1)
            pe.wait_ge(my_done, 1)
            for t in range(TT):
                c0, n = tok(t)
                mb.begin(pe, ("tok", t))
                o = mb.of(("tok", t))
                for k in range(2):
                    pe.transpose(o[0:n, k * P:(k + 1) * P], ckraw[:, k, c0:c0 + n], ident)
                mb.full(pe.transpose(o[0:n, KVR:KVR + ROPE], krraw[0:ROPE, c0:c0 + n], ident[0:ROPE, 0:ROPE]))
            split(pe, "cq")
            for pr in range(2):
                for b in range(3):
                    mb.begin(pe, ("qr", pr, b))
                    c = slice(b * BLK, (b + 1) * BLK)
                    mb.full(passes(pe, mb.of(("qr", pr, b))[:, 0:BLK],
                                   [((wrh[:, pr, k], wrl[:, pr, k]), (cqh[:, k, c], cql[:, k, c])) for k in range(3)]))
                for b in range(3):
                    mb.begin(pe, ("qs", pr, b))
                    pe.wait_ge(qx_done, 3 * pr + b + 1)
                    mb.full(pe.matmul(mb.of(("qs", pr, b))[:, 0:BLK], const("swap"), xr[:, pr, b * BLK:(b + 1) * BLK], start=True, stop=True))
            pe.wait_ge(rows_stored, 64)
            for t in range(8):
                mb.begin(pe, ("v", t))
                c = slice(t * P, (t + 1) * P)
                mb.full(passes(pe, mb.of(("v", t)), [((ckh[:, k, c], ckl[:, k, c]), (wuvh[:, k], wuvl[:, k])) for k in range(2)]))

        sq_read = sem("squares_read")

        def act_mla_in(act):
            g_read(act, ("oT", TT - 1), ("oT", TT - 2))
            for j in range(5):
                act.wait_ge(min_loaded[0 if j < 2 else 1], 16)
                if j == 2:
                    act.wait_ge(sq_read, 1)
                if j == 3:
                    mb.wait(act, ("sqc", 2))
                if j == 4:
                    act.wait_ge(sq_read, 2)
                act.activation(sq[:, j % 2, :], (ckraw[:, j] if j < 2 else cqraw[:, j - 2]), ACT.Square).then_inc(sq_done, 1)
            act.wait_ge(min_loaded[4], 64)
            hi_of(act, "wr")
            act.wait_ge(min_loaded[5], 16)
            hi_of(act, "uv")
            for j, name in enumerate(("ck", "cq")):
                act.wait_ge(mv_done, j + 1)
                alink(act, act.activation(rst[:], var[:], ACT.Ln))
                act.activation(rst[:], rst[:], ACT.Exp, scale=-0.5).then_inc(mr_done, 1)
                act.wait_ge(my_done, j + 1)
                hi_of(act, name)
            act.wait_ge(kr_done, 1)
            hi_of(act, "kr")
            for pr in range(2):
                for b in range(3):
                    mb.wait(act, ("qr", pr, b))
                    ins = act.activation(xr[:, pr, b * BLK:(b + 1) * BLK], mb.of(("qr", pr, b))[:, 0:BLK], ACT.Copy)
                    mb.free(ins, ("qr", pr, b))
                    mb.read(act, ("qr", pr, b))
                    act.sem_inc(qx_done, 1)
                act.wait_ge(qrope_done, pr + 1)
                hi_of(act, f"q{pr}")
            for t in range(8):
                mb.wait(act, ("v", t))
                hi_of(act, f"v{t}")
            head_hi(act, 0)

        def head_hi(act, h):
            act.wait_ge(wh_loaded, 32 * (h + 1))
            if h >= 1:
                wk.wait(act, ("k", h - 1, 1))
            act.activation(wqh[:], wqraw[:], ACT.Copy).then_inc(wh_hi, 1)

        def head_lo(dve, h):
            dve.wait_ge(wh_hi, h + 1)
            dve.tensor_tensor(wql[:], wqraw[:], wqh[:].bitcast(F32), ALU.subtract).then_inc(wh_lo, 1)

        def dve_mla_in(dve):
            lo_of(dve, "wr")
            lo_of(dve, "uv")
            for j, (name, nm, raw, nk, g) in enumerate((("ck", "sqc", ckraw, 2, KVN), ("cq", "sqq", cqraw, 3, QN))):
                for b in range(3):
                    mb.wait(dve, (nm, b))
                    mb.free(dve.tensor_scalar(var[:, b * BLK:(b + 1) * BLK], mb.of((nm, b))[:, 0:BLK], 1.0 / (nk * P), EPS,
                                              ALU.mult, ALU.add), (nm, b))
                mb.read(dve, (nm, 2))
                dve.sem_inc(mv_done, 1)
                dve.wait_ge(mr_done, j + 1)
                newton(dve, rst[:], var[:], ntmp[:])
                for k in range(nk):
                    ins = dve.scalar_tensor_tensor(raw[:, k], raw[:, k], cols[:, g + k:g + k + 1], rst[:], ALU.mult, ALU.mult)
                ins.then_inc(my_done, 1)
                lo_of(dve, name)
            dve.wait_ge(min_loaded[3], 16)
            rotate(dve, "krd", "krs", krraw)
            dve.wait_ge(kr_done, 1)
            lo_of(dve, "kr")
            for t in range(TT):
                c0, n = tok(t)
                mb.wait(dve, ("tok", t))
                mb.free(dve.tensor_copy(tout[0:n, t, :], mb.of(("tok", t))[0:n, 0:KVR + ROPE]), ("tok", t))
            mb.read(dve, ("tok", TT - 1))
            dve.sem_inc(rows_done, 1)
            for pr in range(2):
                for b in range(3):
                    c = slice(b * BLK, (b + 1) * BLK)
                    mb.wait(dve, ("qs", pr, b))
                    dlink(dve, dve.tensor_tensor(xr[:, pr, c], xr[:, pr, c], rope[:, 0, c], ALU.mult))
                    mb.free(dve.tensor_tensor(ntmp[:, c], mb.of(("qs", pr, b))[:, 0:BLK], rope[:, 1, c], ALU.mult), ("qs", pr, b))
                    mb.read(dve, ("qs", pr, b))
                    dlink(dve, dve.tensor_tensor(xr[:, pr, c], xr[:, pr, c], ntmp[:, c], ALU.add))
                dve.sem_inc(qrope_done, 1)
                dlink(dve, dve.tensor_copy(smp[:, 32 + 8 * pr:40 + 8 * pr], xr[:, pr, TP:T]))
                lo_of(dve, f"q{pr}")
            dve.tensor_copy(smp[:, 48:64].rearrange("p (k b) -> p k b", k=2), ckraw[:, :, TP:T])
            dlink(dve, dve.tensor_copy(smp[:, 64:72], krraw[:, TP:T]))
            for t in range(8):
                lo_of(dve, f"v{t}")
            head_lo(dve, 0)

        def rotate(dve, plain, swapped, o):
            for b in range(3):
                c = slice(b * BLK, (b + 1) * BLK)
                mb.wait(dve, (swapped, b))
                mb.wait(dve, (swapped, 2))
                mb.free(dve.tensor_tensor(o[:, c], mb.of((plain, b))[:, 0:BLK], rope[:, 0, c], ALU.mult), (plain, b))
                mb.free(dve.tensor_tensor(ntmp[:, c], mb.of((swapped, b))[:, 0:BLK], rope[:, 1, c], ALU.mult), (swapped, b))
            mb.read(dve, (swapped, 2))
            mb.read(dve, (plain, 2))
            dve.tensor_tensor(o[:], o[:], ntmp[:], ALU.add).then_inc(kr_done, 1)

        UNITS = 8 * HEADS
        W_TASKS = []
        for v in range(UNITS + 3):
            if v == 0:
                W_TASKS += [("q", 0, b) for b in range(3)] + [("k", 0, b) for b in range(2)]
            if v >= 3 and (v - 3) % 4 == 3:
                W_TASKS += [("pv", (v - 3) // 8, (v - 3) % 8 // 4)]
            if v % 8 == 7 and v // 8 + 1 < HEADS:
                W_TASKS += [("q", v // 8 + 1, b) for b in range(3)] + [("k", v // 8 + 1, b) for b in range(2)]
        wk = Banks("head_bank", [6, 7], W_TASKS)
        tp = Banks("pT_bank", [4, 5], [(u, g) for u in range(UNITS) for g in range(1 + (u % 8 >= 4))])
        sc_full, nb_done, ex_done, pn_done, wk_hi, tp_hi = (sem(n) for n in (
            "scores_full", "softmax_bias", "softmax_exp", "p_normed", "head_hi_part", "pT_hi_part"))
        HI = [k for k in W_TASKS if k[0] != "pv"]

        def sc_view(u):
            i = u % 8
            w = max((i + 1) * P, 256)
            nb = 1 if w <= 512 else 2
            return psum[:, 2 * (u % 2):2 * (u % 2) + nb, 0:w // nb], nb, w // nb

        def sc_used(u):
            s, nb, w = sc_view(u)
            return s[:, :, 0:P] if u % 8 == 0 else s

        def blocks(u, g):
            return range(4 * g, min(4 * g + 4, u % 8 + 1))

        def pe_qk(pe, h):
            pe.wait_ge(wh_lo, h + 1)
            for b in range(3):
                wk.begin(pe, ("q", h, b))
                c = slice(b * BLK, (b + 1) * BLK)
                wk.full(passes(pe, wk.of(("q", h, b))[:, 0:BLK], [((wqh[:, k], wql[:, k]), (cqh[:, k, c], cql[:, k, c])) for k in range(3)]))
            for b in range(2):
                wk.begin(pe, ("k", h, b))
                c = slice(b * 512, b * 512 + 512)
                wk.full(passes(pe, wk.of(("k", h, b)), [((wqh[:, 3 + k], wql[:, 3 + k]), (ckh[:, k, c], ckl[:, k, c])) for k in range(2)]))

        def act_qk(act, h):
            for key in [("q", h, b) for b in range(3)] + [("k", h, b) for b in range(2)]:
                wk.wait(act, key)
                b = key[2]
                if key[0] == "q":
                    ins = act.activation(qh[:, b * BLK:(b + 1) * BLK], wk.of(key)[:, 0:BLK], ACT.Copy)
                else:
                    ins = act.activation(knh[:, b * 512:b * 512 + 512], wk.of(key), ACT.Copy)
                ins.then_inc(wk_hi, 1)

        def dve_qk(dve, h):
            for key in [("q", h, b) for b in range(3)] + [("k", h, b) for b in range(2)]:
                dve.wait_ge(wk_hi, HI.index(key) + 1)
                b = key[2]
                if key[0] == "q":
                    if b == 2:
                        dve.tensor_copy(smp[:, 8 * h:8 * h + 8], wk.of(key)[:, BLK - NB:BLK])
                    c = slice(b * BLK, (b + 1) * BLK)
                    ins = dve.tensor_tensor(ql[:, c], wk.of(key)[:, 0:BLK], qh[:, c].bitcast(F32), ALU.subtract)
                else:
                    c = slice(b * 512, b * 512 + 512)
                    ins = dve.tensor_tensor(knl[:, c], wk.of(key), knh[:, c].bitcast(F32), ALU.subtract)
                wk.free(ins, key)

        def pe_mla(pe):
            pe_qk(pe, 0)
            for v in range(UNITS + 3):
                if v < UNITS:
                    h, i = v // 8, v % 8
                    if i == 0:
                        wk.read(pe, ("k", h, 1))
                        wk.read(pe, ("k", h, 0))
                        if h == 0:
                            mb.read(pe, ("v", 7)), mb.read(pe, ("v", 6))
                    if v >= 2:
                        pe.wait_ge(ex_done, v - 1)
                    s, nb, w = sc_view(v)
                    qc, r = slice(i * P, (i + 1) * P), slice(ROPE * (h % 2), ROPE * (h % 2) + ROPE)
                    for p in range(nb):
                        kc = slice(p * w, (p + 1) * w)
                        mm = passes(pe, s[:, p, :], [((qh[:, qc], ql[:, qc]), (knh[:, kc], knl[:, kc])),
                                                     ((qrh[r, h // 2, qc], qrl[r, h // 2, qc]), (krh[r, kc], krl[r, kc]))])
                    mm.then_inc(sc_full, 1)
                u = v - 3
                if u >= 0 and u % 4 == 3:
                    h, hf = u // 8, u % 8 // 4
                    key = ("pv", h, hf)
                    tp.read(pe, (u, len(range(1 + (u % 8 >= 4))) - 1))
                    if hf:
                        tp.read(pe, (u, 0))
                    wk.begin(pe, key)
                    for j in range(4 * hf + 4):
                        q0 = max(0, j - 4 * hf) * P
                        for n, (vv, pp) in enumerate(((vh, pth), (vh, ptl), (vl, pth))):
                            mm = pe.matmul(wk.of(key)[:, q0:512], vv[:, j, h * P:(h + 1) * P], pp[:, j, q0:512],
                                           start=(j == 0 and n == 0), stop=(j == 4 * hf + 3 and n == 2))
                    wk.full(mm)
                u = v - 2
                if 0 <= u < UNITS:
                    pe.wait_ge(pn_done, u + 1)
                    for g in range(1 + (u % 8 >= 4)):
                        tp.begin(pe, (u, g))
                        for j in blocks(u, g):
                            mm = pe.transpose(tp.of((u, g))[:, (j % 4) * P:(j % 4 + 1) * P], prow[:, u % 2, j * P:(j + 1) * P], ident)
                        tp.full(mm)
                if v % 8 == 7 and v // 8 + 1 < HEADS:
                    pe_qk(pe, v // 8 + 1)

        def pt_cols(t, u, g):
            b = blocks(u, g)
            return t[:, b[0]:b[-1] + 1, (u % 4) * P:(u % 4 + 1) * P]

        def tp_cols(u, g):
            return tp.of((u, g))[:, 0:len(blocks(u, g)) * P].rearrange("p (j c) -> p j c", c=P)

        def act_mla(act):
            act_qk(act, 0)
            for v in range(UNITS + 2):
                if v < UNITS:
                    act.wait_ge(nb_done, v + 1)
                    if v >= 2:
                        tp.wait(act, (v - 2, 1 if (v - 2) % 8 >= 4 else 0))
                    s = sc_used(v)
                    act.activation(prow[:, v % 2, 0:(v % 8 + 1) * P].rearrange("p (n w) -> p n w", n=s.shape[1]), s, ACT.Exp,
                                   scale=SCALE, bias=stat[:, v % 4, 1:2], accum_out=stat[:, v % 4, 2:3]).then_inc(ex_done, 1)
                u = v - 2
                if 0 <= u:
                    for g in range(1 + (u % 8 >= 4)):
                        tp.wait(act, (u, g))
                        act.activation(pt_cols(pth, u, g), tp_cols(u, g), ACT.Copy).then_inc(tp_hi, 1)
                if v % 8 == 7 and v // 8 + 1 < HEADS:
                    act_qk(act, v // 8 + 1)
                if v % 8 == 1 and v // 8 + 1 < HEADS:
                    head_hi(act, v // 8 + 1)

        def dve_mla(dve):
            dve_qk(dve, 0)
            for v in range(UNITS + 3):
                if v < UNITS:
                    s, nb, w = sc_view(v)
                    i = v % 8
                    dve.wait_ge(sc_full, v + 1)
                    diag = s[:, 0, 0:P] if i == 0 else s[:, nb - 1, w - P:w]
                    dlink(dve, dve.tensor_tensor(diag, diag, const("causal"), ALU.add))
                    dlink(dve, dve.tensor_reduce(stat[:, v % 4, 0:1], sc_used(v), AX.XY, ALU.max))
                    dve.tensor_scalar(stat[:, v % 4, 1:2], stat[:, v % 4, 0:1], -SCALE, None, ALU.mult).then_inc(nb_done, 1)
                u = v - 1
                if 0 <= u < UNITS:
                    dve.wait_ge(ex_done, u + 1)
                    dlink(dve, dve.reciprocal(stat[:, u % 4, 3:4], stat[:, u % 4, 2:3]))
                    c = slice(0, (u % 8 + 1) * P)
                    dve.tensor_scalar(prow[:, u % 2, c], prow[:, u % 2, c], stat[:, u % 4, 3:4], None, ALU.mult).then_inc(pn_done, 1)
                u = v - 3
                if u >= 0 and u % 4 == 3:
                    h, hf = u // 8, u % 8 // 4
                    key = ("pv", h, hf)
                    wk.wait(dve, key)
                    wk.free(dve.tensor_copy(mixT[:, h, hf * 512:hf * 512 + 512], wk.of(key)), key)
                u = v - 2
                if 0 <= u < UNITS:
                    for g in range(1 + (u % 8 >= 4)):
                        dve.wait_ge(tp_hi, tp.at[(u, g)] + 1)
                        tp.free(dve.tensor_tensor(pt_cols(ptl, u, g), tp_cols(u, g), pt_cols(pth, u, g).bitcast(F32), ALU.subtract), (u, g))
                if v % 8 == 7 and v // 8 + 1 < HEADS:
                    dve_qk(dve, v // 8 + 1)
                if v % 8 == 1 and v // 8 + 1 < HEADS:
                    head_lo(dve, v // 8 + 1)

        def sp_mla(sp):
            for h in range(1, HEADS):
                load_head(sp, h)

        RB = (KVR + ROPE) // 32
        at = AREA
        NAT = 3
        nat = sb(at, "ckv_pages", [P, NAT, PAGES, KVR]); at += NAT * PAGES * KVR
        krn = sb(at, "krope_pages", [P, NAT, PAGES, ROPE]); at += NAT * PAGES * ROPE
        oacc = sb(at, "o_past", [4, NB, KVR])
        cnew = sb(at + NB * KVR, "ckv_new_rows", [4, NB, KVR])
        tt = sb(at, "pages_T", [P, 2, RB, PAGES * 32]); at += 2 * RB * PAGES * 32
        qb = sb(at, "q_blocks", [P, NB, RB, P]); at += NB * RB * P
        pex = sb(at, "p_decode", [P, 2, 512]); at += 1024
        pet = sb(at, "p_decode_T", [P, 2, PAGES, 32]); at += 1024
        ukr = sb(at, "wuk_raw", [P, 2, 512])
        ukt = sb(at + 1024, "wuk_T", [P, HEADS, 2, P])
        o4 = sb(at, "o_groups", [P, NB, KVR]); at += NB * KVR
        qlat = sb(at, "q_latent", [P, 2, 32]); at += 64
        uvf = sb(at, "wuv_f32", [P, 2, 512]); at += 1024
        olat = sb(at, "o_latent", [P, 2, NB, HEADS]); at += 64
        mcol = sb(at, "row_max", [P, 8]); at += 8
        mrow = sb(at, "minus_max_row", [1, 2, 4, 32]); at += 256
        m4 = sb(at, "head_max", [1, 8]); at += 8
        bias = sb(at, "exp_bias", [P, NB]); at += 8
        rsum = sb(at, "exp_sums", [P, NB]); at += 8
        snew = sb(at, "new_products", [P, 3, 32]); at += 96
        half1 = sb(at, "half_rows", [P, 2, 8]); at += 16
        mg = sb(at, "merge", [4, 12, NB]); at += 96
        sn4 = sb(at, "new_scores", [4, 4, NB]); at += 32
        assert at <= 53200, at

        DP_TASKS = [("ukT", i) for i in range(2)] + [("qlat",), ("spread",), ("snew",)]
        for v in range(NB + 2):
            if 1 <= v <= NB:
                DP_TASKS += [("mT", v - 1), ("bias", v - 1)]
        DP_TASKS += [("lsum",)] + [("osum", q) for q in range(4)] + [("oT",), ("uv",)]
        dq = Banks("decode_bank", [4, 5, 6, 7], DP_TASKS)
        ds = Banks("decode_scores", [0, 1], list(range(NB)))
        dv = Banks("decode_values", [2, 3], list(range(NB)))
        pt_loaded, duk_loaded, duv_loaded, cnew_loaded = (sem(n) for n in ("page_table_loaded", "wuk_loaded", "wuv_f32_loaded", "ckv_new_loaded"))
        nat_loaded = [sem(f"ckv_pages_loaded{i}") for i in range(NAT)]
        krn_loaded = [sem(f"krope_pages_loaded{i}") for i in range(NAT)]
        tt_done, max_done, dexp_done, pet_done, qb_done, sp_done = (sem(n) for n in (
            "pages_transposed", "decode_max", "decode_exp", "p_decode_transposed", "q_blocks_done", "new_products_done"))
        mrow_done, bias_done, mg_done, om_done, w_exp, half_done, qb_zero = (sem(n) for n in (
            "minus_max_done", "bias_done", "merge_differences", "o_merged", "merge_exps", "half_rows_done", "q_blocks_zero"))

        def sp_decode(sp):
            sp.dma_start(pt[:], a["page_table"].rearrange("(o b) n -> o (b n)", o=1)).then_inc(pt_loaded, 16)
            wk.read(sp, ("pv", 3, 1)), wk.read(sp, ("pv", 3, 0))
            sp.dma_start(ukr[:], a["w_uk"].rearrange("l (k p) h n -> p (l k) (h n)", p=P)).then_inc(duk_loaded, 16)
            sp.dma_start(uvf[:], a["w_uv"].rearrange("l (k p) h n -> p (l k) (h n)", p=P)).then_inc(duv_loaded, 16)
            sp.wait_ge(pt_loaded, 16)
            for b in range(NB):
                if b >= NAT:
                    dv.wait(sp, b - NAT)
                    sp.wait_ge(tt_done, b - NAT + 1)
                for j, page in enumerate(pages_of(sp, b)):
                    if j < SP_KR:
                        load_kr(sp, b, j, page, nat_loaded)
                    sp.dma_start(nat[:, b % NAT, j, :], a["cache_ckv"][0, bass.ds(page, 1)].rearrange("o p c -> (o p) c")).then_inc(nat_loaded[b % NAT], 16)
            sp.wait_ge(rows_stored, 64)
            ds.wait(sp, NB - 1), ds.wait(sp, NB - 2)
            sp.dma_start(cnew[:], out["ckv_sample"][0].rearrange("b t c -> t b c").broadcast_to([4, NB, KVR])).then_inc(cnew_loaded, 16)

        SP_KR = 2

        def load_kr(eng, b, j, page, loaded):
            src = a["cache_krope"][0, bass.ds(page, 1)].rearrange("o p c -> (o p) c")
            eng.dma_start(krn[:, b % NAT, j, :], src).then_inc(loaded[b % NAT], 16)

        def pages_of(eng, b, j0=0):
            return [eng.value_load(pt[0:1, b * PAGES + j:b * PAGES + j + 1], min_val=0, max_val=N_PHYS - 1) for j in range(j0, PAGES)]

        def pool_decode(pool):
            wk.read(pool, ("pv", 3, 1)), wk.read(pool, ("pv", 3, 0))
            pool.wait_ge(pt_loaded, 16)
            for b in range(NB):
                if b >= NAT:
                    pool.wait_ge(tt_done, b - NAT + 1)
                for j, page in enumerate(pages_of(pool, b, SP_KR)):
                    load_kr(pool, b, SP_KR + j, page, krn_loaded)

        def pe_decode(pe):
            pe.wait_ge(duk_loaded, 16)
            for i in range(2):
                dq.begin(pe, ("ukT", i))
                for j in range(4):
                    h, k = (4 * i + j) // 2, j % 2
                    mm = pe.transpose(dq.of(("ukT", i))[:, j * P:(j + 1) * P], ukr[:, k, h * P:(h + 1) * P], ident)
                dq.full(mm)
            dq.begin(pe, ("qlat",))
            dq.read(pe, ("ukT", 0)), dq.read(pe, ("ukT", 1))
            for h in range(HEADS):
                for k in range(2):
                    mm = pe.matmul(dq.of(("qlat",))[:, 32 * k + 8 * h:32 * k + 8 * h + 8], ukt[:, h, k, :], smp[:, 8 * h:8 * h + 8],
                                   start=True, stop=True)
            dq.full(mm)
            dq.begin(pe, ("spread",))
            dq.read(pe, ("qlat",))
            o = dq.of(("spread",))
            for rq in range(4):
                for k in range(2):
                    rb = 4 * k + rq
                    pe.matmul(o[:, 32 * rb:32 * rb + 32], const("spread")[:, rq * P:(rq + 1) * P], qlat[:, k, :], start=True, stop=True)
                hh, eb_ = rq // 2, rq % 2
                mm = pe.matmul(o[:, 32 * (8 + eb_):32 * (9 + eb_)].rearrange("p (r h b) -> p r h b", r=2, h=2)[:, :, hh, :],
                               const("spread")[:, rq * P:(rq + 1) * P], smp[:, 32:48].rearrange("p (r b) -> p r b", r=2), start=True, stop=True)
            dq.full(mm)
            dq.begin(pe, ("snew",))
            pe.wait_ge(sp_done, 1)
            o = dq.of(("snew",))
            pe.matmul(o[0:4, 0:32], const("ones")[:, 0:4], snew[:, 0, :], start=True, stop=False)
            pe.matmul(o[0:4, 0:32], const("ones")[:, 0:4], snew[:, 1, :], start=False, stop=False)
            dq.full(pe.matmul(o[0:4, 0:32], const("ones")[:, 0:4], snew[:, 2, :], start=False, stop=True))
            def values(u):
                dv.begin(pe, u)
                pe.wait_ge(pet_done, u + 1)
                for j in range(PAGES):
                    g = j % 4
                    mm = pe.matmul(dv.of(u)[32 * g:32 * g + 32, 0:KVR], pet[:, u % 2, j, :], nat[:, u % NAT, j, :],
                                   start=(j < 4), stop=(j >= PAGES - 4))
                dv.full(mm)

            def minus_max(u):
                dq.begin(pe, ("bias", u))
                pe.wait_ge(mrow_done, u + 1)
                dq.full(pe.matmul(dq.of(("bias", u))[:, 0:1], mrow[0:1, u % 2].rearrange("o k h -> o (k h)"), const("ones")[0:1, 0:1], start=True, stop=True))

            pe.wait_ge(qb_done, 1)
            for v in range(NB + 1):
                u = v - 1
                if u >= 1:
                    values(u - 1)
                if u >= 0:
                    dq.begin(pe, ("mT", u))
                    pe.wait_ge(max_done, u + 1)
                    dq.full(pe.transpose(dq.of(("mT", u))[0:1, 0:P], mcol[:, u:u + 1], ident))
                if v < NB:
                    ds.begin(pe, v)
                    pe.wait_ge(tt_done, v + 1)
                    for r in range(RB):
                        if r == RB // 2 and u >= 0:
                            minus_max(u)
                        mm = pe.matmul(ds.of(v), qb[:, v, r, :], tt[:, v % 2, r, :], start=(r == 0), stop=(r == RB - 1))
                    ds.full(mm)
            minus_max(NB - 1)
            values(NB - 1)
            dq.begin(pe, ("lsum",))
            dq.full(pe.matmul(dq.of(("lsum",))[0:4, 0:NB], const("sumkq"), rsum[:], start=True, stop=True))
            dv.read(pe, NB - 1), dv.read(pe, NB - 2)
            for q in range(4):
                dq.begin(pe, ("osum", q))
                dq.full(pe.matmul(dq.of(("osum", q))[0:4, :], const("sumkq"), o4[:, 2 * q:2 * q + 2, :].rearrange("p b c -> p (b c)"), start=True, stop=True))
            dq.begin(pe, ("oT",))
            pe.wait_ge(om_done, 1)
            for k in range(2):
                for b in range(NB):
                    mm = pe.transpose(dq.of(("oT",))[:, (k * NB + b) * 4:(k * NB + b) * 4 + 4], oacc[:, b, k * P:(k + 1) * P], ident[0:4, 0:4])
            dq.full(mm)
            dq.begin(pe, ("uv",))
            dq.read(pe, ("oT",))
            pe.wait_ge(duv_loaded, 16)
            for h in range(HEADS):
                for k in range(2):
                    mm = pe.matmul(dq.of(("uv",))[:, NB * h:NB * h + NB], uvf[:, k, h * P:(h + 1) * P], olat[:, k, :, h], start=(k == 0), stop=(k == 1))
            dq.full(mm)

        def act_decode(act):
            for i in range(2):
                key = ("ukT", i)
                dq.wait(act, key)
                dq.free(act.activation(ukt[:, 2 * i:2 * i + 2].rearrange("p h k c -> p (h k c)"), dq.of(key), ACT.Copy), key)
            dq.wait(act, ("qlat",))
            dq.free(act.activation(qlat[:].rearrange("p k c -> p (k c)"), dq.of(("qlat",))[:, 0:64], ACT.Copy), ("qlat",))
            for v in range(NB + 1):
                u = v - 1
                if u >= 0:
                    act.wait_ge(bias_done, u + 1)
                    if u >= 2:
                        act.wait_ge(pet_done, u - 1)
                    ds.wait(act, u)
                    ds.free(act.activation(pex[:, u % 2], ds.of(u), ACT.Exp, scale=SCALE, bias=bias[:, u:u + 1],
                                           accum_out=rsum[:, u:u + 1]), u)
                if u >= 1:
                    dv.wait(act, u - 1)
                    dv.free(act.activation(o4[:, u - 1, :], dv.of(u - 1)[:, 0:KVR], ACT.Copy), u - 1)
            dv.wait(act, NB - 1)
            dv.free(act.activation(o4[:, NB - 1, :], dv.of(NB - 1)[:, 0:KVR], ACT.Copy), NB - 1)
            act.wait_ge(mg_done, 1)
            act.activation(mg[:, 3:5], mg[:, 3:5], ACT.Exp).then_inc(w_exp, 1)

        def dve_decode(dve):
            wk.read(dve, ("pv", 3, 1))
            dve.memset(qb[:, 0:4], 0.0)
            dlink(dve, dve.memset(qb[:, 4:8], 0.0))
            dlink(dve, dve.memset(mrow[:], 0.0))
            dq.wait(dve, ("spread",))
            src = dq.of(("spread",))[:, 0:32 * RB].rearrange("p (r h b) -> p r h b", r=RB, h=HEADS)
            for kq in range(4):
                q = slice(32 * kq, 32 * kq + 32)
                for h in range(HEADS):
                    ins = dve.tensor_copy(qb[q, :, :, 32 * kq + h], src[q, :, h, :].rearrange("p r b -> p b r"))
            dq.free(ins, ("spread",))
            dq.read(dve, ("spread",))
            dve.sem_inc(qb_done, 1)
            for k in range(2):
                dve.tensor_tensor(snew[:, k].rearrange("p (h b) -> p h b", h=HEADS), qlat[:, k].rearrange("p (h b) -> p h b", h=HEADS),
                                  smp[:, 48 + 8 * k:56 + 8 * k].unsqueeze(1).broadcast_to([P, HEADS, NB]), ALU.mult)
            dlink(dve, dve.memset(snew[:, 2], 0.0))
            for hh in range(2):
                r = half(hh)
                ins = dve.tensor_tensor(snew[r, 2].rearrange("p (r h b) -> p r h b", r=2, h=2)[:, :, hh, :],
                                        smp[r, 32:48].rearrange("p (r b) -> p r b", r=2), smp[r, 64:72].unsqueeze(1).broadcast_to([DK, 2, NB]), ALU.mult)
            ins.then_inc(sp_done, 1)
            dq.wait(dve, ("snew",))
            dq.free(dve.tensor_tensor(sn4[:], dq.of(("snew",))[0:4, 0:32].rearrange("p (h b) -> p h b", h=HEADS),
                                      const("diagh", 4).unsqueeze(2).broadcast_to([4, HEADS, NB]), ALU.mult), ("snew",))
            dq.read(dve, ("snew",))
            dlink(dve, dve.tensor_reduce(mg[:, 0], sn4[:].rearrange("p h b -> p b h"), AX.X, ALU.add))
            def pages_T(v):
                if v >= 2:
                    ds.wait(dve, v - 2)
                dve.wait_ge(nat_loaded[v % NAT], 16 * (PAGES + SP_KR) * (v // NAT + 1))
                dve.transpose(tt[:, v % 2, 0:8, :].rearrange("p r (t c) -> p t r c", c=32), nat[:, v % NAT].rearrange("p t (r c) -> p t r c", c=32))
                dve.wait_ge(krn_loaded[v % NAT], 16 * (PAGES - SP_KR) * (v // NAT + 1))
                dve.transpose(tt[:, v % 2, 8:10, :].rearrange("p r (t c) -> p t r c", c=32),
                              krn[:, v % NAT].rearrange("p t (r c) -> p t r c", c=32)).then_inc(tt_done, 1)

            pages_T(0)
            for u in range(NB):
                if u + 1 < NB:
                    pages_T(u + 1)
                ds.wait(dve, u)
                dve.tensor_reduce(mcol[:, u:u + 1], ds.of(u), AX.X, ALU.max).then_inc(max_done, 1)
                dq.wait(dve, ("mT", u))
                dq.free(dve.tensor_reduce(m4[0:1, 0:4], dq.of(("mT", u))[0:1, 0:P].rearrange("o (k h) -> o h k", k=4)[:, 0:4, :], AX.X, ALU.max), ("mT", u))
                dq.read(dve, ("mT", u))
                dve.tensor_scalar(mrow[0:1, u % 2, :, 0:4], m4[0:1, 0:4].unsqueeze(1).broadcast_to([1, 4, 4]), -SCALE, None, ALU.mult).then_inc(mrow_done, 1)
                dq.wait(dve, ("bias", u))
                dq.free(dve.tensor_copy(bias[:, u:u + 1], dq.of(("bias", u))[:, 0:1]), ("bias", u))
                dq.read(dve, ("bias", u))
                dve.sem_inc(bias_done, 1)
                ds.read(dve, u)
                if u >= 2:
                    dv.wait(dve, u - 2)
                dve.transpose(pet[:, u % 2].rearrange("p t c -> p (t c)"), pex[:, u % 2]).then_inc(pet_done, 1)
            dlink(dve, dve.tensor_scalar(mg[:, 0], mg[:, 0], SCALE, None, ALU.mult))
            dlink(dve, dve.tensor_scalar(mg[:, 1], bias[0:4, :], -1.0, None, ALU.mult))
            dlink(dve, dve.tensor_tensor(mg[:, 2], mg[:, 0], mg[:, 1], ALU.max))
            dve.tensor_tensor(mg[:, 3], mg[:, 1], mg[:, 2], ALU.subtract)
            dve.tensor_tensor(mg[:, 4], mg[:, 0], mg[:, 2], ALU.subtract).then_inc(mg_done, 1)
            dve.wait_ge(w_exp, 1)
            dq.wait(dve, ("lsum",))
            dq.free(dve.tensor_tensor(mg[:, 5], dq.of(("lsum",))[0:4, 0:NB], mg[:, 3], ALU.mult), ("lsum",))
            dq.read(dve, ("lsum",))
            dlink(dve, dve.tensor_tensor(mg[:, 6], mg[:, 5], mg[:, 4], ALU.add))
            dlink(dve, dve.reciprocal(mg[:, 7], mg[:, 6]))
            dve.tensor_tensor(mg[:, 8], mg[:, 3], mg[:, 7], ALU.mult)
            dlink(dve, dve.tensor_tensor(mg[:, 9], mg[:, 4], mg[:, 7], ALU.mult))
            dve.wait_ge(cnew_loaded, 16)
            for q in range(4):
                key = ("osum", q)
                dq.wait(dve, key)
                dq.free(dve.tensor_tensor(oacc[:, 2 * q:2 * q + 2, :], dq.of(key)[0:4, :].rearrange("p (b c) -> p b c", b=2),
                                          mg[:, 8, 2 * q:2 * q + 2].unsqueeze(2).broadcast_to([4, 2, KVR]), ALU.mult), key)
            dlink(dve, dve.tensor_tensor(cnew[:], cnew[:], mg[:, 9].unsqueeze(2).broadcast_to([4, NB, KVR]), ALU.mult))
            dq.read(dve, ("osum", 3))
            dve.tensor_tensor(oacc[:], oacc[:], cnew[:], ALU.add).then_inc(om_done, 1)
            dq.wait(dve, ("oT",))
            dq.free(dve.tensor_copy(olat[:].rearrange("p k b h -> p (k b h)"), dq.of(("oT",))[:, 0:64]), ("oT",))
            dq.wait(dve, ("uv",))
            dq.free(dve.tensor_copy(mixT[:, 0:4, TP:T], dq.of(("uv",))[:, 0:32].rearrange("p (h b) -> p h b", h=HEADS)), ("uv",))

        at = AREA
        x1h, x1l = (sb(at + i * KD * T, f"x1_{n}", [P, KD, T], F32R) for i, n in enumerate(("hi", "lo"))); at += 2 * KD * T
        WO_AT = at
        woh, wol = (sb(at + i * 8192, f"wout_{n}", [P, KD, D], F32R) for i, n in enumerate(("hi", "lo"))); at += 16384
        woraw = sb(at, "wout_raw", [P, 2, D]); at += 2 * D
        mxh, mxl = (sb(at + i * 2048, f"mix_{n}", [P, 2, KD, P], F32R) for i, n in enumerate(("hi", "lo"))); at += 4096
        zrow = sb(at, "z_rows", [P, 2, D]); at += 2 * D
        x1t = sb(at, "x1_tile", [P, KD, P]); at += D
        lst = sb(at, "ln1_stats", [P, 2, 24]); at += 48
        assert at <= 53200
        wo_loaded = [sem(f"wout_loaded{i}") for i in range(2)]
        xr_loaded = [sem(f"x_rows_loaded{i}") for i in range(2)]
        wo_hi, wo_lo, mx_hi, mx_lo, wo_mm, z_done, zv_done, zy_done, zn_done = (sem(n) for n in (
            "wout_hi_done", "wout_lo_done", "mix_hi_done", "mix_lo_done", "wout_multiplied", "z_done", "ln1_var", "ln1_lnexp", "ln1_normed"))
        z_tr, x1_read, x1_hi, x1_lo, x1_done = (sem(n) for n in ("z_transposed", "x1_evacuated", "x1_hi_done", "x1_lo_done", "x1_all"))

        def sp_out(sp):
            dq.read(sp, ("uv",))

            def load_x(t):
                n = tok(t)[1]
                src = a["x_prompt"][0, t * P:(t + 1) * P, :] if t < 8 else a["x_sample"].rearrange("b s d -> (b s) d")
                sp.dma_start(zrow[0:n, t % 2, :], src).then_inc(xr_loaded[t % 2], 16)

            for k in range(KD):
                if k >= 2:
                    sp.wait_ge(wo_lo, k - 1)
                sp.dma_start(woraw[:, k % 2, :], a["w_out"][0, k * P:(k + 1) * P, :]).then_inc(wo_loaded[k % 2], 16)
                if k in (2, 3):
                    load_x(k - 2)
            for t in range(2, TT):
                sp.wait_ge(z_tr, t - 1)
                load_x(t)

        def pe_out(pe):
            for t in range(TT + 1):
                if t < TT:
                    n = tok(t)[1]
                    pe.wait_ge(mx_lo, t + 1)
                    if t >= 2:
                        pe.wait_ge(z_done, t - 1)
                    for k in range(KD):
                        if t == 0:
                            pe.wait_ge(wo_lo, k + 1)
                        for i, (m, w) in enumerate(((mxh, woh), (mxh, wol), (mxl, woh))):
                            for c in range(2):
                                mm = pe.matmul(psum[0:n, 2 * (t % 2) + c, :], m[:, t % 2, k, 0:n], w[:, k, c * 512:c * 512 + 512],
                                               start=(k == 0 and i == 0), stop=(k == KD - 1 and i == 2))
                    mm.then_inc(wo_mm, 1)
                u = t - 1
                if u >= 0:
                    n = tok(u)[1]
                    pe.wait_ge(zn_done, u + 1)
                    if u >= 2:
                        pe.wait_ge(x1_read, u - 1)
                    for k in range(KD):
                        mm = pe.transpose(x1_bank(u)[:, k, 0:n], zrow[0:n, u % 2, k * P:(k + 1) * P], ident[0:n, 0:n])
                    mm.then_inc(z_tr, 1)

        def x1_bank(t):
            return psum[:, 4 + 2 * (t % 2):6 + 2 * (t % 2), :].rearrange("p b (k c) -> p (b k) c", c=P)

        def act_out(act):
            dq.read(act, ("uv",))

            def mix_hi(t):
                c0, n = tok(t)
                if t >= 2:
                    act.wait_ge(wo_mm, t - 1)
                act.activation(mxh[:, t % 2, :, 0:n], mixT[:, :, c0:c0 + n], ACT.Copy).then_inc(mx_hi, 1)

            mix_hi(0)
            for k in range(KD):
                act.wait_ge(wo_loaded[k % 2], 16 * (k // 2 + 1))
                act.activation(woh[:, k, :], woraw[:, k % 2, :], ACT.Copy).then_inc(wo_hi, 1)
            mix_hi(1)
            for t in range(TT):
                c0, n = tok(t)
                act.wait_ge(zv_done, t + 1)
                s = lst[0:n, t % 2]
                alink(act, act.activation(s[:, 16:17], s[:, 15:16], ACT.Ln))
                act.activation(s[:, 17:18], s[:, 16:17], ACT.Exp, scale=-0.5).then_inc(zy_done, 1)
                if t + 2 < TT:
                    mix_hi(t + 2)
                act.wait_ge(z_tr, t + 1)
                if t >= 1:
                    act.wait_ge(x1_lo, t)
                for k in range(KD):
                    ins = act.activation(x1t[:, k, 0:n], x1_bank(t)[:, k, 0:n], ACT.Identity, scale=cols[:, L1G + k:L1G + k + 1],
                                         bias=cols[:, L1B + k:L1B + k + 1])
                ins.then_inc(x1_read, 1)
                act.wait_ge(x1_read, t + 1)
                act.activation(x1h[:, :, c0:c0 + n], x1t[:, :, 0:n], ACT.Copy).then_inc(x1_hi, 1)

        def dve_out(dve):
            dq.read(dve, ("uv",))

            def mix_lo(t):
                c0, n = tok(t)
                dve.wait_ge(mx_hi, t + 1)
                dve.tensor_tensor(mxl[:, t % 2, :, 0:n], mixT[:, :, c0:c0 + n], mxh[:, t % 2, :, 0:n].bitcast(F32), ALU.subtract).then_inc(mx_lo, 1)

            mix_lo(0)
            for k in range(KD):
                dve.wait_ge(wo_hi, k + 1)
                dve.tensor_tensor(wol[:, k, :], woraw[:, k % 2, :], woh[:, k, :].bitcast(F32), ALU.subtract).then_inc(wo_lo, 1)
            mix_lo(1)
            for t in range(TT + 1):
                if t < TT:
                    n = tok(t)[1]
                    z, s = zrow[0:n, t % 2, :], lst[0:n, t % 2]
                    dve.wait_ge(xr_loaded[t % 2], 16 * (t // 2 + 1))
                    dve.wait_ge(wo_mm, t + 1)
                    ins = dve.scalar_tensor_tensor(z.rearrange("p (c d) -> p c d", c=2), z.rearrange("p (c d) -> p c d", c=2), ALPHA,
                                                   psum[0:n, 2 * (t % 2):2 * (t % 2) + 2, :], ALU.mult, ALU.add)
                    ins.then_inc(z_done, 1)
                    dve.wait_ge(z_done, t + 1)
                    norm_stats(dve, z[:, 0:512], z[:, 512:1024], s)
                    dve.tensor_scalar(s[:, 15:16], s[:, 13:14], EPS, None, ALU.add).then_inc(zv_done, 1)
                    dve.wait_ge(zy_done, t + 1)
                    newton(dve, s[:, 17:18], s[:, 15:16], s[:, 18:19])
                    dve.tensor_scalar(z, z, s[:, 12:13], s[:, 17:18], ALU.subtract, ALU.mult).then_inc(zn_done, 1)
                    if t + 2 < TT:
                        mix_lo(t + 2)
                u = t - 1
                if u >= 0:
                    c0, n = tok(u)
                    dve.wait_ge(x1_hi, u + 1)
                    dve.tensor_tensor(x1l[:, :, c0:c0 + n], x1t[:, :, 0:n], x1h[:, :, c0:c0 + n].bitcast(F32), ALU.subtract).then_inc(x1_lo, 1)

        def norm_stats(dve, z0, z1, s):
            dve.bn_stats(s[:, 0:6], z0)
            dlink(dve, dve.bn_stats(s[:, 6:12], z1))
            dlink(dve, dve.bn_aggr(s[:, 12:14], s[:, 0:12]))

        GF = 4
        GROUPS = DFF // (GF * P)
        ym = sb(PERSIST, "y_sum", [P, KD, T])
        at = WO_AT
        w1h, w1l = (sb(at + i * 2048, f"w1_{n}", [P, 2, KD, P], F32R) for i, n in enumerate(("hi", "lo"))); at += 4096
        raw = sb(at, "mlp_raw", [P, 2, D]); at += 2 * D
        w2h, w2l = (sb(at + i * 4096, f"w2_{n}", [P, GF, D], F32R) for i, n in enumerate(("hi", "lo"))); at += 8192
        hh_, hl_ = (sb(at + i * GF * T, f"hid_{n}", [P, GF, T], F32R) for i, n in enumerate(("hi", "lo"))); at += 2 * GF * T
        ht = sb(at, "hid_tmp", [P, 2, T]); at += 2 * T
        assert at <= 53200
        at = WO_AT
        g2 = sb(at, "ln2_g_rows", [P, D]); b2 = sb(at + D, "ln2_b_rows", [P, D]); at += 2 * D
        yrow = sb(at, "y_rows", [P, 3, D]); at += 3 * D
        lst2 = sb(at, "ln2_stats", [P, 3, 24]); at += 72
        raw_loaded = [sem(f"mlp_raw_loaded{i}") for i in range(2)]
        mw_hi, mw_lo, set_full, h_free, y_free, h_done, h_hi, h_lo = (sem(n) for n in (
            "mlp_w_hi", "mlp_w_lo", "mlp_set_full", "hid_set_read", "out_set_read", "hid_done", "hid_hi", "hid_lo"))
        ITEMS = [("w1", 2), ("w2", 0), ("w1", 3), ("w2", 1), ("w2", 2), ("w2", 3), ("w1n", 0), ("w1n", 1)]

        def item(kind, i):
            return (w1h[:, i % 2], w1l[:, i % 2]) if kind[:2] == "w1" else (w2h[:, i], w2l[:, i])

        def raw_view(kind, s):
            return raw[:, s, :].rearrange("p (k c) -> p k c", k=KD) if kind[:2] == "w1" else raw[:, s, :]

        def sp_mlp(sp):
            w1 = a["w1"].rearrange("l (k p) f -> p (l k) f", p=P)
            sp.wait_ge(wo_mm, TT)

            def load(kind, i, g, j):
                sp.wait_ge(mw_lo, j + 1)
                if kind == "w2":
                    src = a["w2"][0, bass.ds((g * GF + i) * P, P), :]
                else:
                    gg = g + 1 if kind == "w1n" else g
                    src = w1[:, :, bass.ds((gg * GF + i) * P, P)]
                sp.dma_start(raw_view(kind, i_slot), src).then_inc(raw_loaded[i_slot], 16)

            for i_slot in range(2):
                load("w1", i_slot, 0, i_slot)
            with sp.Fori(0, GROUPS - 1) as g:
                for n, (kind, i) in enumerate(ITEMS):
                    i_slot = n % 2
                    load(kind, i, g, 8 * g + n + 2)
            for n, (kind, i) in enumerate(ITEMS[:6]):
                i_slot = n % 2
                load(kind, i, GROUPS - 1, 8 * (GROUPS - 1) + n + 2)

        def mlp_set(j):
            return psum[:, 3 * (j % 2):3 * (j % 2) + 3, 0:BLK]

        def pe_group(pe, g, last):
            for i in range(GF):
                pe.wait_ge(mw_lo, 8 * g + {0: 1, 1: 2, 2: 3, 3: 5}[i] + 2)
                if i < 2:
                    pe.wait_ge(y_free, KD * g + i + 1)
                else:
                    pe.wait_ge(h_free, GF * g + i - 1)
                for k in range(KD):
                    for n, (w, x) in enumerate(((w1h, x1h), (w1h, x1l), (w1l, x1h))):
                        for b in range(3):
                            mm = pe.matmul(psum[:, 3 * (i % 2) + b, 0:BLK], w[:, i % 2, k], x[:, k, b * BLK:(b + 1) * BLK],
                                           start=(k == 0 and n == 0), stop=(k == KD - 1 and n == 2))
                mm.then_inc(set_full, 1)
            if last:
                return
            for m in range(KD):
                if m < 2:
                    pe.wait_ge(h_free, GF * g + m + 3)
                else:
                    pe.wait_ge(y_free, KD * g + m + 1)
                for k in range(GF):
                    if m == 0:
                        pe.wait_ge(mw_lo, 8 * g + {0: 4, 1: 6, 2: 7, 3: 8}[k] + 2)
                        pe.wait_ge(h_lo, GF * g + k + 1)
                    for n, (w, x) in enumerate(((w2h, hh_), (w2h, hl_), (w2l, hh_))):
                        for b in range(3):
                            mm = pe.matmul(psum[:, 3 * (m % 2) + b, 0:BLK], w[:, k, m * P:(m + 1) * P], x[:, k, b * BLK:(b + 1) * BLK],
                                           start=(k == 0 and n == 0), stop=(k == GF - 1 and n == 2))
                mm.then_inc(set_full, 1)

        def pe_mlp(pe):
            pe.wait_ge(x1_lo, TT)
            with pe.Fori(0, GROUPS - 1) as g:
                pe_group(pe, g, False)
            pe_group(pe, GROUPS - 1, True)

        AFTER = {0: (0, 1), 1: (2, 3), 2: (4, 5), 3: (6, 7)}

        def act_group(act, g, first, last):
            for i in range(GF):
                act.wait_ge(set_full, 12 * g + i + 1)
                if i >= 2 or not first:
                    act.wait_ge(h_lo, GF * g + i - 1)
                act.activation(ht[:, i % 2, :].rearrange("p (b c) -> p b c", b=3), mlp_set(i), ACT.Relu).then_inc(h_free, 1)
                for n in AFTER[i]:
                    kind, j = ITEMS[n]
                    if last and n >= 6:
                        continue
                    act.wait_ge(raw_loaded[n % 2], 16 * (4 * g + n // 2 + 2))
                    if kind == "w2" and not first:
                        act.wait_ge(set_full, 12 * g)
                    elif kind == "w1":
                        act.wait_ge(set_full, 12 * g + j - 1)
                    elif kind == "w1n":
                        act.wait_ge(set_full, 12 * g + j + 3)
                    act.activation(item(kind, j)[0], raw_view(kind, n % 2), ACT.Copy).then_inc(mw_hi, 1)
                act.wait_ge(h_done, GF * g + i + 1)
                act.activation(hh_[:, i, :], ht[:, i % 2, :], ACT.Copy).then_inc(h_hi, 1)

        def act_mlp(act):
            act.wait_ge(wo_mm, TT)
            for i in range(2):
                act.wait_ge(raw_loaded[i], 16)
                act.activation(item("w1", i)[0], raw_view("w1", i), ACT.Copy).then_inc(mw_hi, 1)
            act_group(act, 0, True, False)
            with act.Fori(1, GROUPS - 1) as g:
                act_group(act, g, False, False)
            act_group(act, GROUPS - 1, False, True)

        def dve_group(dve, g, last):
            for i in range(GF):
                dve.wait_ge(h_free, GF * g + i + 1)
                dve.tensor_tensor(ht[:, i % 2, :], ht[:, i % 2, :], ht[:, i % 2, :], ALU.mult).then_inc(h_done, 1)
                for n in AFTER[i]:
                    if not (last and n >= 6):
                        kind, j = ITEMS[n]
                        dve.wait_ge(mw_hi, 8 * g + n + 3)
                        dve.tensor_tensor(item(kind, j)[1], raw_view(kind, n % 2), item(kind, j)[0].bitcast(F32), ALU.subtract).then_inc(mw_lo, 1)
                dve.wait_ge(h_hi, GF * g + i + 1)
                dve.tensor_tensor(hl_[:, i, :], ht[:, i % 2, :], hh_[:, i, :].bitcast(F32), ALU.subtract).then_inc(h_lo, 1)
            if last:
                return
            for m in range(KD):
                dve.wait_ge(set_full, 12 * g + GF + m + 1)
                y = ym[:, m, :].rearrange("p (b c) -> p b c", b=3)
                dve.tensor_tensor(y, y, mlp_set(m), ALU.add).then_inc(y_free, 1)
            dve.wait_ge(y_free, KD * g + KD + 2)

        def dve_mlp(dve):
            dve.sem_inc(y_free, 2)
            dve.sem_inc(mw_lo, 2)
            for i in range(2):
                dve.wait_ge(mw_hi, i + 1)
                dve.tensor_tensor(item("w1", i)[1], raw_view("w1", i), item("w1", i)[0].bitcast(F32), ALU.subtract).then_inc(mw_lo, 1)
            dve.wait_ge(x1_lo, TT)
            dlink(dve, dve.tensor_tensor(ym[:], x1h[:].bitcast(F32), x1l[:].bitcast(F32), ALU.add))
            dlink(dve, dve.tensor_scalar(ym[:], ym[:], ALPHA, None, ALU.mult))
            with dve.Fori(0, GROUPS - 1) as g:
                dve_group(dve, g, False)
            dve_group(dve, GROUPS - 1, True)

        G1 = GROUPS - 1
        L_TASKS, LN_AFTER = [], {0: [0, 1], 1: [2, 3, 4], 2: [5, 6, 7, 8]}
        for b in range(3):
            L_TASKS += [(b, m) for m in range(KD)]
        lb = Banks("last_out_bank", [0, 1, 2, 3], L_TASKS, after=dq)
        yt_full, yn_done, yrow_done, ln2_loaded = sem("y_transposed"), sem("y_bank_read"), sem("y_rows_done"), sem("ln2_rows_loaded")
        yv_done, yy_done, yg_done = sem("ln2_var"), sem("ln2_lnexp"), sem("ln2_scaled")
        y_stored = [sem(f"y_stored{i}") for i in range(3)]

        def y_bank(t):
            return psum[:, 4 + 2 * (t % 2):6 + 2 * (t % 2), :]

        def pe_last(pe):
            pe.wait_ge(h_free, GF * G1 + GF)
            first = True

            def turn(t):
                c0, n = tok(t)
                if t >= 2:
                    pe.wait_ge(yn_done, t - 1)
                for k in range(KD):
                    mm = pe.transpose(y_bank(t)[0:n, k // 4, (k % 4) * P:(k % 4 + 1) * P], ym[:, k, c0:c0 + n], ident)
                mm.then_inc(yt_full, 1)

            for b in range(3):
                for m in range(KD):
                    key = (b, m)
                    lb.begin(pe, key)
                    for k in range(GF):
                        if first and m == 0:
                            pe.wait_ge(mw_lo, 8 * G1 + {0: 4, 1: 6, 2: 7, 3: 8}[k] + 2)
                            pe.wait_ge(h_lo, GF * G1 + k + 1)
                        for n, (w, x) in enumerate(((w2h, hh_), (w2h, hl_), (w2l, hh_))):
                            mm = pe.matmul(lb.of(key)[:, 0:BLK], w[:, k, m * P:(m + 1) * P], x[:, k, b * BLK:(b + 1) * BLK],
                                           start=(k == 0 and n == 0), stop=(k == GF - 1 and n == 2))
                    first = False
                    lb.full(mm)
                    if b and m in (1, 3, 5) and (m - 1) // 2 < len(LN_AFTER[b - 1]):
                        if m == 1:
                            for q in range(4):
                                lb.read(pe, (b - 1, KD - 4 + q))
                        turn(LN_AFTER[b - 1][(m - 1) // 2])
            for q in range(4):
                lb.read(pe, (2, KD - 4 + q))
            for t in LN_AFTER[2]:
                turn(t)

        def dve_last(dve):
            dve.wait_ge(ln2_loaded, 32)

            def rows(t):
                n = tok(t)[1]
                z, s = yrow[0:n, t % 3, :], lst2[0:n, t % 3]
                dve.wait_ge(yt_full, t + 1)
                if t >= 3:
                    dve.wait_ge(y_stored[t % 3], 16 * (t // 3))
                norm_stats(dve, y_bank(t)[0:n, 0, :], y_bank(t)[0:n, 1, :], s)
                dve.tensor_scalar(s[:, 15:16], s[:, 13:14], EPS, None, ALU.add).then_inc(yv_done, 1)
                dve.wait_ge(yy_done, t + 1)
                newton(dve, s[:, 17:18], s[:, 15:16], s[:, 18:19])
                dve.scalar_tensor_tensor(s[:, 19:20], s[:, 12:13], -1.0, s[:, 17:18], ALU.mult, ALU.mult).then_inc(yg_done, 1)
                dve.wait_ge(yn_done, t + 1)
                dlink(dve, dve.tensor_tensor(z, z, g2[0:n, :], ALU.mult))
                dve.tensor_tensor(z, z, b2[0:n, :], ALU.add).then_inc(yrow_done, 1)

            for b in range(3):
                for m in range(KD):
                    key = (b, m)
                    lb.wait(dve, key)
                    c = slice(b * BLK, (b + 1) * BLK)
                    lb.free(dve.tensor_tensor(ym[:, m, c], ym[:, m, c], lb.of(key)[:, 0:BLK], ALU.add), key)
                    if b and m in (2, 4, 6) and (m - 2) // 2 < len(LN_AFTER[b - 1]):
                        rows(LN_AFTER[b - 1][(m - 2) // 2])
            for t in LN_AFTER[2]:
                rows(t)

        def act_last(act):
            for t in range(TT):
                n = tok(t)[1]
                s = lst2[0:n, t % 3]
                act.wait_ge(yv_done, t + 1)
                alink(act, act.activation(s[:, 16:17], s[:, 15:16], ACT.Ln))
                act.activation(s[:, 17:18], s[:, 16:17], ACT.Exp, scale=-0.5).then_inc(yy_done, 1)
                act.wait_ge(yg_done, t + 1)
                act.activation(yrow[0:n, t % 3, :].rearrange("p (c d) -> p c d", c=2), y_bank(t)[0:n], ACT.Identity,
                               scale=s[:, 17:18], bias=s[:, 19:20]).then_inc(yn_done, 1)

        def sp_last(sp):
            sp.wait_ge(set_full, 12 * G1 + GF)
            sp.wait_ge(mw_lo, 8 * G1 + 10)
            sp.dma_start(g2[:], a["ln2_g"].broadcast_to([P, D])).then_inc(ln2_loaded, 16)
            sp.dma_start(b2[:], a["ln2_b"].broadcast_to([P, D])).then_inc(ln2_loaded, 16)
            for t in range(TT):
                n = tok(t)[1]
                dst = out["y_prompt"][0, t * P:(t + 1) * P, :] if t < 8 else out["y_sample"].rearrange("b s d -> (b s) d")
                sp.wait_ge(yrow_done, t + 1)
                sp.dma_start(dst, yrow[0:n, t % 3, :]).then_inc(y_stored[t % 3], 16)
            for i in range(3):
                sp.wait_ge(y_stored[i], 48)
            sp.wait_ge(gst_stored, 48)
            sp.wait_ge(rows_stored, 64)

        SP = [sp_project, sp_gla, sp_mla_in, sp_mla, sp_decode, sp_out, sp_mlp, sp_last]
        PE = [pe_project, pe_gla, pe_mla_in, pe_mla, pe_decode, pe_out, pe_mlp, pe_last]
        AC = [act_project, act_gla, act_mla_in, act_mla, act_decode, act_out, act_mlp, act_last]
        DV_ = [dve_gla_early, dve_project, dve_gla, dve_mla_in, dve_mla, dve_decode, dve_out, dve_mlp, dve_last]

        block = ctx.enter_context(nc.Block())

        @block.sync
        def _(sp):
            for stage in SP:
                stage(sp)

        @block.tensor
        def _(pe):
            for stage in PE:
                stage(pe)

        @block.scalar
        def _(act):
            for stage in AC:
                stage(act)

        @block.vector
        def _(dve):
            for stage in DV_:
                stage(dve)

        @block.gpsimd
        def _(pool):
            pool_decode(pool)


def _tables():
    import numpy as np

    c = np.zeros((P, CONST_W), np.float32)

    def put(name, v):
        at, w = CONST_COLS[name]
        c[:, at:at + w] = v

    i, j = np.arange(P)[:, None], np.arange(P)[None, :]
    put("ident", i == j)
    put("swap", (i ^ (ROPE // 2)) == j)
    same = i // CH == j // CH
    put("tri16", (same & (i <= j)) / 16.0)
    put("chunkmask", same & (i <= j))
    put("causal", np.where(j <= i, 0.0, NEG))
    put("spread", np.concatenate([(i // 32 == q) & (i % 32 == j % 32) for q in range(4)], 1))
    put("ones", 1.0)
    put("dup", (i < ROPE) & (j % ROPE == i))
    put("swapdup", (i < ROPE) & ((j % ROPE) ^ (ROPE // 2) == i))
    h = np.arange(4)[None, :]
    put("sumkq", i % 32 == h)
    put("diagh", i == h)
    inv = 10000.0 ** (-np.arange(0, ROPE, 2, dtype=np.float64) / ROPE)
    pos = np.concatenate([np.arange(TP), np.full(NB, PAST)]).astype(np.float32)
    ang = (pos[None, :] * inv.astype(np.float32)[:, None]).astype(np.float64)
    cos, sin = np.cos(ang).astype(np.float32), np.sin(ang).astype(np.float32)
    rope = np.stack([np.concatenate([cos] * 4), np.concatenate([-sin, sin] * 2)], 1)
    return c, rope.reshape(P, 2 * T)


_OUTS = dict(
    y_prompt=(1, TP, D), y_sample=(NB, 1, D), ckv_prompt=(1, 1, TP, KVR), krope_prompt=(1, 1, TP, ROPE),
    gla_prompt=(1, 1, HEADS, DK, DV), ckv_sample=(1, NB, 1, KVR), krope_sample=(1, NB, 1, ROPE),
    gla_sample=(1, NB, HEADS, DK, DV))


def kernel(x_prompt, x_sample, cache_ckv, cache_krope, state_gla, page_table, w_in, mla_q_norm, mla_w_uq,
           mla_kv_norm, mla_w_uk, mla_w_uv, gla_w_gate2, gla_b_gate, gla_norm, w_out, ln1_g, ln1_b,
           mlp_w1, mlp_w2, ln2_g, ln2_b):
    import numpy as np
    import concourse.bacc as bacc
    from concourse.bass_utils import run_bass_kernel_spmd

    def columns(v):
        return np.ascontiguousarray(np.asarray(v).reshape(-1, P).T)

    consts, rope = _tables()
    cols = np.zeros((P, 24), np.float32)
    for at, v in ((0, mla_q_norm), (3, mla_kv_norm), (5, gla_norm), (6, ln1_g), (14, ln1_b)):
        c = columns(v)
        cols[:, at:at + c.shape[1]] = c
    arrays = dict(
        x_prompt=x_prompt, x_sample=x_sample, cache_ckv=cache_ckv, cache_krope=cache_krope, state_gla=state_gla,
        page_table=page_table, w_in=w_in, w_uq=mla_w_uq, w_uk=mla_w_uk, w_uv=mla_w_uv, w_gate2=gla_w_gate2,
        b_gate=gla_b_gate, w_out=w_out, w1=mlp_w1, w2=mlp_w2, ln2_g=ln2_g, ln2_b=ln2_b,
        consts=consts, rope=rope, cols=cols)
    arrays = {k: np.ascontiguousarray(v) for k, v in arrays.items()}
    nc = bacc.Bacc("TRN2", target_bir_lowering=False, num_devices=1)
    a = {k: nc.dram_tensor("in_" + k, v.shape, mybir.dt.from_np(v.dtype), kind="ExternalInput").ap()
         for k, v in arrays.items()}
    out = {k: nc.dram_tensor("out_" + k, s, F32, kind="ExternalOutput").ap() for k, s in _OUTS.items()}
    scratch = nc.dram_tensor("scratch", (NT, P, T), F32, kind="Internal").ap()
    hymba_step(nc, a, out, scratch)
    r = run_bass_kernel_spmd(nc, [{"in_" + k: v for k, v in arrays.items()}], core_ids=[0])
    return tuple(r.results[0]["out_" + k] for k in _OUTS)
```

```python
from contextlib import ExitStack

import concourse.bass as bass
from concourse import mybir

ALU = mybir.AluOpType
ACT = mybir.ActivationFunctionType
AX = mybir.AxisListType
F32 = mybir.dt.float32
F32R = mybir.dt.float32r
U32 = mybir.dt.uint32
I32 = mybir.dt.int32

P = 128
D = 1024
TP, NB = 1024, 8
T = TP + NB
BLK = T // 3
KD = D // P
TT = TP // P + 1
QR, KVR, ROPE, NOPE = 384, 256, 64, 128
HEADS, DK, DV, GR = 4, 64, 128, 16
CH = 64
NCH = TP // CH
PAST, PAGE = 2048, 128
PAGES = PAST // PAGE
N_PHYS = NB * PAGES + NB * PAGES // 4
DFF = 4096
ALPHA = 2.0 ** 0.25
EPS = 1e-5
SCALE = (NOPE + ROPE) ** -0.5
NEG = -1.0e30

OFF = dict(cq=0, ckv=384, kr=640, gq=704, gk=960, gv=1216, gr=1728, gg=1744)
TILES = [("krgr", None)]
TILES += [("gq", OFF["gq"] + P * i) for i in range(2)] + [("gk", OFF["gk"] + P * i) for i in range(2)]
TILES += [("gv", OFF["gv"] + P * i) for i in range(4)] + [("gg", OFF["gg"] + P * i) for i in range(4)]
TILES += [("ckv", OFF["ckv"] + P * i) for i in range(2)] + [("cq", OFF["cq"] + P * i) for i in range(3)]
NT = len(TILES)
ROW_GQ, ROW_GK, ROW_GV, ROW_GG, ROW_CKV, ROW_CQ = 1, 3, 5, 9, 13, 15

CONST_COLS = {}
_at = 0
for _n, _w in (("ident", P), ("swap", P), ("tri16", P), ("chunkmask", P), ("causal", P), ("spread", 4 * P),
               ("ones", P), ("dup", P), ("swapdup", P), ("sumkq", 4), ("diagh", 4)):
    CONST_COLS[_n] = (_at, _w)
    _at += _w
CONST_W = _at


def tok(t):
    return (t * P, P) if t < TP // P else (TP, NB)


def hymba_step(nc, a, out, scratch):
    with ExitStack() as ctx:
        def sem(name):
            return ctx.enter_context(nc.semaphore(name))

        def sb(at, name, shape, dt=F32):
            assert at % 8 == 0, name
            with nc.sbuf_tensor(name + "_below", [P, at], F32):
                with nc.sbuf_tensor(name, shape, dt) as t:
                    return t

        psum = ctx.enter_context(nc.psum_tensor("psum", [P, 8, 512], F32))

        consts = sb(8, "consts", [P, CONST_W])
        cols = sb(8 + CONST_W, "cols", [P, 24])
        smp = sb(8 + CONST_W + 24, "decode_cols", [P, 72])
        pt = sb(8 + CONST_W + 96, "page_table", [1, NB * PAGES], I32)
        PERSIST = 8 + CONST_W + 96 + NB * PAGES
        mixT = sb(PERSIST, "mixT", [P, KD, T])
        AREA = PERSIST + KD * T

        def const(name, rows=P):
            c, w = CONST_COLS[name]
            return consts[0:rows, c:c + w]

        ident = const("ident")
        QN, KVN, GN, L1G, L1B = 0, 3, 5, 6, 14

        s_const = sem("const_loaded")

        at = AREA
        xTh = sb(at, "xTh", [P, KD, T], F32R); at += KD * T
        xTl = sb(at, "xTl", [P, KD, T], F32R); at += KD * T
        xnat = sb(at, "xnat", [P, 2, D]); at += 2 * D
        w1raw = sb(at, "win_raw", [P, 3, KD, P]); at += 3 * D
        winh = sb(at, "win_hi", [P, 2, KD, P], F32R); at += 2 * D
        winl = sb(at, "win_lo", [P, 2, KD, P], F32R); at += 2 * D
        pstage = sb(at, "proj_stage", [P, 3, T]); at += 3 * T
        GLA_IN = at + 8

        x_loaded = [sem(f"x_loaded{i}") for i in range(2)]
        xt_done, xh_done, xl_done = sem("xt_transposed"), sem("xT_hi"), sem("xT_lo")
        win_loaded = [sem(f"win_loaded{i}") for i in range(3)]
        winh_done, winl_done = sem("win_hi_done"), sem("win_lo_done")
        proj_mm, proj_out = sem("proj_multiplied"), sem("proj_evacuated")
        proj_stored = [sem(f"proj_stored{i}") for i in range(3)]

        def stored(eng, m):
            eng.wait_ge(proj_stored[m % 3], 16 * (m // 3 + 1))

        GATE_FROM = 4

        def sp_project(sp):
            sp.dma_start(consts[:], a["consts"]).then_inc(s_const, 16)
            sp.dma_start(cols[:], a["cols"]).then_inc(s_const, 16)

            def load_w(m):
                if m >= 3:
                    sp.wait_ge(winl_done, m - 2)
                kind, c0 = TILES[m]
                w = a["w_in"].rearrange("l (k p) n -> p (l k) n", p=P)
                if kind == "krgr":
                    sp.dma_start(w1raw[:, m % 3, :, 0:ROPE], w[:, :, OFF["kr"]:OFF["kr"] + ROPE]).then_inc(win_loaded[m % 3], 16)
                    sp.dma_start(w1raw[:, m % 3, :, ROPE:ROPE + GR], w[:, :, OFF["gr"]:OFF["gr"] + GR]).then_inc(win_loaded[m % 3], 16)
                else:
                    sp.dma_start(w1raw[:, m % 3, :, :], w[:, :, c0:c0 + P]).then_inc(win_loaded[m % 3], 16)

            for t in range(TT):
                if t >= 2:
                    sp.wait_ge(xt_done, t - 1)
                n = tok(t)[1]
                src = a["x_prompt"][0, t * P:(t + 1) * P, :] if t < 8 else a["x_sample"].rearrange("b s d -> (b s) d")
                sp.dma_start(xnat[0:n, t % 2, :], src).then_inc(x_loaded[t % 2], 16)
                if 1 <= t <= 3:
                    load_w(t - 1)
            for m in range(3, NT + 3):
                if m < NT:
                    load_w(m)
                j = m - 3
                rows = ROPE + GR if j == 0 else P
                sp.wait_ge(proj_out, j + 1)
                sp.dma_start(scratch[j, 0:rows, :], pstage[0:rows, j % 3, :]).then_inc(proj_stored[j % 3], 16)
                if j >= 1:
                    sp_gla_in(sp, j - 1)

        def xt_bank(t, n):
            return psum[:, 2 * (t % 3):2 * (t % 3) + 2, :].rearrange("p b (k c) -> p (b k) c", c=P)[:, :, 0:n]

        def pe_project(pe):
            pe.wait_ge(s_const, 32)
            for t in range(TT):
                n = tok(t)[1]
                pe.wait_ge(x_loaded[t % 2], 16 * (t // 2 + 1))
                if t >= 3:
                    pe.wait_ge(xl_done, t - 2)
                for k in range(KD):
                    mm = pe.transpose(xt_bank(t, n)[:, k, :], xnat[0:n, t % 2, k * P:(k + 1) * P], ident[0:n, 0:n])
                mm.then_inc(xt_done, 1)
            pe.wait_ge(xl_done, TT)
            for m in range(NT):
                if 0 <= m - GATE_FROM < TT:
                    pe_gate(pe, m - GATE_FROM)
                M = ROPE + GR if m == 0 else P
                pe.wait_ge(winl_done, m + 1)
                if m >= 2:
                    pe.wait_ge(proj_out, m - 1)
                for b in range(3):
                    for k in range(KD):
                        for i, (w, x) in enumerate(((winh, xTh), (winh, xTl), (winl, xTh))):
                            mm = pe.matmul(psum[0:M, 3 * (m % 2) + b, 0:BLK], w[:, m % 2, k, 0:M],
                                           x[:, k, b * BLK:(b + 1) * BLK], start=(k == 0 and i == 0),
                                           stop=(k == KD - 1 and i == 2))
                mm.then_inc(proj_mm, 1)

        def act_project(act):
            for t in range(TT):
                c0, n = tok(t)
                act.wait_ge(xt_done, t + 1)
                act.activation(xTh[:, :, c0:c0 + n], xt_bank(t, n), ACT.Copy).then_inc(xh_done, 1)
                if t in (2, 3):
                    split_hi(act, t - 2)
            for m in range(NT):
                if 2 <= m + 1 < NT:
                    split_hi(act, m + 1)
                if m == GATE_FROM + TT + 1:
                    act_gate(act)
                M = ROPE + GR if m == 0 else P
                act.wait_ge(proj_mm, m + 1)
                if m >= 3:
                    act.wait_ge(proj_stored[m % 3], 16 * (m // 3))
                act.activation(pstage[0:M, m % 3, :].rearrange("p (b c) -> p b c", b=3),
                               psum[0:M, 3 * (m % 2):3 * (m % 2) + 3, 0:BLK], ACT.Copy).then_inc(proj_out, 1)

        def split_hi(act, m):
            M = ROPE + GR if m == 0 else P
            act.wait_ge(win_loaded[m % 3], 16 * (m // 3 + 1) + (16 if m % 3 == 0 else 0))
            if m >= 2:
                act.wait_ge(proj_mm, m - 1)
            act.activation(winh[:, m % 2, :, 0:M], w1raw[:, m % 3, :, 0:M], ACT.Copy).then_inc(winh_done, 1)

        def dve_project(dve):
            def split_lo(m):
                M = ROPE + GR if m == 0 else P
                dve.wait_ge(winh_done, m + 1)
                dve.tensor_tensor(winl[:, m % 2, :, 0:M], w1raw[:, m % 3, :, 0:M], winh[:, m % 2, :, 0:M].bitcast(F32),
                                  ALU.subtract).then_inc(winl_done, 1)

            for t in range(TT):
                c0, n = tok(t)
                dve.wait_ge(xh_done, t + 1)
                dve.tensor_tensor(xTl[:, :, c0:c0 + n], xt_bank(t, n), xTh[:, :, c0:c0 + n].bitcast(F32),
                                  ALU.subtract).then_inc(xl_done, 1)
                if t in (2, 3):
                    split_lo(t - 2)
            for m in range(2, NT):
                split_lo(m)
                if m == GATE_FROM + TT + 2:
                    dve_gate(dve, TT)
                if 0 <= m - GATE_FROM - 1 < TT:
                    dve_gate(dve, m - GATE_FROM - 1)

        G_TASKS = [(("z", t), 1) for t in range(TT)]
        G_TASKS += [(("cum", f, h), 1) for f in range(2) for h in range(2)] + [(("cums",), 1)]
        G_TASKS += [(("v", t), 1) for t in range(TT)]
        G_TASKS += [(("kh", i), 1) for i in range(4)] + [(("vb", b), 1) for b in range(NB)]
        G_TASKS += [(("kv", n), 1) for n in range(NCH)] + [(("A", 0), 1)]
        for t in range(TT):
            G_TASKS += [(("A", t + 1), 1)] * (t + 1 < 8) + [(("O", t), 1)]
        G_TASKS += [(("oT", t), 1) for t in range(TT)]
        G_AT = {key: i for i, (key, _) in enumerate(G_TASKS)}
        g_full = sem("gla_bank_full")
        g_free = [sem(f"gla_bank_free{i}") for i in range(2)]

        def g_bank(key):
            return psum[:, 6 + G_AT[key] % 2, :]

        def g_begin(pe, key):
            i = G_AT[key]
            reads = sum(r for j, (_, r) in enumerate(G_TASKS[:i]) if j % 2 == i % 2)
            if reads:
                pe.wait_ge(g_free[i % 2], reads)

        def g_wait(eng, key):
            eng.wait_ge(g_full, G_AT[key] + 1)

        def g_read(eng, *keys):
            for key in keys:
                i = G_AT[key]
                eng.wait_ge(g_free[i % 2], sum(r for j, (_, r) in enumerate(G_TASKS[:i + 1]) if j % 2 == i % 2))

        def g_done(ins, key):
            ins.then_inc(g_free[G_AT[key] % 2], 1)

        at = GLA_IN
        gqk = sb(at, "gqk", [P, 4, T]); at += 4 * T
        gvT = sb(at, "gvT", [P, 4, T])
        state = sb(at, "state", [P, NB, 2, DV])
        vk = sb(at + NB * 2 * DV, "vk", [P, NB, 2, DV]); at += 4 * T
        grT = sb(at, "grT", [32, T]); at += T
        w2g = sb(at, "w_gate2", [32, 256]); at += 256
        ggT = sb(at, "ggT", [P, 4, T])
        loga = sb(at, "loga", [P, TT, 256]); zabs = sb(at + TT * 256, "zabs", [P, TT, 256]); at += 2 * TT * 256
        assert at <= 53200
        at = AREA
        gout = sb(at, "gla_out", [P, TT, 512]); at += TT * 512
        blast = sb(at, "b_last", [P, 2, NCH]); at += 2 * NCH
        gss = sb(at, "gla_sumsq", [P, 4 * TT]); at += 40
        grs = sb(at, "gla_rstd", [P, 4 * TT]); at += 40
        gtmp = sb(at, "gla_tmp", [P, 4 * TT]); at += 40
        qz = sb(at, "q_diag", [P, 2, 2, NB, NB]); at += 4 * NB * NB
        gjunk = sb(at, "square_out", [P, P]); at += P
        gv = sb(at, "gv", [P, TT, 512]); at += TT * 512
        eb = sb(at, "exp_b", [P, 2, T]); at += 2 * T
        kt = sb(at, "k_tilde", [P, 2, TP]); at += 2 * TP
        khT = sb(at, "k_hat_T", [P, 2, TP]); at += 2 * TP
        kh = sb(at, "k_hat", [P, 8, 256]); at += 8 * 256
        hist = sb(at, "state_hist", [P, NCH + 1, 2, DV]); at += (NCH + 1) * 2 * DV
        qt = sb(at, "q_tilde", [P, 2, 2, TP]); at += 4 * T
        am = sb(at, "a_masked", [P, 2, 4, P]); at += 8 * P
        assert at <= GLA_IN

        gr_ones, gin_loaded, gst_loaded = sem("gate_ones"), [sem(f"gla_in{i}") for i in range(4)], sem("state_loaded")
        abs_done, ln_done, lg_done, silu_e = sem("abs_done"), sem("ln_done"), sem("loga_done"), sem("silu_exp")
        exb_done, sub_done, qk_done, seen_done = sem("exp_b_done"), sem("b_differences"), sem("gla_qk"), sem("exp_hat")
        gss_set, gss_done = sem("sumsq_preset"), sem("sumsq_done")
        st_done, grv_done, gry_done = sem("state_new"), sem("gla_var"), sem("gla_lnexp")
        gon_done, silu_done, gst_stored = sem("gla_normed"), sem("silu_done"), sem("gla_stored")
        dve_step, act_step = sem("dve_step"), sem("act_step")
        steps = {"dve": 0, "act": 0}

        def dlink(dve, ins):
            steps["dve"] += 1
            ins.then_inc(dve_step, 1)
            dve.wait_ge(dve_step, steps["dve"])

        def alink(act, ins):
            steps["act"] += 1
            ins.then_inc(act_step, 1)
            act.wait_ge(act_step, steps["act"])

        def sp_gla_in(sp, j):
            if j == 0:
                stored(sp, 0)
                sp.wait_ge(gr_ones, 1)
                sp.dma_start(grT[0:GR, :], scratch[0, ROPE:ROPE + GR, :]).then_inc(gin_loaded[0], 16)
                sp.dma_start(w2g[0:GR, :], a["w_gate2"][0]).then_inc(gin_loaded[0], 16)
                sp.dma_start(w2g[GR:GR + 1, :], a["b_gate"]).then_inc(gin_loaded[0], 16)
            elif j == ROW_GK + 1:
                stored(sp, j), stored(sp, j - 1), stored(sp, j - 2)
                sp.dma_start(gqk[:], scratch[ROW_GQ:ROW_GQ + 4].rearrange("m p t -> p m t")).then_inc(gin_loaded[1], 16)
            elif j == ROW_GV + 3:
                stored(sp, j), stored(sp, j - 1), stored(sp, j - 2)
                sp.dma_start(gvT[:], scratch[ROW_GV:ROW_GV + 4].rearrange("m p t -> p m t")).then_inc(gin_loaded[2], 16)

        def sp_gla(sp):
            g_wait(sp, ("cums",))
            sp.dma_start(ggT[:], scratch[ROW_GG:ROW_GG + 4].rearrange("m p t -> p m t")).then_inc(gin_loaded[3], 16)
            g_wait(sp, ("v", TT - 1))
            for f in range(2):
                sp.dma_start(state[:, :, f, :], a["state_gla"][0].rearrange("b (f h) d v -> f (h d) b v", f=2)[f]).then_inc(gst_loaded, 16)
            g_read(sp, ("vb", NB - 1), ("vb", NB - 2))
            sp_mla_early(sp)
            g_read(sp, ("kv", NCH - 1))
            sp.dma_start(out["gla_prompt"][0, 0].rearrange("(f h) d v -> (h d) f v", f=2), hist[:, NCH, :, :]).then_inc(gst_stored, 16)
            sp.wait_ge(st_done, 1)
            for f in range(2):
                sp.dma_start(out["gla_sample"][0].rearrange("b (f h) d v -> f (h d) b v", f=2)[f], state[:, :, f, :]).then_inc(gst_stored, 16)

        def half(hh):
            return slice(DK * hh, DK * hh + DK)

        def pe_gate(pe, t):
            c0, n = tok(t)
            key = ("z", t)
            if t == 0:
                pe.wait_ge(gin_loaded[0], 48)
            g_begin(pe, key)
            pe.matmul(g_bank(key)[0:n, 0:256], grT[0:GR + 1, c0:c0 + n], w2g[0:GR + 1, :], start=True, stop=True).then_inc(g_full, 1)

        NORM_A = 5

        def pe_gla(pe):
            pe.wait_ge(lg_done, 2)
            for f in range(2):
                for h in range(2):
                    key = ("cum", f, h)
                    g_begin(pe, key)
                    for i in range(4):
                        t = 4 * h + i
                        mm = pe.matmul(g_bank(key)[:, i * P:(i + 1) * P], loga[:, t, f * P:(f + 1) * P], const("tri16"),
                                       start=True, stop=True)
                    mm.then_inc(g_full, 1)
            key = ("cums",)
            g_begin(pe, key)
            for f in range(2):
                mm = pe.matmul(g_bank(key)[:, f * NB:(f + 1) * NB], loga[0:NB, TT - 1, f * P:(f + 1) * P], ident[0:NB, 0:NB],
                               start=True, stop=True)
            mm.then_inc(g_full, 1)
            for t in range(TT):
                c0, n = tok(t)
                key = ("v", t)
                if t == 0:
                    pe.wait_ge(gin_loaded[2], 16)
                g_begin(pe, key)
                for h in range(HEADS):
                    mm = pe.transpose(g_bank(key)[0:n, h * P:(h + 1) * P], gvT[:, h, c0:c0 + n], ident)
                mm.then_inc(g_full, 1)
            for i in range(4):
                key = ("kh", i)
                if i == 0:
                    pe.wait_ge(qk_done, 2)
                g_begin(pe, key)
                for j in range(2):
                    for f in range(2):
                        t = 2 * i + j
                        mm = pe.transpose(g_bank(key)[:, (2 * j + f) * P:(2 * j + f + 1) * P], khT[:, f, t * P:(t + 1) * P], ident)
                mm.then_inc(g_full, 1)
            g_read(pe, ("v", TT - 1), ("v", TT - 2))
            for b in range(NB):
                key = ("vb", b)
                g_begin(pe, key)
                pe.matmul(g_bank(key), ident[0:NB, b:b + 1].broadcast_to([NB, P]), gv[0:NB, TT - 1, :], start=True, stop=True).then_inc(g_full, 1)
            for n in range(NCH):
                key = ("kv", n)
                if n % 4 == 0:
                    g_read(pe, ("kh", n // 4))
                g_begin(pe, key)
                r = slice(CH * (n % 2), CH * (n % 2) + CH)
                for f in range(2):
                    mm = pe.matmul(g_bank(key)[:, f * 256:(f + 1) * 256], kh[r, n // 2, f * P:(f + 1) * P],
                                   gv[r, n // 2, f * 256:(f + 1) * 256], start=True, stop=True)
                mm.then_inc(g_full, 1)

            def inner(t):
                key = ("A", t)
                g_begin(pe, key)
                for h in range(HEADS):
                    f = h // 2
                    mm = pe.matmul(g_bank(key)[:, h * P:(h + 1) * P], kt[:, f, t * P:(t + 1) * P], qt[:, f, h % 2, t * P:(t + 1) * P],
                                   start=True, stop=True)
                mm.then_inc(g_full, 1)

            pe.wait_ge(qk_done, 6)
            inner(0)
            pe_mla_early(pe)
            g_read(pe, ("kv", NCH - 2), ("kv", NCH - 1))
            for t in range(TT):
                if t + 1 < 8:
                    inner(t + 1)
                key = ("O", t)
                if t < 8:
                    g_read(pe, ("A", t))
                else:
                    pe.wait_ge(st_done, 2)
                g_begin(pe, key)
                o = g_bank(key)
                for h in range(HEADS):
                    f = h // 2
                    if t < 8:
                        pe.matmul(o[:, h * P:(h + 1) * P], am[:, t % 2, h, :], gv[:, t, h * P:(h + 1) * P], start=True, stop=True,
                                  skip_group_check=True)
                        for c in range(2):
                            q0 = t * P + CH * c
                            mm = pe.matmul(o[CH * c:CH * c + CH, h * P:(h + 1) * P], qt[:, f, h % 2, q0:q0 + CH], hist[:, 2 * t + c, f, :],
                                           start=False, stop=True, skip_group_check=True)
                    else:
                        for b in range(NB):
                            mm = pe.matmul(o[0:NB, h * P:(h + 1) * P], qz[:, f, h % 2, b, :], state[:, b, f, :], start=(b == 0), stop=(b == NB - 1))
                mm.then_inc(g_full, 1)
            for t in range(TT):
                pe.wait_ge(gon_done, 1 if t < NORM_A else 2)
                c0, n = tok(t)
                key = ("oT", t)
                g_begin(pe, key)
                for h in range(HEADS):
                    mm = pe.transpose(g_bank(key)[:, h * P:h * P + n], gout[0:n, t, h * P:(h + 1) * P], ident[0:n, 0:n])
                mm.then_inc(g_full, 1)

        def act_gate(act):
            g_read(act, ("z", TT - 1), ("z", TT - 2))
            for n, ts in ((P, slice(0, 8)), (NB, slice(8, 9))):
                alink(act, act.activation(zabs[0:n, ts, :], loga[0:n, ts, :], ACT.Abs))
                alink(act, act.activation(zabs[0:n, ts, :], zabs[0:n, ts, :], ACT.Exp, scale=-1.0))
                act.activation(zabs[0:n, ts, :], zabs[0:n, ts, :], ACT.Ln, bias=1.0).then_inc(ln_done, 1)

        def act_gla(act):
            for f in range(2):
                for h in range(2):
                    key = ("cum", f, h)
                    g_wait(act, key)
                    c = slice(512 * h, 512 * h + 512)
                    act.activation(eb[:, f, c], g_bank(key), ACT.Exp)
                    act.activation(kt[:, f, c], g_bank(key), ACT.Exp, scale=-1.0).then_inc(exb_done, 1)
            key = ("cums",)
            g_wait(act, key)
            g_done(act.activation(eb[:, :, TP:T], g_bank(key)[:, 0:2 * NB].rearrange("p (f b) -> p f b", f=2), ACT.Exp,
                                  scale=1.0 / 16.0), key)
            for t in range(TT):
                n = tok(t)[1]
                g_wait(act, ("v", t))
                ins = act.activation(gv[0:n, t, :], g_bank(("v", t))[0:n, :], ACT.Copy)
                g_done(ins, ("v", t))
            for f in range(2):
                act.wait_ge(sub_done, 2 * f + 2)
                act.activation(khT[:, f, :], khT[:, f, :], ACT.Exp).then_inc(seen_done, 1)
            for i in range(4):
                key = ("kh", i)
                g_wait(act, key)
                g_done(act.activation(kh[:, 2 * i:2 * i + 2, :], g_bank(key).rearrange("p (t c) -> p t c", t=2), ACT.Copy), key)
            act.wait_ge(gin_loaded[3], 16)
            act.activation(ggT[:], ggT[:], ACT.Silu).then_inc(silu_e, 1)
            act.wait_ge(gss_set, 1)
            for t in range(TT):
                n = tok(t)[1]
                key = ("O", t)
                g_read(act, key)
                for h in range(HEADS):
                    alink(act, act.activation(gjunk[0:n, :], gout[0:n, t, h * P:(h + 1) * P], ACT.Square,
                                              accum_out=gss[0:n, 4 * t + h:4 * t + h + 1]))
                if t in (NORM_A - 1, TT - 1):
                    act.sem_inc(gss_done, 1)
                    i = 0 if t < NORM_A else 1
                    act.wait_ge(grv_done, i + 1)
                    c = slice(0, 4 * NORM_A) if i == 0 else slice(4 * NORM_A, 4 * TT)
                    alink(act, act.activation(grs[:, c], gtmp[:, c], ACT.Ln))
                    act.activation(grs[:, c], grs[:, c], ACT.Exp, scale=-0.5).then_inc(gry_done, 1)

        def dve_gla_early(dve):
            dve.memset(grT[:], 1.0).then_inc(gr_ones, 1)

        def dve_gate(dve, t):
            if t < TT:
                n = tok(t)[1]
                key = ("z", t)
                g_wait(dve, key)
                g_done(dve.tensor_copy(loga[0:n, t, :], g_bank(key)[0:n, 0:256]), key)
                return
            g_read(dve, ("z", TT - 1), ("z", TT - 2))
            for i, (n, ts) in enumerate(((P, slice(0, 8)), (NB, slice(8, 9)))):
                dve.wait_ge(ln_done, i + 1)
                dve.scalar_tensor_tensor(loga[0:n, ts, :], loga[0:n, ts, :], 0.0, zabs[0:n, ts, :], ALU.min, ALU.subtract).then_inc(lg_done, 1)

        def dve_gla(dve):
            dve.wait_ge(proj_mm, NT)
            for f in range(2):
                for h in range(2):
                    key = ("cum", f, h)
                    dve.wait_ge(exb_done, 2 * f + h + 1)
                    b3 = g_bank(key).rearrange("p (n c) -> p n c", c=CH)
                    dlink(dve, dve.tensor_copy(blast[:, f, 8 * h:8 * h + 8], b3[:, :, CH - 1]))
                    ins = dve.tensor_tensor(khT[:, f, 512 * h:512 * h + 512].rearrange("p (n c) -> p n c", c=CH),
                                            blast[:, f, 8 * h:8 * h + 8].unsqueeze(2).broadcast_to([P, 8, CH]), b3, ALU.subtract)
                    g_done(ins, key)
                    g_read(dve, key)
                    dve.sem_inc(sub_done, 1)
            dve.memset(gss[:], 1.0).then_inc(gss_set, 1)
            for m in range(NT - 3, NT):
                stored(dve, m)
            dlink(dve, dve.memset(hist[:, 0], 0.0))
            dlink(dve, dve.memset(qz[:], 0.0))
            dlink(dve, dve.memset(am[:], 0.0))
            dlink(dve, dve.memset(qt[:], 0.0))
            dve.wait_ge(gin_loaded[1], 16)
            for f in range(2):
                dve.wait_ge(seen_done, f + 1)
                dve.tensor_tensor(khT[:, f, :], khT[:, f, :], gqk[:, 2 + f, 0:TP], ALU.mult).then_inc(qk_done, 1)
            g_read(dve, ("cums",), ("cum", 1, 1))
            for f in range(2):
                dve.tensor_tensor(kt[:, f, :], kt[:, f, :], gqk[:, 2 + f, 0:TP], ALU.mult).then_inc(qk_done, 1)
                for hh in range(2):
                    r = half(hh)
                    dve.tensor_scalar(qz[r, f, hh].rearrange("p b c -> p (b c)")[:, 0:NB * NB:NB + 1], gqk[r, f, TP:T], DK ** -0.5, None, ALU.mult)
                    ins = dve.scalar_tensor_tensor(qt[r, f, hh], gqk[r, f, 0:TP], DK ** -0.5, eb[r, f, 0:TP], ALU.mult, ALU.mult)
                ins.then_inc(qk_done, 1)
            dve.wait_ge(gst_loaded, 32)
            dlink(dve, dve.tensor_tensor(state[:], state[:],
                                         eb[:, :, TP:T].rearrange("p f b -> p b f").unsqueeze(3).broadcast_to([P, NB, 2, DV]), ALU.mult))
            for b in range(NB):
                key = ("vb", b)
                g_wait(dve, key)
                vb = g_bank(key).rearrange("p (f h v) -> p f h v", f=2, h=2)
                for hh in range(2):
                    r = half(hh)
                    ins = dve.tensor_tensor(vk[r, b], vb[r, :, hh, :],
                                            gqk[r, 2:4, TP + b:TP + b + 1].broadcast_to([DK, 2, DV]), ALU.mult)
                g_done(ins, key)
            g_read(dve, ("vb", NB - 1), ("vb", NB - 2))
            dve.tensor_tensor(state[:], state[:], vk[:], ALU.add).then_inc(st_done, 1)
            dve.wait_ge(st_done, 1)
            dve.sem_inc(st_done, 1)
            for n in range(NCH):
                key = ("kv", n)
                g_wait(dve, key)
                if n >= 1:
                    g_read(dve, ("kv", n - 1))
                for i in range(4):
                    f, hh = i // 2, i % 2
                    r = half(hh)
                    ins = dve.scalar_tensor_tensor(hist[r, n + 1, f, :], hist[r, n, f, :], eb[r, f, CH * n + CH - 1:CH * n + CH],
                                                   g_bank(key)[r, f * 256 + hh * DV:f * 256 + hh * DV + DV], ALU.mult, ALU.add)
                g_done(ins, key)

            def mask_a(t):
                key = ("A", t)
                g_wait(dve, key)
                if t >= 2:
                    g_wait(dve, ("O", t - 2))
                for h in range(HEADS):
                    ins = dve.copy_predicated(am[:, t % 2, h, :], const("chunkmask").bitcast(U32), g_bank(key)[:, h * P:(h + 1) * P])
                g_done(ins, key)

            def variance(i):
                c = slice(0, 4 * NORM_A) if i == 0 else slice(4 * NORM_A, 4 * TT)
                dve.wait_ge(gss_done, i + 1)
                dve.tensor_scalar(gtmp[:, c], gss[:, c], 1.0 / DV, EPS, ALU.mult, ALU.add).then_inc(grv_done, 1)

            def norm(i):
                c = slice(0, 4 * NORM_A) if i == 0 else slice(4 * NORM_A, 4 * TT)
                dve.wait_ge(gry_done, i + 1)
                newton(dve, grs[:, c], gtmp[:, c], gss[:, c])
                for n, t0, t1 in (((P, 0, NORM_A),) if i == 0 else ((P, NORM_A, 8), (NB, 8, 9))):
                    for t in range(t0, t1):
                        g_read(dve, ("O", t))
                    o = gout[0:n, t0:t1].rearrange("p t (h v) -> p (t h) v", h=4)
                    ins = dve.tensor_tensor(o, o, grs[0:n, 4 * t0:4 * t1].unsqueeze(2).broadcast_to([n, 4 * (t1 - t0), DV]), ALU.mult)
                ins.then_inc(gon_done, 1)

            def gated(t):
                c0, n = tok(t)
                key = ("oT", t)
                g_wait(dve, key)
                g_done(dve.scalar_tensor_tensor(mixT[:, 4:8, c0:c0 + n], g_bank(key).rearrange("p (h c) -> p h c", h=4)[:, :, 0:n],
                                                cols[:, GN:GN + 1], ggT[:, :, c0:c0 + n], ALU.mult, ALU.mult), key)

            mask_a(0)
            for t in range(TT):
                n = tok(t)[1]
                if t + 1 < 8:
                    mask_a(t + 1)
                key = ("O", t)
                g_wait(dve, key)
                g_done(dve.tensor_copy(gout[0:n, t, :], g_bank(key)[0:n, :]), key)
                if t == NORM_A:
                    variance(0)
                if t == NORM_A + 1:
                    dve_mla_early(dve)
                if t == NORM_A + 2:
                    norm(0)
            variance(1)
            dve.wait_ge(silu_e, 1)
            for t in range(NORM_A):
                gated(t)
            norm(1)
            for t in range(NORM_A, TT):
                gated(t)

        def newton(dve, y, v, tmp):
            dlink(dve, dve.tensor_tensor(tmp, y, y, ALU.mult))
            dlink(dve, dve.scalar_tensor_tensor(tmp, tmp, -0.5, v, ALU.mult, ALU.mult))
            dlink(dve, dve.scalar_tensor_tensor(y, tmp, 1.5, y, ALU.add, ALU.mult))

        class Banks:

            def __init__(self, name, banks, keys, after=None):
                self.banks, self.at, B = banks, {k: i for i, k in enumerate(keys)}, len(banks)
                assert len(self.at) == len(keys)
                if after is None:
                    self.full_sem, self.full0 = sem(name + "_full"), 0
                    self.free_sem, self.free0 = [sem(f"{name}_free{b}") for b in banks], [0] * B
                else:
                    n = len(after.at)
                    self.full_sem, self.full0 = after.full_sem, after.full0 + n
                    self.free_sem, self.free0 = after.free_sem, [f + (n - q + B - 1) // B for q, f in enumerate(after.free0)]

            def of(self, key):
                return psum[:, self.banks[self.at[key] % len(self.banks)], :]

            def begin(self, pe, key):
                q = self.at[key] % len(self.banks)
                n = self.free0[q] + self.at[key] // len(self.banks)
                if n:
                    pe.wait_ge(self.free_sem[q], n)

            def full(self, ins):
                ins.then_inc(self.full_sem, 1)

            def wait(self, eng, key):
                eng.wait_ge(self.full_sem, self.full0 + self.at[key] + 1)

            def free(self, ins, key):
                ins.then_inc(self.free_sem[self.at[key] % len(self.banks)], 1)

            def read(self, eng, key):
                q = self.at[key] % len(self.banks)
                eng.wait_ge(self.free_sem[q], self.free0[q] + self.at[key] // len(self.banks) + 1)

        at = AREA
        cqh, cql = (sb(at + i * 3 * T, f"cq_{n}", [P, 3, T], F32R) for i, n in enumerate(("hi", "lo"))); at += 6 * T
        ckh, ckl = (sb(at + i * 2 * T, f"ckv_{n}", [P, 2, T], F32R) for i, n in enumerate(("hi", "lo"))); at += 4 * T
        krh, krl = (sb(at + i * T, f"krope_{n}", [P, T], F32R) for i, n in enumerate(("hi", "lo"))); at += 2 * T
        qrh, qrl = (sb(at + i * 2 * T, f"qrope_{n}", [P, 2, T], F32R) for i, n in enumerate(("hi", "lo"))); at += 4 * T
        rst = sb(at - 4 * T, "rstd_rows", [P, 2, T])
        var = sb(at - 2 * T, "var_rows", [P, 2, T])
        V_AT = at
        vh, vl = (sb(at + i * 4096, f"v_{n}", [P, 8, 512], F32R) for i, n in enumerate(("hi", "lo"))); at += 8192
        LOOP_AT = at
        pth, ptl = (sb(at + i * 4096, f"pT_{n}", [P, 8, 512], F32R) for i, n in enumerate(("hi", "lo"))); at += 8192
        prow = sb(at, "p_rows", [P, 2, TP]); at += 2 * TP
        qh, ql = (sb(at + i * T, f"q_{n}", [P, T], F32R) for i, n in enumerate(("hi", "lo"))); at += 2 * T
        knh, knl = (sb(at + i * TP, f"kn_{n}", [P, TP], F32R) for i, n in enumerate(("hi", "lo"))); at += 2 * TP
        LOOP_END = at
        wqh, wql = (sb(at + i * 640, f"whead_{n}", [P, 5, P], F32R) for i, n in enumerate(("hi", "lo"))); at += 1280
        wqraw = sb(at, "whead_raw", [P, 5, P]); at += 640
        wuvh, wuvl = (sb(at + i * 1024, f"wuv_{n}", [P, 2, 512], F32R) for i, n in enumerate(("hi", "lo")))
        qh, ql = ((sb(at + i * T, f"q_even_{n}", [P, T], F32R), e) for i, (e, n) in enumerate(((qh, "hi"), (ql, "lo")))); at += 2 * T
        stat = sb(at, "softmax_stats", [P, 4, 8]); at += 32
        MLA_END = at
        at = LOOP_AT
        cqraw = sb(at, "cq_raw", [P, 3, T]); at += 3 * T
        ckraw = sb(at, "ckv_raw", [P, 2, T]); at += 2 * T
        krraw = sb(at, "krope_raw", [P, T]); at += T
        rope = sb(at, "rope_tables", [P, 2, T]); at += 2 * T
        sq = sb(at, "squares", [P, 2, T])
        xr = sb(at, "q_rope_in", [P, 2, T]); at += 2 * T
        ntmp = sb(at, "newton_tmp", [P, T]); at += T
        assert at <= LOOP_END
        at = V_AT
        uvraw = sb(at, "wuv_raw", [P, 2, 512]); at += 1024
        wrraw = sb(at, "wqrope_raw", [P, 2, 3, P]); at += 768
        wrh, wrl = (sb(at + i * 768, f"wqrope_{n}", [P, 2, 3, P], F32R) for i, n in enumerate(("hi", "lo"))); at += 1536
        tout = sb(at, "latent_rows", [P, TT, KVR + ROPE]); at += 2880
        assert at <= LOOP_AT

        M_TASKS = [("krd", b) for b in range(3)] + [("krs", b) for b in range(3)]
        M_TASKS += [("sqc", b) for b in range(3)] + [("sqq", b) for b in range(3)]
        M_TASKS += [("tok", t) for t in range(TT)]
        for pr in range(2):
            M_TASKS += [("qr", pr, b) for b in range(3)] + [("qs", pr, b) for b in range(3)]
        M_TASKS += [("v", t) for t in range(8)]
        mb = Banks("mla_setup_bank", list(range(6)), M_TASKS)
        min_loaded = [sem(f"mla_in{i}") for i in range(6)]
        sq_done, mv_done, mr_done, my_done = sem("squares_done"), sem("mla_var"), sem("mla_lnexp"), sem("mla_scaled")
        mh_done, ml_done, rows_done, rows_stored = sem("mla_hi"), sem("mla_lo"), sem("latent_rows_done"), sem("latent_stored")
        kr_done, qx_done, qrope_done = sem("krope_done"), sem("qrope_in"), sem("qrope_done")
        POOL_SPLITS = ["ck0", "ck1", "uv", "kr"]
        ml_pool = sem("mla_lo_by_gpsimd")
        SPLITS = ["wr", "ck0", "ck1", "cq0", "cq1", "cq2", "uv", "kr", "q0", "q1"] + [f"v{t}" for t in range(8)]

        def split_src(name):
            if name == "wr":
                return wrh[:], wrl[:], wrraw[:]
            if name == "uv":
                return wuvh[:], wuvl[:], uvraw[:]
            if name[:2] == "ck":
                k = int(name[2])
                return ckh[:, k], ckl[:, k], ckraw[:, k]
            if name[:2] == "cq":
                k = int(name[2])
                return cqh[:, k], cql[:, k], cqraw[:, k]
            if name == "kr":
                return krh[:], krl[:], krraw[:]
            if name[0] == "q":
                i = int(name[1])
                return qrh[:, i], qrl[:, i], xr[:, i]
            t = int(name[1])
            return vh[:, t], vl[:, t], mb.of(("v", t))

        def hi_of(act, name):
            h, _, s = split_src(name)
            act.activation(h, s, ACT.Copy).then_inc(mh_done, 1)

        def lo_of(dve, name):
            h, l, s = split_src(name)
            dve.wait_ge(mh_done, SPLITS.index(name) + 1)
            ins = dve.tensor_tensor(l, s, h.bitcast(F32), ALU.subtract)
            if name[0] == "v":
                mb.free(ins, ("v", int(name[1])))
            else:
                ins.then_inc(ml_pool if name in POOL_SPLITS else ml_done, 1)

        def split(eng, name):
            if name in POOL_SPLITS:
                eng.wait_ge(ml_pool, POOL_SPLITS.index(name) + 1)
            else:
                eng.wait_ge(ml_done, [x for x in SPLITS if x not in POOL_SPLITS].index(name) + 1)

        def pool_mla_in(pool):
            for name in POOL_SPLITS:
                lo_of(pool, name)

        def passes(pe, o, pairs, stop=True, start=True):
            n = 3 * len(pairs)
            for i, (w, x) in enumerate((w, x) for (wh, wl), (xh, xl) in pairs for w, x in ((wh, xh), (wh, xl), (wl, xh))):
                mm = pe.matmul(o, w, x, start=(start and i == 0), stop=(stop and i == n - 1))
            return mm

        def sp_mla_early(sp):
            sp.dma_start(krraw[0:ROPE, :], scratch[0, 0:ROPE, :]).then_inc(min_loaded[2], 16)
            sp.dma_start(rope[:], a["rope"].rearrange("p (c t) -> p c t", c=2)).then_inc(min_loaded[3], 16)
            sp.dma_start(ckraw[:], scratch[ROW_CKV:ROW_CKV + 2].rearrange("m p t -> p m t")).then_inc(min_loaded[0], 16)

        def sp_mla_in(sp):
            g_wait(sp, ("O", TT - 1))
            sp.wait_ge(gst_stored, 48)
            sp.dma_start(cqraw[:], scratch[ROW_CQ:ROW_CQ + 3].rearrange("m p t -> p m t")).then_inc(min_loaded[1], 16)
            uq = a["w_uq"].rearrange("l (k p) (g h c) -> p (l k) g h c", p=P, g=2, h=2)
            for pr in range(2):
                for hh in range(2):
                    sp.dma_start(wrraw[:, pr, :, ROPE * hh:ROPE * hh + ROPE], uq[:, :, pr, hh, NOPE:]).then_inc(min_loaded[4], 16)
            sp.dma_start(uvraw[:], a["w_uv"].rearrange("l (k p) h n -> p (l k) (h n)", p=P)).then_inc(min_loaded[5], 16)
            g_read(sp, ("oT", TT - 1), ("oT", TT - 2))
            load_head(sp, 0)
            sp.wait_ge(rows_done, 1)
            for t0, n, o1, o2 in ((0, P, out["ckv_prompt"], out["krope_prompt"]), (8, NB, out["ckv_sample"], out["krope_sample"])):
                ts = slice(0, 8) if t0 == 0 else slice(8, 9)
                for o, c in ((o1, slice(0, KVR)), (o2, slice(KVR, KVR + ROPE))):
                    dst = o[0, 0].rearrange("(t p) c -> p t c", p=P) if t0 == 0 else o[0].rearrange("b t c -> b t c")
                    sp.dma_start(dst, tout[0:n, ts, c]).then_inc(rows_stored, 16)

        wh_loaded, wh_hi, wh_lo = sem("whead_loaded"), sem("whead_hi"), sem("whead_lo")

        def load_head(sp, h):
            if h >= 1:
                sp.wait_ge(wh_lo, h)
            uq = a["w_uq"].rearrange("l (k p) (h c) -> p (l k) h c", p=P, h=HEADS)
            sp.dma_start(wqraw[:, 0:3, :], uq[:, :, h, 0:NOPE]).then_inc(wh_loaded, 16)
            sp.dma_start(wqraw[:, 3:5, :], a["w_uk"].rearrange("l (k p) h n -> p (l k) h n", p=P)[:, :, h, :]).then_inc(wh_loaded, 16)

        def pe_mla_early(pe):
            pe.wait_ge(min_loaded[2], 16)
            for name, c in (("krd", "dup"), ("krs", "swapdup")):
                for b in range(3):
                    mb.begin(pe, (name, b))
                    mb.full(pe.matmul(mb.of((name, b))[:, 0:BLK], const(c)[0:ROPE, :],
                                      krraw[0:ROPE, b * BLK:(b + 1) * BLK], start=True, stop=True))

        def pe_mla_in(pe):
            for j, (name, nk) in enumerate((("sqc", 2), ("sqq", 3))):
                for b in range(3):
                    mb.begin(pe, (name, b))
                for k in range(nk):
                    pe.wait_ge(sq_done, 2 * j + k + 1)
                    for b in range(3):
                        mm = pe.matmul(mb.of((name, b))[:, 0:BLK], const("ones"), sq[:, (2 * j + k) % 2, b * BLK:(b + 1) * BLK],
                                       start=(k == 0), stop=(k == nk - 1))
                        if k == nk - 1:
                            mb.full(mm)
                        elif b == 2:
                            mm.then_inc(sq_read, 1)
            pe.wait_ge(kr_done, 1)
            pe.wait_ge(my_done, 2)
            for t in range(TT):
                c0, n = tok(t)
                mb.begin(pe, ("tok", t))
                o = mb.of(("tok", t))
                for k in range(2):
                    pe.transpose(o[0:n, k * P:(k + 1) * P], ckraw[:, k, c0:c0 + n], ident)
                mb.full(pe.transpose(o[0:n, KVR:KVR + ROPE], krraw[0:ROPE, c0:c0 + n], ident[0:ROPE, 0:ROPE]))
            split(pe, "cq2")
            for pr in range(2):
                for b in range(3):
                    mb.begin(pe, ("qr", pr, b))
                    c = slice(b * BLK, (b + 1) * BLK)
                    mb.full(passes(pe, mb.of(("qr", pr, b))[:, 0:BLK],
                                   [((wrh[:, pr, k], wrl[:, pr, k]), (cqh[:, k, c], cql[:, k, c])) for k in range(3)]))
                for b in range(3):
                    mb.begin(pe, ("qs", pr, b))
                    pe.wait_ge(qx_done, 3 * pr + b + 1)
                    mb.full(pe.matmul(mb.of(("qs", pr, b))[:, 0:BLK], const("swap"), xr[:, pr, b * BLK:(b + 1) * BLK], start=True, stop=True))
            pe.wait_ge(rows_stored, 64)
            split(pe, "uv")
            for t in range(8):
                mb.begin(pe, ("v", t))
                c = slice(t * P, (t + 1) * P)
                mb.full(passes(pe, mb.of(("v", t)), [((ckh[:, k, c], ckl[:, k, c]), (wuvh[:, k], wuvl[:, k])) for k in range(2)]))

        sq_read = sem("squares_read")

        def act_mla_in(act):
            act.wait_ge(gst_stored, 48)
            for j in range(5):
                act.wait_ge(min_loaded[0 if j < 2 else 1], 16)
                if j == 2:
                    act.wait_ge(sq_read, 1)
                if j == 3:
                    mb.wait(act, ("sqc", 2))
                if j == 4:
                    act.wait_ge(sq_read, 2)
                act.activation(sq[:, j % 2, :], (ckraw[:, j] if j < 2 else cqraw[:, j - 2]), ACT.Square).then_inc(sq_done, 1)
            act.wait_ge(min_loaded[4], 64)
            hi_of(act, "wr")
            for j in range(2):
                act.wait_ge(mv_done, j + 1)
                ins = act.activation(rst[:, j], var[:, j], ACT.Ln)
            alink(act, ins)
            for j in range(2):
                act.activation(rst[:, j], rst[:, j], ACT.Exp, scale=-0.5).then_inc(mr_done, 1)
            for j, name in enumerate(SPLITS[1:6]):
                act.wait_ge(my_done, j + 1)
                hi_of(act, name)
            act.wait_ge(min_loaded[5], 16)
            g_read(act, ("oT", TT - 1), ("oT", TT - 2))
            hi_of(act, "uv")
            act.wait_ge(kr_done, 1)
            hi_of(act, "kr")
            for pr in range(2):
                for b in range(3):
                    mb.wait(act, ("qr", pr, b))
                    ins = act.activation(xr[:, pr, b * BLK:(b + 1) * BLK], mb.of(("qr", pr, b))[:, 0:BLK], ACT.Copy)
                    mb.free(ins, ("qr", pr, b))
                    mb.read(act, ("qr", pr, b))
                    act.sem_inc(qx_done, 1)
                act.wait_ge(qrope_done, pr + 1)
                hi_of(act, f"q{pr}")
            for t in range(8):
                mb.wait(act, ("v", t))
                hi_of(act, f"v{t}")
            head_hi(act, 0)

        def head_hi(act, h):
            act.wait_ge(wh_loaded, 32 * (h + 1))
            if h >= 1:
                wk.wait(act, ("k", h - 1, 1))
            act.activation(wqh[:], wqraw[:], ACT.Copy).then_inc(wh_hi, 1)

        def head_lo(dve, h):
            dve.wait_ge(wh_hi, h + 1)
            dve.tensor_tensor(wql[:], wqraw[:], wqh[:].bitcast(F32), ALU.subtract).then_inc(wh_lo, 1)

        def dve_mla_early(dve):
            dve.wait_ge(min_loaded[3], 16)
            rotate(dve, "krd", "krs", krraw)
            dve.wait_ge(kr_done, 1)

        def dve_mla_in(dve):
            NORMS = (("ck", "sqc", ckraw, 2, KVN), ("cq", "sqq", cqraw, 3, QN))
            for j, (name, nm, raw, nk, g) in enumerate(NORMS):
                for b in range(3):
                    mb.wait(dve, (nm, b))
                    mb.free(dve.tensor_scalar(var[:, j, b * BLK:(b + 1) * BLK], mb.of((nm, b))[:, 0:BLK], 1.0 / (nk * P), EPS,
                                              ALU.mult, ALU.add), (nm, b))
                mb.read(dve, (nm, 2))
                dve.sem_inc(mv_done, 1)
            lo_of(dve, "wr")
            for j, (name, nm, raw, nk, g) in enumerate(NORMS):
                dve.wait_ge(mr_done, j + 1)
                newton(dve, rst[:, j], var[:, j], ntmp[:])
                for k in range(nk):
                    dve.scalar_tensor_tensor(raw[:, k], raw[:, k], cols[:, g + k:g + k + 1], rst[:, j], ALU.mult, ALU.mult).then_inc(my_done, 1)
            for name in ("cq0", "cq1", "cq2"):
                lo_of(dve, name)
            for t in range(TT):
                c0, n = tok(t)
                mb.wait(dve, ("tok", t))
                mb.free(dve.tensor_copy(tout[0:n, t, :], mb.of(("tok", t))[0:n, 0:KVR + ROPE]), ("tok", t))
            mb.read(dve, ("tok", TT - 1))
            dve.sem_inc(rows_done, 1)
            for pr in range(2):
                for b in range(3):
                    c = slice(b * BLK, (b + 1) * BLK)
                    mb.wait(dve, ("qs", pr, b))
                    dlink(dve, dve.tensor_tensor(xr[:, pr, c], xr[:, pr, c], rope[:, 0, c], ALU.mult))
                    mb.free(dve.tensor_tensor(ntmp[:, c], mb.of(("qs", pr, b))[:, 0:BLK], rope[:, 1, c], ALU.mult), ("qs", pr, b))
                    mb.read(dve, ("qs", pr, b))
                    dlink(dve, dve.tensor_tensor(xr[:, pr, c], xr[:, pr, c], ntmp[:, c], ALU.add))
                dve.sem_inc(qrope_done, 1)
                dlink(dve, dve.tensor_copy(smp[:, 32 + 8 * pr:40 + 8 * pr], xr[:, pr, TP:T]))
                lo_of(dve, f"q{pr}")
            dve.tensor_copy(smp[:, 48:64].rearrange("p (k b) -> p k b", k=2), ckraw[:, :, TP:T])
            dlink(dve, dve.tensor_copy(smp[:, 64:72], krraw[:, TP:T]))
            for t in range(8):
                lo_of(dve, f"v{t}")
            head_lo(dve, 0)

        def rotate(dve, plain, swapped, o):
            for b in range(3):
                c = slice(b * BLK, (b + 1) * BLK)
                mb.wait(dve, (swapped, b))
                mb.wait(dve, (swapped, 2))
                mb.free(dve.tensor_tensor(o[:, c], mb.of((plain, b))[:, 0:BLK], rope[:, 0, c], ALU.mult), (plain, b))
                mb.free(dve.tensor_tensor(ntmp[:, c], mb.of((swapped, b))[:, 0:BLK], rope[:, 1, c], ALU.mult), (swapped, b))
            mb.read(dve, (swapped, 2))
            mb.read(dve, (plain, 2))
            dve.tensor_tensor(o[:], o[:], ntmp[:], ALU.add).then_inc(kr_done, 1)

        UNITS = 8 * HEADS
        def qk_tasks(v):
            if v == -1:
                return [("q", 0, b) for b in range(3)] + [("k", 0, b) for b in range(2)]
            h, i = v // 8 + 1, v % 8
            if h >= HEADS:
                return []
            return [("q", h, i - 2)] if i in (2, 3, 4) else [("k", h, b) for b in range(2)] if i == 7 else []

        W_TASKS = []
        for v in range(UNITS + 3):
            if v == 0:
                W_TASKS += qk_tasks(-1)
            if v >= 3 and (v - 3) % 4 == 3:
                W_TASKS += [("pv", (v - 3) // 8, (v - 3) % 8 // 4)]
            W_TASKS += qk_tasks(v)
        wk = Banks("head_bank", [6, 7], W_TASKS)
        tp = Banks("pT_bank", [4, 5], [(u, g) for u in range(UNITS) for g in range(1 + (u % 8 >= 4))])
        sc_full, nb_done, ex_done, pn_done, wk_hi, tp_hi = (sem(n) for n in (
            "scores_full", "softmax_bias", "softmax_exp", "p_normed", "head_hi_part", "pT_hi_part"))
        HI = [k for k in W_TASKS if k[0] != "pv"]

        def sc_view(u):
            i = u % 8
            w = max((i + 1) * P, 256)
            nb = 1 if w <= 512 else 2
            return psum[:, 2 * (u % 2):2 * (u % 2) + nb, 0:w // nb], nb, w // nb

        def sc_used(u):
            s, nb, w = sc_view(u)
            return s[:, :, 0:P] if u % 8 == 0 else s

        def blocks(u, g):
            return range(4 * g, min(4 * g + 4, u % 8 + 1))

        def pe_qk(pe, v):
            for kind, h, b in qk_tasks(v):
                key = (kind, h, b)
                pe.wait_ge(wh_lo, h + 1)
                wk.begin(pe, key)
                if kind == "q":
                    c = slice(b * BLK, (b + 1) * BLK)
                    wk.full(passes(pe, wk.of(key)[:, 0:BLK], [((wqh[:, k], wql[:, k]), (cqh[:, k, c], cql[:, k, c])) for k in range(3)]))
                else:
                    c = slice(b * 512, b * 512 + 512)
                    wk.full(passes(pe, wk.of(key), [((wqh[:, 3 + k], wql[:, 3 + k]), (ckh[:, k, c], ckl[:, k, c])) for k in range(2)]))

        def act_qk(act, v):
            for key in qk_tasks(v):
                h = key[1]
                wk.wait(act, key)
                b = key[2]
                if key[0] == "q":
                    ins = act.activation(qh[h % 2][:, b * BLK:(b + 1) * BLK], wk.of(key)[:, 0:BLK], ACT.Copy)
                else:
                    ins = act.activation(knh[:, b * 512:b * 512 + 512], wk.of(key), ACT.Copy)
                ins.then_inc(wk_hi, 1)

        def dve_qk(dve, v):
            for key in qk_tasks(v):
                h = key[1]
                dve.wait_ge(wk_hi, HI.index(key) + 1)
                b = key[2]
                if key[0] == "q":
                    if b == 2:
                        dve.tensor_copy(smp[:, 8 * h:8 * h + 8], wk.of(key)[:, BLK - NB:BLK])
                    c = slice(b * BLK, (b + 1) * BLK)
                    ins = dve.tensor_tensor(ql[h % 2][:, c], wk.of(key)[:, 0:BLK], qh[h % 2][:, c].bitcast(F32), ALU.subtract)
                else:
                    c = slice(b * 512, b * 512 + 512)
                    ins = dve.tensor_tensor(knl[:, c], wk.of(key), knh[:, c].bitcast(F32), ALU.subtract)
                wk.free(ins, key)

        def pe_mla(pe):
            pe_qk(pe, -1)
            def scores(v):
                h, i = v // 8, v % 8
                if i == 0:
                    wk.read(pe, ("k", h, 1))
                    wk.read(pe, ("k", h, 0))
                    wk.read(pe, ("q", h, 2)), wk.read(pe, ("q", h, 1))
                    if h == 0:
                        split(pe, "kr")
                        mb.read(pe, ("v", 7)), mb.read(pe, ("v", 6))
                if v >= 2:
                    pe.wait_ge(ex_done, v - 1)
                s, nb, w = sc_view(v)
                qc, r = slice(i * P, (i + 1) * P), slice(ROPE * (h % 2), ROPE * (h % 2) + ROPE)
                for p in range(nb):
                    kc = slice(p * w, (p + 1) * w)
                    mm = passes(pe, s[:, p, :], [((qh[h % 2][:, qc], ql[h % 2][:, qc]), (knh[:, kc], knl[:, kc])),
                                                 ((qrh[r, h // 2, qc], qrl[r, h // 2, qc]), (krh[r, kc], krl[r, kc]))])
                mm.then_inc(sc_full, 1)

            def values(u):
                h, hf = u // 8, u % 8 // 4
                key = ("pv", h, hf)
                tp.read(pe, (u, len(range(1 + (u % 8 >= 4))) - 1))
                if hf:
                    tp.read(pe, (u, 0))
                wk.begin(pe, key)
                for j in range(4 * hf + 4):
                    q0 = max(0, j - 4 * hf) * P
                    for n, (vv, pp) in enumerate(((vh, pth), (vh, ptl), (vl, pth))):
                        mm = pe.matmul(wk.of(key)[:, q0:512], vv[:, j, h * P:(h + 1) * P], pp[:, j, q0:512],
                                       start=(j == 0 and n == 0), stop=(j == 4 * hf + 3 and n == 2))
                wk.full(mm)

            def probabilities_T(u):
                pe.wait_ge(pn_done, u + 1)
                for g in range(1 + (u % 8 >= 4)):
                    tp.begin(pe, (u, g))
                    for j in blocks(u, g):
                        mm = pe.transpose(tp.of((u, g))[:, (j % 4) * P:(j % 4 + 1) * P], prow[:, u % 2, j * P:(j + 1) * P], ident)
                    tp.full(mm)

            for v in range(UNITS + 3):
                late = v % 8 == 0 and 0 < v < UNITS
                if v < UNITS and not late:
                    scores(v)
                if v >= 3 and (v - 3) % 4 == 3:
                    values(v - 3)
                if 0 <= v - 2 < UNITS:
                    probabilities_T(v - 2)
                if late:
                    scores(v)
                pe_qk(pe, v)

        def pt_cols(t, u, g):
            b = blocks(u, g)
            return t[:, b[0]:b[-1] + 1, (u % 4) * P:(u % 4 + 1) * P]

        def tp_cols(u, g):
            return tp.of((u, g))[:, 0:len(blocks(u, g)) * P].rearrange("p (j c) -> p j c", c=P)

        def act_mla(act):
            act_qk(act, -1)
            for v in range(UNITS + 2):
                if v < UNITS:
                    act.wait_ge(nb_done, v + 1)
                    if v >= 2:
                        tp.wait(act, (v - 2, 1 if (v - 2) % 8 >= 4 else 0))
                    s = sc_used(v)
                    act.activation(prow[:, v % 2, 0:(v % 8 + 1) * P].rearrange("p (n w) -> p n w", n=s.shape[1]), s, ACT.Exp,
                                   scale=SCALE, bias=stat[:, v % 4, 1:2], accum_out=stat[:, v % 4, 2:3]).then_inc(ex_done, 1)
                u = v - 2
                if 0 <= u:
                    for g in range(1 + (u % 8 >= 4)):
                        tp.wait(act, (u, g))
                        act.activation(pt_cols(pth, u, g), tp_cols(u, g), ACT.Copy).then_inc(tp_hi, 1)
                act_qk(act, v)
                if v % 8 == 1 and v // 8 + 1 < HEADS:
                    head_hi(act, v // 8 + 1)

        def dve_mla(dve):
            dve_qk(dve, -1)
            for v in range(UNITS + 3):
                if v < UNITS:
                    s, nb, w = sc_view(v)
                    i = v % 8
                    dve.wait_ge(sc_full, v + 1)
                    diag = s[:, 0, 0:P] if i == 0 else s[:, nb - 1, w - P:w]
                    dlink(dve, dve.tensor_tensor(diag, diag, const("causal"), ALU.add))
                    dlink(dve, dve.tensor_reduce(stat[:, v % 4, 0:1], sc_used(v), AX.XY, ALU.max))
                    dve.tensor_scalar(stat[:, v % 4, 1:2], stat[:, v % 4, 0:1], -SCALE, None, ALU.mult).then_inc(nb_done, 1)
                u = v - 1
                if 0 <= u < UNITS:
                    dve.wait_ge(ex_done, u + 1)
                    dlink(dve, dve.reciprocal(stat[:, u % 4, 3:4], stat[:, u % 4, 2:3]))
                    c = slice(0, (u % 8 + 1) * P)
                    dve.tensor_scalar(prow[:, u % 2, c], prow[:, u % 2, c], stat[:, u % 4, 3:4], None, ALU.mult).then_inc(pn_done, 1)
                u = v - 3
                if u >= 0 and u % 4 == 3:
                    h, hf = u // 8, u % 8 // 4
                    key = ("pv", h, hf)
                    wk.wait(dve, key)
                    wk.free(dve.tensor_copy(mixT[:, h, hf * 512:hf * 512 + 512], wk.of(key)), key)
                u = v - 2
                if 0 <= u < UNITS:
                    for g in range(1 + (u % 8 >= 4)):
                        dve.wait_ge(tp_hi, tp.at[(u, g)] + 1)
                        tp.free(dve.tensor_tensor(pt_cols(ptl, u, g), tp_cols(u, g), pt_cols(pth, u, g).bitcast(F32), ALU.subtract), (u, g))
                dve_qk(dve, v)
                if v % 8 == 1 and v // 8 + 1 < HEADS:
                    head_lo(dve, v // 8 + 1)

        def sp_mla(sp):
            for h in range(1, HEADS):
                load_head(sp, h)

        RB = (KVR + ROPE) // 32
        at = AREA
        NAT = 3
        nat = sb(at, "ckv_pages", [P, NAT, PAGES, KVR]); at += NAT * PAGES * KVR
        krn = sb(LOOP_END, "krope_pages", [P, NAT, PAGES, ROPE])
        oacc = sb(at, "o_past", [4, NB, KVR])
        cnew = sb(at + NB * KVR, "ckv_new_rows", [4, NB, KVR])
        tt = sb(at, "pages_T", [P, 2, RB, PAGES * 32]); at += 2 * RB * PAGES * 32
        QB_AT = at
        qb = sb(at, "q_blocks", [P, NB, RB, P]); at += NB * RB * P
        pex = sb(at, "p_decode", [P, 2, 512]); at += 1024
        pet = sb(at, "p_decode_T", [P, 2, PAGES, 32]); at += 1024
        ukr = sb(at, "wuk_raw", [P, 2, 512])
        ukt = sb(at + 1024, "wuk_T", [P, HEADS, 2, P])
        o4 = sb(at, "o_groups", [P, NB, KVR]); at += NB * KVR
        qlat = sb(at, "q_latent", [P, 2, 32]); at += 64
        uvf = sb(at, "wuv_f32", [P, 2, 512]); at += 1024
        olat = sb(at, "o_latent", [P, 2, NB, HEADS]); at += 64
        mcol = sb(at, "row_max", [P, 8]); at += 8
        mrow = sb(at, "minus_max_row", [1, 2, 4, 32]); at += 256
        m4 = sb(at, "head_max", [1, 8]); at += 8
        bias = sb(at, "exp_bias", [P, NB]); at += 8
        rsum = sb(at, "exp_sums", [P, NB]); at += 8
        snew = sb(at, "new_products", [P, 3, 32]); at += 96
        mg = sb(at, "merge", [4, 12, NB]); at += 96
        sn4 = sb(at, "new_scores", [4, 4, NB]); at += 32
        assert at <= LOOP_END and LOOP_END + NAT * PAGES * ROPE <= 53200
        assert 2 * PAGES * KVR <= 10 * T

        DP_TASKS = [("ukT", i) for i in range(2)] + [("qlat",), ("spread",), ("snew",)]
        for v in range(NB + 2):
            if 1 <= v <= NB:
                DP_TASKS += [("mT", v - 1), ("bias", v - 1)]
        DP_TASKS += [("lsum",)] + [("osum", q) for q in range(4)] + [("oT",), ("uv",)]
        dq = Banks("decode_bank", [4, 5, 6, 7], DP_TASKS)
        ds = Banks("decode_scores", [0, 1], list(range(NB)))
        dv = Banks("decode_values", [2, 3], list(range(NB)))
        pt_loaded, duk_loaded, duv_loaded, cnew_loaded = (sem(n) for n in ("page_table_loaded", "wuk_loaded", "wuv_f32_loaded", "ckv_new_loaded"))
        nat_loaded = [sem(f"ckv_pages_loaded{i}") for i in range(NAT)]
        krn_loaded = [sem(f"krope_pages_loaded{i}") for i in range(NAT)]
        tt_done, max_done, pet_done, qb_done, sp_done = (sem(n) for n in (
            "pages_transposed", "decode_max", "p_decode_transposed", "q_blocks_done", "new_products_done"))
        mrow_done, bias_done, mg_done, om_done, w_exp = (sem(n) for n in (
            "minus_max_done", "bias_done", "merge_differences", "o_merged", "merge_exps"))

        def sp_decode(sp):
            sp.dma_start(pt[:], a["page_table"].rearrange("(o b) n -> o (b n)", o=1)).then_inc(pt_loaded, 16)
            sp.wait_ge(pt_loaded, 16)
            wk.wait(sp, ("k", HEADS - 1, 1))
            for b in range(NB):
                if b == 2:
                    wk.read(sp, ("pv", 3, 1)), wk.read(sp, ("pv", 3, 0))
                    sp.dma_start(ukr[:], a["w_uk"].rearrange("l (k p) h n -> p (l k) (h n)", p=P)).then_inc(duk_loaded, 16)
                    sp.dma_start(uvf[:], a["w_uv"].rearrange("l (k p) h n -> p (l k) (h n)", p=P)).then_inc(duv_loaded, 16)
                pages = pages_of(sp, b)
                if b >= NAT:
                    dv.wait(sp, b - NAT)
                    sp.wait_ge(tt_done, b - NAT + 1)
                for j, page in enumerate(pages):
                    if j < SP_KR:
                        load_kr(sp, b, j, page, nat_loaded)
                    load_ckv(sp, b, j, page)
            ds.wait(sp, 3)
            for k in range(WO_SLOTS):
                load_wo(sp, k)
            sp.wait_ge(rows_stored, 64)
            ds.wait(sp, NB - 1), ds.wait(sp, NB - 2)
            sp.dma_start(cnew[:], out["ckv_sample"][0].rearrange("b t c -> t b c").broadcast_to([4, NB, KVR])).then_inc(cnew_loaded, 16)

        SP_KR = 2

        def load_ckv(eng, b, j, page):
            src = a["cache_ckv"][0, bass.ds(page, 1)].rearrange("o p c -> (o p) c")
            eng.dma_start(nat[:, b % NAT, j, :], src).then_inc(nat_loaded[b % NAT], 16)

        def load_kr(eng, b, j, page, loaded):
            src = a["cache_krope"][0, bass.ds(page, 1)].rearrange("o p c -> (o p) c")
            eng.dma_start(krn[:, b % NAT, j, :], src).then_inc(loaded[b % NAT], 16)

        def pages_of(eng, b, j0=0):
            return [eng.value_load(pt[0:1, b * PAGES + j:b * PAGES + j + 1], min_val=0, max_val=N_PHYS - 1) for j in range(j0, PAGES)]

        def pool_decode(pool):
            wk.wait(pool, ("k", HEADS - 1, 1))
            pool.wait_ge(pt_loaded, 16)
            for b in range(NB):
                pages = pages_of(pool, b, SP_KR)
                if b >= NAT:
                    pool.wait_ge(tt_done, b - NAT + 1)
                for j, page in enumerate(pages):
                    load_kr(pool, b, SP_KR + j, page, krn_loaded)

        def pe_decode(pe):
            pe.wait_ge(duk_loaded, 16)
            for i in range(2):
                dq.begin(pe, ("ukT", i))
                for j in range(4):
                    h, k = (4 * i + j) // 2, j % 2
                    mm = pe.transpose(dq.of(("ukT", i))[:, j * P:(j + 1) * P], ukr[:, k, h * P:(h + 1) * P], ident)
                dq.full(mm)
            dq.begin(pe, ("qlat",))
            dq.read(pe, ("ukT", 0)), dq.read(pe, ("ukT", 1))
            for h in range(HEADS):
                for k in range(2):
                    mm = pe.matmul(dq.of(("qlat",))[:, 32 * k + 8 * h:32 * k + 8 * h + 8], ukt[:, h, k, :], smp[:, 8 * h:8 * h + 8],
                                   start=True, stop=True)
            dq.full(mm)
            dq.begin(pe, ("spread",))
            dq.read(pe, ("qlat",))
            o = dq.of(("spread",))
            for rq in range(4):
                for k in range(2):
                    rb = 4 * k + rq
                    pe.matmul(o[:, 32 * rb:32 * rb + 32], const("spread")[:, rq * P:(rq + 1) * P], qlat[:, k, :], start=True, stop=True)
                hh, eb_ = rq // 2, rq % 2
                mm = pe.matmul(o[:, 32 * (8 + eb_):32 * (9 + eb_)].rearrange("p (r h b) -> p r h b", r=2, h=2)[:, :, hh, :],
                               const("spread")[:, rq * P:(rq + 1) * P], smp[:, 32:48].rearrange("p (r b) -> p r b", r=2), start=True, stop=True)
            dq.full(mm)
            dq.begin(pe, ("snew",))
            pe.wait_ge(sp_done, 1)
            o = dq.of(("snew",))
            pe.matmul(o[0:4, 0:32], const("ones")[:, 0:4], snew[:, 0, :], start=True, stop=False)
            pe.matmul(o[0:4, 0:32], const("ones")[:, 0:4], snew[:, 1, :], start=False, stop=False)
            dq.full(pe.matmul(o[0:4, 0:32], const("ones")[:, 0:4], snew[:, 2, :], start=False, stop=True))
            def values(u):
                dv.begin(pe, u)
                pe.wait_ge(pet_done, u + 1)
                for j in range(PAGES):
                    g = j % 4
                    mm = pe.matmul(dv.of(u)[32 * g:32 * g + 32, 0:KVR], pet[:, u % 2, j, :], nat[:, u % NAT, j, :],
                                   start=(j < 4), stop=(j >= PAGES - 4))
                dv.full(mm)

            def minus_max(u):
                dq.begin(pe, ("bias", u))
                pe.wait_ge(mrow_done, u + 1)
                dq.full(pe.matmul(dq.of(("bias", u))[:, 0:1], mrow[0:1, u % 2].rearrange("o k h -> o (k h)"), const("ones")[0:1, 0:1], start=True, stop=True))

            pe.wait_ge(qb_done, 1)
            for v in range(NB + 1):
                u = v - 1
                if u >= 1:
                    values(u - 1)
                if u >= 0:
                    dq.begin(pe, ("mT", u))
                    pe.wait_ge(max_done, u + 1)
                    dq.full(pe.transpose(dq.of(("mT", u))[0:1, 0:P], mcol[:, u:u + 1], ident))
                if v < NB:
                    ds.begin(pe, v)
                    pe.wait_ge(tt_done, v + 1)
                    for r in range(RB):
                        if r == RB // 2 and u >= 0:
                            minus_max(u)
                        mm = pe.matmul(ds.of(v), qb[:, v, r, :], tt[:, v % 2, r, :], start=(r == 0), stop=(r == RB - 1))
                    ds.full(mm)
            minus_max(NB - 1)
            values(NB - 1)
            dq.begin(pe, ("lsum",))
            dq.full(pe.matmul(dq.of(("lsum",))[0:4, 0:NB], const("sumkq"), rsum[:], start=True, stop=True))
            dv.read(pe, NB - 1), dv.read(pe, NB - 2)
            for q in range(4):
                dq.begin(pe, ("osum", q))
                dq.full(pe.matmul(dq.of(("osum", q))[0:4, :], const("sumkq"), o4[:, 2 * q:2 * q + 2, :].rearrange("p b c -> p (b c)"), start=True, stop=True))
            dq.begin(pe, ("oT",))
            pe.wait_ge(om_done, 1)
            for k in range(2):
                for b in range(NB):
                    mm = pe.transpose(dq.of(("oT",))[:, (k * NB + b) * 4:(k * NB + b) * 4 + 4], oacc[:, b, k * P:(k + 1) * P], ident[0:4, 0:4])
            dq.full(mm)
            dq.begin(pe, ("uv",))
            dq.read(pe, ("oT",))
            pe.wait_ge(duv_loaded, 16)
            for h in range(HEADS):
                for k in range(2):
                    mm = pe.matmul(dq.of(("uv",))[:, NB * h:NB * h + NB], uvf[:, k, h * P:(h + 1) * P], olat[:, k, :, h], start=(k == 0), stop=(k == 1))
            dq.full(mm)

        def act_decode(act):
            for i in range(2):
                key = ("ukT", i)
                dq.wait(act, key)
                dq.free(act.activation(ukt[:, 2 * i:2 * i + 2].rearrange("p h k c -> p (h k c)"), dq.of(key), ACT.Copy), key)
            dq.wait(act, ("qlat",))
            dq.free(act.activation(qlat[:].rearrange("p k c -> p (k c)"), dq.of(("qlat",))[:, 0:64], ACT.Copy), ("qlat",))
            for v in range(NB + 1):
                u = v - 1
                if u >= 0:
                    act.wait_ge(bias_done, u + 1)
                    if u >= 2:
                        act.wait_ge(pet_done, u - 1)
                    ds.wait(act, u)
                    ds.free(act.activation(pex[:, u % 2], ds.of(u), ACT.Exp, scale=SCALE, bias=bias[:, u:u + 1],
                                           accum_out=rsum[:, u:u + 1]), u)
                if u >= 1:
                    dv.wait(act, u - 1)
                    dv.free(act.activation(o4[:, u - 1, :], dv.of(u - 1)[:, 0:KVR], ACT.Copy), u - 1)
            dv.wait(act, NB - 1)
            dv.free(act.activation(o4[:, NB - 1, :], dv.of(NB - 1)[:, 0:KVR], ACT.Copy), NB - 1)
            act.wait_ge(mg_done, 1)
            act.activation(mg[:, 3:5], mg[:, 3:5], ACT.Exp).then_inc(w_exp, 1)

        def dve_decode(dve):
            wk.read(dve, ("pv", 3, 1))
            dve.memset(qb[:, 0:4], 0.0)
            dlink(dve, dve.memset(qb[:, 4:8], 0.0))
            dlink(dve, dve.memset(mrow[:], 0.0))

            def pages_T(v):
                if v >= 2:
                    ds.wait(dve, v - 2)
                dve.wait_ge(nat_loaded[v % NAT], 16 * (PAGES + SP_KR) * (v // NAT + 1))
                dve.transpose(tt[:, v % 2, 0:8, :].rearrange("p r (t c) -> p t r c", c=32), nat[:, v % NAT].rearrange("p t (r c) -> p t r c", c=32))
                dve.wait_ge(krn_loaded[v % NAT], 16 * (PAGES - SP_KR) * (v // NAT + 1))
                dve.transpose(tt[:, v % 2, 8:10, :].rearrange("p r (t c) -> p t r c", c=32),
                              krn[:, v % NAT].rearrange("p t (r c) -> p t r c", c=32)).then_inc(tt_done, 1)

            pages_T(0)
            dq.wait(dve, ("spread",))
            src = dq.of(("spread",))[:, 0:32 * RB].rearrange("p (r h b) -> p r h b", r=RB, h=HEADS)
            for kq in range(4):
                q = slice(32 * kq, 32 * kq + 32)
                for h in range(HEADS):
                    ins = dve.tensor_copy(qb[q, :, :, 32 * kq + h], src[q, :, h, :].rearrange("p r b -> p b r"))
            dq.free(ins, ("spread",))
            dq.read(dve, ("spread",))
            dve.sem_inc(qb_done, 1)
            for k in range(2):
                dve.tensor_tensor(snew[:, k].rearrange("p (h b) -> p h b", h=HEADS), qlat[:, k].rearrange("p (h b) -> p h b", h=HEADS),
                                  smp[:, 48 + 8 * k:56 + 8 * k].unsqueeze(1).broadcast_to([P, HEADS, NB]), ALU.mult)
            dlink(dve, dve.memset(snew[:, 2], 0.0))
            for hh in range(2):
                r = half(hh)
                ins = dve.tensor_tensor(snew[r, 2].rearrange("p (r h b) -> p r h b", r=2, h=2)[:, :, hh, :],
                                        smp[r, 32:48].rearrange("p (r b) -> p r b", r=2), smp[r, 64:72].unsqueeze(1).broadcast_to([DK, 2, NB]), ALU.mult)
            ins.then_inc(sp_done, 1)
            dq.wait(dve, ("snew",))
            dq.free(dve.tensor_tensor(sn4[:], dq.of(("snew",))[0:4, 0:32].rearrange("p (h b) -> p h b", h=HEADS),
                                      const("diagh", 4).unsqueeze(2).broadcast_to([4, HEADS, NB]), ALU.mult), ("snew",))
            dq.read(dve, ("snew",))
            dlink(dve, dve.tensor_reduce(mg[:, 0], sn4[:].rearrange("p h b -> p b h"), AX.X, ALU.add))
            for u in range(NB):
                if u + 1 < NB:
                    pages_T(u + 1)
                ds.wait(dve, u)
                dve.tensor_reduce(mcol[:, u:u + 1], ds.of(u), AX.X, ALU.max).then_inc(max_done, 1)
                dq.wait(dve, ("mT", u))
                dq.free(dve.tensor_reduce(m4[0:1, 0:4], dq.of(("mT", u))[0:1, 0:P].rearrange("o (k h) -> o h k", k=4)[:, 0:4, :], AX.X, ALU.max), ("mT", u))
                dq.read(dve, ("mT", u))
                dve.tensor_scalar(mrow[0:1, u % 2, :, 0:4], m4[0:1, 0:4].unsqueeze(1).broadcast_to([1, 4, 4]), -SCALE, None, ALU.mult).then_inc(mrow_done, 1)
                dq.wait(dve, ("bias", u))
                dq.free(dve.tensor_copy(bias[:, u:u + 1], dq.of(("bias", u))[:, 0:1]), ("bias", u))
                dq.read(dve, ("bias", u))
                dve.sem_inc(bias_done, 1)
                ds.read(dve, u)
                if u >= 2:
                    dv.wait(dve, u - 2)
                dve.transpose(pet[:, u % 2].rearrange("p t c -> p (t c)"), pex[:, u % 2]).then_inc(pet_done, 1)
            dlink(dve, dve.tensor_scalar(mg[:, 0], mg[:, 0], SCALE, None, ALU.mult))
            dlink(dve, dve.tensor_scalar(mg[:, 1], bias[0:4, :], -1.0, None, ALU.mult))
            dlink(dve, dve.tensor_tensor(mg[:, 2], mg[:, 0], mg[:, 1], ALU.max))
            dve.tensor_tensor(mg[:, 3], mg[:, 1], mg[:, 2], ALU.subtract)
            dve.tensor_tensor(mg[:, 4], mg[:, 0], mg[:, 2], ALU.subtract).then_inc(mg_done, 1)
            dve.wait_ge(w_exp, 1)
            dq.wait(dve, ("lsum",))
            dq.free(dve.tensor_tensor(mg[:, 5], dq.of(("lsum",))[0:4, 0:NB], mg[:, 3], ALU.mult), ("lsum",))
            dq.read(dve, ("lsum",))
            dlink(dve, dve.tensor_tensor(mg[:, 6], mg[:, 5], mg[:, 4], ALU.add))
            dlink(dve, dve.reciprocal(mg[:, 7], mg[:, 6]))
            dve.tensor_tensor(mg[:, 8], mg[:, 3], mg[:, 7], ALU.mult)
            dlink(dve, dve.tensor_tensor(mg[:, 9], mg[:, 4], mg[:, 7], ALU.mult))
            dve.wait_ge(cnew_loaded, 16)
            for q in range(4):
                key = ("osum", q)
                dq.wait(dve, key)
                dq.free(dve.tensor_tensor(oacc[:, 2 * q:2 * q + 2, :], dq.of(key)[0:4, :].rearrange("p (b c) -> p b c", b=2),
                                          mg[:, 8, 2 * q:2 * q + 2].unsqueeze(2).broadcast_to([4, 2, KVR]), ALU.mult), key)
            dlink(dve, dve.tensor_tensor(cnew[:], cnew[:], mg[:, 9].unsqueeze(2).broadcast_to([4, NB, KVR]), ALU.mult))
            dq.read(dve, ("osum", 3))
            dve.tensor_tensor(oacc[:], oacc[:], cnew[:], ALU.add).then_inc(om_done, 1)
            dq.wait(dve, ("oT",))
            dq.free(dve.tensor_copy(olat[:].rearrange("p k b h -> p (k b h)"), dq.of(("oT",))[:, 0:64]), ("oT",))
            dq.wait(dve, ("uv",))
            dq.free(dve.tensor_copy(mixT[:, 0:4, TP:T], dq.of(("uv",))[:, 0:32].rearrange("p (h b) -> p h b", h=HEADS)), ("uv",))

        X1_AT = QB_AT
        x1h, x1l = (sb(X1_AT + i * KD * T, f"x1_{n}", [P, KD, T], F32R) for i, n in enumerate(("hi", "lo")))
        X1_END = X1_AT + 2 * KD * T
        WO_SLOTS = 5
        assert WO_SLOTS * D <= 4 * RB * P
        woraw = sb(X1_AT, "wout_raw", [P, WO_SLOTS, D])
        at = AREA
        woh, wol = (sb(at + i * 8192, f"wout_{n}", [P, KD, D], F32R) for i, n in enumerate(("hi", "lo"))); at += 16384
        mxh, mxl = (sb(at + i * 2048, f"mix_{n}", [P, 2, KD, P], F32R) for i, n in enumerate(("hi", "lo"))); at += 4096
        zrow = sb(at, "z_rows", [P, 2, D]); at += 2 * D
        assert at <= X1_AT
        x1t = sb(X1_END + 3072, "x1_tile", [P, KD, P])
        lst = sb(8 + CONST_W + 24, "ln1_stats", [P, 2, 24])
        wo_loaded = win_loaded + x_loaded
        WO_BASE = [16 * (NT // 3) + (16 if i == 0 else 0) for i in range(3)] + [16 * ((TT + 1 - i) // 2) for i in range(2)]
        xr_loaded = [sem(f"x_rows_loaded{i}") for i in range(2)]
        wo_hi, wo_lo, mx_hi, mx_lo, wo_mm, z_done, zv_done, zy_done, zn_done = (sem(n) for n in (
            "wout_hi_done", "wout_lo_done", "mix_hi_done", "mix_lo_done", "wout_multiplied", "z_done", "ln1_var", "ln1_lnexp", "ln1_normed"))
        z_tr, x1_read, x1_hi, x1_lo = (sem(n) for n in ("z_transposed", "x1_evacuated", "x1_hi_done", "x1_lo_done"))

        def load_wo(sp, k):
            sp.dma_start(woraw[:, k % WO_SLOTS, :], a["w_out"][0, k * P:(k + 1) * P, :]).then_inc(wo_loaded[k % WO_SLOTS], 16)

        def sp_out(sp):
            dq.read(sp, ("uv",))

            def load_x(t):
                n = tok(t)[1]
                src = a["x_prompt"][0, t * P:(t + 1) * P, :] if t < 8 else a["x_sample"].rearrange("b s d -> (b s) d")
                sp.dma_start(zrow[0:n, t % 2, :], src).then_inc(xr_loaded[t % 2], 16)

            load_x(0), load_x(1)
            for k in range(WO_SLOTS, KD):
                sp.wait_ge(wo_lo, k - WO_SLOTS + 1)
                load_wo(sp, k)
            for t in range(2, TT):
                sp.wait_ge(z_tr, t - 1)
                load_x(t)

        def z_bank(t):
            return 0 if t % 2 else 4

        def z_transpose(pe, u):
            n = tok(u)[1]
            pe.wait_ge(zn_done, u + 1)
            if u >= 2:
                pe.wait_ge(x1_read, u - 1)
            for k in range(KD):
                mm = pe.transpose(x1_bank(u)[:, k, 0:n], zrow[0:n, u % 2, k * P:(k + 1) * P], ident[0:n, 0:n])
            mm.then_inc(z_tr, 1)

        def pe_out(pe):
            for t in range(TT):
                n = tok(t)[1]
                pe.wait_ge(mx_lo, t + 1)
                if t >= 2:
                    pe.wait_ge(z_done, t - 1)
                for k in range(KD):
                    if t == 0:
                        pe.wait_ge(wo_lo, k + 1)
                    for i, (m, w) in enumerate(((mxh, woh), (mxh, wol), (mxl, woh))):
                        for c in range(2):
                            mm = pe.matmul(psum[0:n, z_bank(t) + c, :], m[:, t % 2, k, 0:n], w[:, k, c * 512:c * 512 + 512],
                                           start=(k == 0 and i == 0), stop=(k == KD - 1 and i == 2))
                mm.then_inc(wo_mm, 1)
                u = t - 1
                if u >= 0:
                    z_transpose(pe, u)

        def x1_bank(t):
            b = 2 if t % 2 else 6
            return psum[:, b:b + 2, :].rearrange("p b (k c) -> p (b k) c", c=P)

        def x1_evac(eng, t):
            eng.wait_ge(x1_read, t + 1)

        def act_out(act):
            dq.read(act, ("uv",))

            def mix_hi(t):
                c0, n = tok(t)
                if t >= 2:
                    act.wait_ge(wo_mm, t - 1)
                act.activation(mxh[:, t % 2, :, 0:n], mixT[:, :, c0:c0 + n], ACT.Copy).then_inc(mx_hi, 1)

            mix_hi(0)
            for k in range(KD):
                act.wait_ge(wo_loaded[k % WO_SLOTS], WO_BASE[k % WO_SLOTS] + 16 * (k // WO_SLOTS + 1))
                act.activation(woh[:, k, :], woraw[:, k % WO_SLOTS, :], ACT.Copy).then_inc(wo_hi, 1)
            mix_hi(1)
            for t in range(TT):
                c0, n = tok(t)
                act.wait_ge(zv_done, t + 1)
                s = lst[0:n, t % 2]
                act.activation(s[:, 17:18], s[:, 16:17], ACT.Sqrt).then_inc(zy_done, 1)
                if t + 2 < TT:
                    mix_hi(t + 2)
                if t == TT - 1:
                    act_w1_first(act)
                act.wait_ge(z_tr, t + 1)
                if t >= 1:
                    act.wait_ge(x1_lo, t)
                for k in range(KD):
                    ins = act.activation(x1t[:, k, 0:n], x1_bank(t)[:, k, 0:n], ACT.Identity, scale=cols[:, L1G + k:L1G + k + 1],
                                         bias=cols[:, L1B + k:L1B + k + 1])
                ins.then_inc(x1_read, 1)
                act.wait_ge(x1_read, t + 1)
                act.activation(x1h[:, :, c0:c0 + n], x1t[:, :, 0:n], ACT.Copy).then_inc(x1_hi, 1)

        def dve_out(dve):
            dq.read(dve, ("uv",))

            def mix_lo(t):
                c0, n = tok(t)
                dve.wait_ge(mx_hi, t + 1)
                dve.tensor_tensor(mxl[:, t % 2, :, 0:n], mixT[:, :, c0:c0 + n], mxh[:, t % 2, :, 0:n].bitcast(F32), ALU.subtract).then_inc(mx_lo, 1)

            mix_lo(0)
            for k in range(KD):
                dve.wait_ge(wo_hi, k + 1)
                dve.tensor_tensor(wol[:, k, :], woraw[:, k % WO_SLOTS, :], woh[:, k, :].bitcast(F32), ALU.subtract).then_inc(wo_lo, 1)
            mix_lo(1)
            for t in range(TT + 1):
                if t < TT:
                    n = tok(t)[1]
                    z, s = zrow[0:n, t % 2, :], lst[0:n, t % 2]
                    dve.wait_ge(xr_loaded[t % 2], 16 * (t // 2 + 1))
                    dve.wait_ge(wo_mm, t + 1)
                    ins = dve.scalar_tensor_tensor(z.rearrange("p (c d) -> p c d", c=2), z.rearrange("p (c d) -> p c d", c=2), ALPHA,
                                                   psum[0:n, z_bank(t):z_bank(t) + 2, :], ALU.mult, ALU.add)
                    ins.then_inc(z_done, 1)
                    dve.wait_ge(z_done, t + 1)
                    norm_stats(dve, z[:, 0:512], z[:, 512:1024], s)
                    dlink(dve, dve.tensor_scalar(s[:, 15:16], s[:, 13:14], EPS, None, ALU.add))
                    dve.reciprocal(s[:, 16:17], s[:, 15:16]).then_inc(zv_done, 1)
                    dve.wait_ge(zy_done, t + 1)
                    newton(dve, s[:, 17:18], s[:, 15:16], s[:, 18:19])
                    dve.tensor_scalar(z, z, s[:, 12:13], s[:, 17:18], ALU.subtract, ALU.mult).then_inc(zn_done, 1)
                    if t + 2 < TT:
                        mix_lo(t + 2)
                u = t - 1
                if u >= 0:
                    c0, n = tok(u)
                    dve.wait_ge(x1_hi, u + 1)
                    dve.tensor_tensor(x1l[:, :, c0:c0 + n], x1t[:, :, 0:n], x1h[:, :, c0:c0 + n].bitcast(F32), ALU.subtract).then_inc(x1_lo, 1)
                if t == TT - 1:
                    dve_w1_first(dve)

        def norm_stats(dve, z0, z1, s):
            dve.bn_stats(s[:, 0:6], z0)
            dlink(dve, dve.bn_stats(s[:, 6:12], z1))
            dlink(dve, dve.bn_aggr(s[:, 12:14], s[:, 0:12]))

        GF = 4
        GROUPS = DFF // (GF * P)
        ym = sb(PERSIST, "y_sum", [P, KD, T])
        at = AREA
        w1h, w1l = (sb(at + i * 2048, f"w1_{n}", [P, 2, KD, P], F32R) for i, n in enumerate(("hi", "lo"))); at += 4096
        w2h, w2l = (sb(at + i * 4096, f"w2_{n}", [P, GF, D], F32R) for i, n in enumerate(("hi", "lo"))); at += 8192
        hh_, hl_ = (sb(at + i * GF * T, f"hid_{n}", [P, GF, T], F32R) for i, n in enumerate(("hi", "lo"))); at += 2 * GF * T
        assert at <= X1_AT
        raw = sb(X1_END, "mlp_raw", [P, 2, D])
        ht = sb(X1_END + 2 * D, "hid_tmp", [P, 2, T])
        assert X1_END + 2 * D + 2 * T <= 53200
        g2 = sb(AREA, "ln2_g_rows", [P, D]); b2 = sb(AREA + D, "ln2_b_rows", [P, D])
        lst2 = sb(AREA + 2 * D, "ln2_stats", [P, 3, 24])
        yrow = sb(X1_END, "y_rows", [P, 3, D])
        raw_loaded = [sem(f"mlp_raw_loaded{i}") for i in range(2)]
        mw_hi, mw_lo, set_full, h_free, y_free, h_done, h_hi, h_lo = (sem(n) for n in (
            "mlp_w_hi", "mlp_w_lo", "mlp_set_full", "hid_set_read", "out_set_read", "hid_done", "hid_hi", "hid_lo"))
        ITEMS = [("w1", 2), ("w2", 0), ("w1", 3), ("w2", 1), ("w2", 2), ("w2", 3), ("w1n", 0), ("w1n", 1)]

        def item(kind, i):
            return (w1h[:, i % 2], w1l[:, i % 2]) if kind[:2] == "w1" else (w2h[:, i], w2l[:, i])

        def raw_view(kind, s):
            return raw[:, s, :].rearrange("p (k c) -> p k c", k=KD) if kind[:2] == "w1" else raw[:, s, :]

        def dve_mlp_start(dve):
            dve.sem_inc(mw_lo, 2)

        def sp_mlp(sp):
            w1 = a["w1"].rearrange("l (k p) f -> p (l k) f", p=P)

            def load(kind, i, g, j):
                sp.wait_ge(mw_lo, j + 1)
                if kind == "w2":
                    src = a["w2"][0, bass.ds((g * GF + i) * P, P), :]
                else:
                    gg = g + 1 if kind == "w1n" else g
                    src = w1[:, :, bass.ds((gg * GF + i) * P, P)]
                sp.dma_start(raw_view(kind, i_slot), src).then_inc(raw_loaded[i_slot], 16)

            for i_slot in range(2):
                load("w1", i_slot, 0, i_slot)
            with sp.Fori(0, GROUPS - 1) as g:
                for n, (kind, i) in enumerate(ITEMS):
                    i_slot = n % 2
                    load(kind, i, g, 8 * g + n + 2)
            for n, (kind, i) in enumerate(ITEMS[:6]):
                i_slot = n % 2
                load(kind, i, GROUPS - 1, 8 * (GROUPS - 1) + n + 2)

        def mlp_set(j):
            return psum[:, 3 * (j % 2):3 * (j % 2) + 3, 0:BLK]

        def pe_group(pe, g, first, last):
            if first:
                pe.wait_ge(mw_lo, 3)
                for b in range(3):
                    if b == 2:
                        z_transpose(pe, TT - 1)
                        x1_evac(pe, TT - 2)
                    pe.wait_ge(x1_lo, min(-(-(b + 1) * BLK // P), TT))
                    for k in range(KD):
                        for n, (w, x) in enumerate(((w1h, x1h), (w1h, x1l), (w1l, x1h))):
                            mm = pe.matmul(psum[:, b, 0:BLK], w[:, 0, k], x[:, k, b * BLK:(b + 1) * BLK],
                                           start=(k == 0 and n == 0), stop=(k == KD - 1 and n == 2))
                mm.then_inc(set_full, 1)
            for i in range(1 if first else 0, GF):
                pe.wait_ge(mw_lo, 8 * g + {0: 1, 1: 2, 2: 3, 3: 5}[i] + 2)
                if i < 2:
                    pe.wait_ge(y_free, KD * g + i + 1)
                else:
                    pe.wait_ge(h_free, GF * g + i - 1)
                for k in range(KD):
                    for n, (w, x) in enumerate(((w1h, x1h), (w1h, x1l), (w1l, x1h))):
                        for b in range(3):
                            mm = pe.matmul(psum[:, 3 * (i % 2) + b, 0:BLK], w[:, i % 2, k], x[:, k, b * BLK:(b + 1) * BLK],
                                           start=(k == 0 and n == 0), stop=(k == KD - 1 and n == 2))
                mm.then_inc(set_full, 1)
            if last:
                return
            for m in range(KD):
                if m < 2:
                    pe.wait_ge(h_free, GF * g + m + 3)
                else:
                    pe.wait_ge(y_free, KD * g + m + 1)
                for k in range(GF):
                    if m == 0:
                        pe.wait_ge(mw_lo, 8 * g + {0: 4, 1: 6, 2: 7, 3: 8}[k] + 2)
                        pe.wait_ge(h_lo, GF * g + k + 1)
                    for n, (w, x) in enumerate(((w2h, hh_), (w2h, hl_), (w2l, hh_))):
                        for b in range(3):
                            mm = pe.matmul(psum[:, 3 * (m % 2) + b, 0:BLK], w[:, k, m * P:(m + 1) * P], x[:, k, b * BLK:(b + 1) * BLK],
                                           start=(k == 0 and n == 0), stop=(k == GF - 1 and n == 2))
                mm.then_inc(set_full, 1)

        def pe_mlp(pe):
            pe_group(pe, 0, True, False)
            with pe.Fori(1, GROUPS - 1) as g:
                pe_group(pe, g, False, False)
            pe_group(pe, GROUPS - 1, False, True)

        AFTER = {0: (0, 1), 1: (2, 3), 2: (4, 5), 3: (6, 7)}

        def act_group(act, g, first, last):
            for i in range(GF):
                act.wait_ge(set_full, 12 * g + i + 1)
                if i >= 2 or not first:
                    act.wait_ge(h_lo, GF * g + i - 1)
                act.activation(ht[:, i % 2, :].rearrange("p (b c) -> p b c", b=3), mlp_set(i), ACT.Relu).then_inc(h_free, 1)
                for n in AFTER[i]:
                    kind, j = ITEMS[n]
                    if last and n >= 6:
                        continue
                    act.wait_ge(raw_loaded[n % 2], 16 * (4 * g + n // 2 + 2))
                    if kind == "w2" and not first:
                        act.wait_ge(set_full, 12 * g)
                    elif kind == "w1":
                        act.wait_ge(set_full, 12 * g + j - 1)
                    elif kind == "w1n":
                        act.wait_ge(set_full, 12 * g + j + 3)
                    act.activation(item(kind, j)[0], raw_view(kind, n % 2), ACT.Copy).then_inc(mw_hi, 1)
                act.wait_ge(h_done, GF * g + i + 1)
                act.activation(hh_[:, i, :], ht[:, i % 2, :], ACT.Copy).then_inc(h_hi, 1)

        def act_w1_first(act):
            act.wait_ge(wo_mm, TT)
            for i in range(2):
                act.wait_ge(raw_loaded[i], 16)
                act.activation(item("w1", i)[0], raw_view("w1", i), ACT.Copy).then_inc(mw_hi, 1)

        def act_mlp(act):
            act_group(act, 0, True, False)
            with act.Fori(1, GROUPS - 1) as g:
                act_group(act, g, False, False)
            act_group(act, GROUPS - 1, False, True)

        def dve_group(dve, g, last):
            for i in range(GF):
                dve.wait_ge(h_free, GF * g + i + 1)
                dve.tensor_tensor(ht[:, i % 2, :], ht[:, i % 2, :], ht[:, i % 2, :], ALU.mult).then_inc(h_done, 1)
                for n in AFTER[i]:
                    if not (last and n >= 6):
                        kind, j = ITEMS[n]
                        dve.wait_ge(mw_hi, 8 * g + n + 3)
                        dve.tensor_tensor(item(kind, j)[1], raw_view(kind, n % 2), item(kind, j)[0].bitcast(F32), ALU.subtract).then_inc(mw_lo, 1)
                dve.wait_ge(h_hi, GF * g + i + 1)
                dve.tensor_tensor(hl_[:, i, :], ht[:, i % 2, :], hh_[:, i, :].bitcast(F32), ALU.subtract).then_inc(h_lo, 1)
            if last:
                return
            for m in range(KD):
                dve.wait_ge(set_full, 12 * g + GF + m + 1)
                y = ym[:, m, :].rearrange("p (b c) -> p b c", b=3)
                dve.tensor_tensor(y, y, mlp_set(m), ALU.add).then_inc(y_free, 1)
            dve.wait_ge(y_free, KD * g + KD + 2)

        def dve_w1_first(dve):
            for i in range(2):
                dve.wait_ge(mw_hi, i + 1)
                dve.tensor_tensor(item("w1", i)[1], raw_view("w1", i), item("w1", i)[0].bitcast(F32), ALU.subtract).then_inc(mw_lo, 1)

        def dve_mlp(dve):
            dve.sem_inc(y_free, 2)
            dve.wait_ge(x1_lo, TT)
            dlink(dve, dve.tensor_tensor(ym[:], x1h[:].bitcast(F32), x1l[:].bitcast(F32), ALU.add))
            dlink(dve, dve.tensor_scalar(ym[:], ym[:], ALPHA, None, ALU.mult))
            with dve.Fori(0, GROUPS - 1) as g:
                dve_group(dve, g, False)
            dve_group(dve, GROUPS - 1, True)

        G1 = GROUPS - 1
        L_TASKS, LN_AFTER = [], {0: [0, 1], 1: [2, 3, 4], 2: [5, 6, 7, 8]}
        for b in range(3):
            L_TASKS += [(b, m) for m in range(KD)]
        lb = Banks("last_out_bank", [0, 1, 2, 3], L_TASKS, after=dq)
        yt_full, yn_done, yrow_done, ln2_loaded = sem("y_transposed"), sem("y_bank_read"), sem("y_rows_done"), sem("ln2_rows_loaded")
        yscaled, yrow_dve = sem("y_rows_scaled"), sem("y_rows_done_by_vector")
        yv_done, yy_done, yg_done = sem("ln2_var"), sem("ln2_lnexp"), sem("ln2_scaled")
        y_stored, Y_BASE = proj_stored, 16 * (NT // 3)

        def y_bank(t):
            return psum[:, 4 + 2 * (t % 2):6 + 2 * (t % 2), :]

        def pe_last(pe):
            pe.wait_ge(h_free, GF * G1 + GF)
            first = True

            def turn(t):
                c0, n = tok(t)
                if t >= 2:
                    pe.wait_ge(yn_done, t - 1)
                for k in range(KD):
                    mm = pe.transpose(y_bank(t)[0:n, k // 4, (k % 4) * P:(k % 4 + 1) * P], ym[:, k, c0:c0 + n], ident)
                mm.then_inc(yt_full, 1)

            for b in range(3):
                for m in range(KD):
                    key = (b, m)
                    lb.begin(pe, key)
                    for k in range(GF):
                        if first and m == 0:
                            pe.wait_ge(mw_lo, 8 * G1 + {0: 4, 1: 6, 2: 7, 3: 8}[k] + 2)
                            pe.wait_ge(h_lo, GF * G1 + k + 1)
                        for n, (w, x) in enumerate(((w2h, hh_), (w2h, hl_), (w2l, hh_))):
                            mm = pe.matmul(lb.of(key)[:, 0:BLK], w[:, k, m * P:(m + 1) * P], x[:, k, b * BLK:(b + 1) * BLK],
                                           start=(k == 0 and n == 0), stop=(k == GF - 1 and n == 2))
                    first = False
                    lb.full(mm)
                    if b and m in (1, 3, 5) and (m - 1) // 2 < len(LN_AFTER[b - 1]):
                        if m == 1:
                            for q in range(4):
                                lb.read(pe, (b - 1, KD - 4 + q))
                        turn(LN_AFTER[b - 1][(m - 1) // 2])
            for q in range(4):
                lb.read(pe, (2, KD - 4 + q))
            for t in LN_AFTER[2]:
                turn(t)

        DVE_ROWS = [6, 8]
        POOL_ROWS = [t for t in range(TT) if t not in DVE_ROWS]

        def pool_last(pool):
            pool.wait_ge(ln2_loaded, 32)
            for i, t in enumerate(POOL_ROWS):
                n = tok(t)[1]
                z = yrow[0:n, t % 3, :]
                pool.wait_ge(yn_done, t + 1)
                pool.tensor_tensor(z, z, g2[0:n, :], ALU.mult).then_inc(yscaled, 1)
                pool.wait_ge(yscaled, i + 1)
                pool.tensor_tensor(z, z, b2[0:n, :], ALU.add).then_inc(yrow_done, 1)

        def dve_last(dve):

            def rows(t):
                n = tok(t)[1]
                z, s = yrow[0:n, t % 3, :], lst2[0:n, t % 3]
                dve.wait_ge(yt_full, t + 1)
                if t >= 3:
                    dve.wait_ge(y_stored[t % 3], Y_BASE + 16 * (t // 3))
                norm_stats(dve, y_bank(t)[0:n, 0, :], y_bank(t)[0:n, 1, :], s)
                dlink(dve, dve.tensor_scalar(s[:, 15:16], s[:, 13:14], EPS, None, ALU.add))
                dve.reciprocal(s[:, 16:17], s[:, 15:16]).then_inc(yv_done, 1)
                dve.wait_ge(yy_done, t + 1)
                newton(dve, s[:, 17:18], s[:, 15:16], s[:, 18:19])
                dve.scalar_tensor_tensor(s[:, 19:20], s[:, 12:13], -1.0, s[:, 17:18], ALU.mult, ALU.mult).then_inc(yg_done, 1)

            for b in range(3):
                for m in range(KD):
                    key = (b, m)
                    lb.wait(dve, key)
                    c = slice(b * BLK, (b + 1) * BLK)
                    lb.free(dve.tensor_tensor(ym[:, m, c], ym[:, m, c], lb.of(key)[:, 0:BLK], ALU.add), key)
                    if b and m in (2, 4, 6) and (m - 2) // 2 < len(LN_AFTER[b - 1]):
                        rows(LN_AFTER[b - 1][(m - 2) // 2])
            def scaled(t):
                n = tok(t)[1]
                z = yrow[0:n, t % 3, :]
                dve.wait_ge(ln2_loaded, 32)
                dve.wait_ge(yn_done, t + 1)
                dlink(dve, dve.tensor_tensor(z, z, g2[0:n, :], ALU.mult))
                dve.tensor_tensor(z, z, b2[0:n, :], ALU.add).then_inc(yrow_dve, 1)

            for t in LN_AFTER[2]:
                rows(t)
                if t - 1 in DVE_ROWS:
                    scaled(t - 1)
            scaled(TT - 1)

        def act_last(act):
            for t in range(TT):
                n = tok(t)[1]
                s = lst2[0:n, t % 3]
                act.wait_ge(yv_done, t + 1)
                act.activation(s[:, 17:18], s[:, 16:17], ACT.Sqrt).then_inc(yy_done, 1)
                act.wait_ge(yg_done, t + 1)
                act.activation(yrow[0:n, t % 3, :].rearrange("p (c d) -> p c d", c=2), y_bank(t)[0:n], ACT.Identity,
                               scale=s[:, 17:18], bias=s[:, 19:20]).then_inc(yn_done, 1)

        def sp_last(sp):
            sp.wait_ge(set_full, 12 * G1 + GF)
            sp.wait_ge(mw_lo, 8 * G1 + 10)
            sp.dma_start(g2[:], a["ln2_g"].broadcast_to([P, D])).then_inc(ln2_loaded, 16)
            sp.dma_start(b2[:], a["ln2_b"].broadcast_to([P, D])).then_inc(ln2_loaded, 16)
            for t in range(TT):
                n = tok(t)[1]
                dst = out["y_prompt"][0, t * P:(t + 1) * P, :] if t < 8 else out["y_sample"].rearrange("b s d -> (b s) d")
                if t in DVE_ROWS:
                    sp.wait_ge(yrow_dve, DVE_ROWS.index(t) + 1)
                else:
                    sp.wait_ge(yrow_done, POOL_ROWS.index(t) + 1)
                sp.dma_start(dst, yrow[0:n, t % 3, :]).then_inc(y_stored[t % 3], 16)
            for i in range(3):
                sp.wait_ge(y_stored[i], Y_BASE + 48)
            sp.wait_ge(gst_stored, 48)
            sp.wait_ge(rows_stored, 64)

        SP = [sp_project, sp_gla, sp_mla_in, sp_mla, sp_decode, sp_out, sp_mlp, sp_last]
        PE = [pe_project, pe_gla, pe_mla_in, pe_mla, pe_decode, pe_out, pe_mlp, pe_last]
        AC = [act_project, act_gla, act_mla_in, act_mla, act_decode, act_out, act_mlp, act_last]
        DV_ = [dve_gla_early, dve_project, dve_gla, dve_mla_in, dve_mla, dve_decode, dve_mlp_start, dve_out, dve_mlp, dve_last]

        block = ctx.enter_context(nc.Block())

        @block.sync
        def _(sp):
            for stage in SP:
                stage(sp)

        @block.tensor
        def _(pe):
            for stage in PE:
                stage(pe)

        @block.scalar
        def _(act):
            for stage in AC:
                stage(act)

        @block.vector
        def _(dve):
            for stage in DV_:
                stage(dve)

        @block.gpsimd
        def _(pool):
            pool_mla_in(pool)
            pool_decode(pool)
            pool_last(pool)


def _tables():
    import numpy as np

    c = np.zeros((P, CONST_W), np.float32)

    def put(name, v):
        at, w = CONST_COLS[name]
        c[:, at:at + w] = v

    i, j = np.arange(P)[:, None], np.arange(P)[None, :]
    put("ident", i == j)
    put("swap", (i ^ (ROPE // 2)) == j)
    same = i // CH == j // CH
    put("tri16", (same & (i <= j)) / 16.0)
    put("chunkmask", same & (i <= j))
    put("causal", np.where(j <= i, 0.0, NEG))
    put("spread", np.concatenate([(i // 32 == q) & (i % 32 == j % 32) for q in range(4)], 1))
    put("ones", 1.0)
    put("dup", (i < ROPE) & (j % ROPE == i))
    put("swapdup", (i < ROPE) & ((j % ROPE) ^ (ROPE // 2) == i))
    h = np.arange(4)[None, :]
    put("sumkq", i % 32 == h)
    put("diagh", i == h)
    inv = 10000.0 ** (-np.arange(0, ROPE, 2, dtype=np.float64) / ROPE)
    pos = np.concatenate([np.arange(TP), np.full(NB, PAST)]).astype(np.float32)
    ang = (pos[None, :] * inv.astype(np.float32)[:, None]).astype(np.float64)
    cos, sin = np.cos(ang).astype(np.float32), np.sin(ang).astype(np.float32)
    rope = np.stack([np.concatenate([cos] * 4), np.concatenate([-sin, sin] * 2)], 1)
    return c, rope.reshape(P, 2 * T)


_OUTS = dict(
    y_prompt=(1, TP, D), y_sample=(NB, 1, D), ckv_prompt=(1, 1, TP, KVR), krope_prompt=(1, 1, TP, ROPE),
    gla_prompt=(1, 1, HEADS, DK, DV), ckv_sample=(1, NB, 1, KVR), krope_sample=(1, NB, 1, ROPE),
    gla_sample=(1, NB, HEADS, DK, DV))


def kernel(x_prompt, x_sample, cache_ckv, cache_krope, state_gla, page_table, w_in, mla_q_norm, mla_w_uq,
           mla_kv_norm, mla_w_uk, mla_w_uv, gla_w_gate2, gla_b_gate, gla_norm, w_out, ln1_g, ln1_b,
           mlp_w1, mlp_w2, ln2_g, ln2_b):
    import numpy as np
    import concourse.bacc as bacc
    from concourse.bass_utils import run_bass_kernel_spmd

    def columns(v):
        return np.ascontiguousarray(np.asarray(v).reshape(-1, P).T)

    consts, rope = _tables()
    cols = np.zeros((P, 24), np.float32)
    for at, v in ((0, mla_q_norm), (3, mla_kv_norm), (5, gla_norm), (6, ln1_g), (14, ln1_b)):
        c = columns(v)
        cols[:, at:at + c.shape[1]] = c
    arrays = dict(
        x_prompt=x_prompt, x_sample=x_sample, cache_ckv=cache_ckv, cache_krope=cache_krope, state_gla=state_gla,
        page_table=page_table, w_in=w_in, w_uq=mla_w_uq, w_uk=mla_w_uk, w_uv=mla_w_uv, w_gate2=gla_w_gate2,
        b_gate=gla_b_gate, w_out=w_out, w1=mlp_w1, w2=mlp_w2, ln2_g=ln2_g, ln2_b=ln2_b,
        consts=consts, rope=rope, cols=cols)
    arrays = {k: np.ascontiguousarray(v) for k, v in arrays.items()}
    nc = bacc.Bacc("TRN2", target_bir_lowering=False, num_devices=1)
    a = {k: nc.dram_tensor("in_" + k, v.shape, mybir.dt.from_np(v.dtype), kind="ExternalInput").ap()
         for k, v in arrays.items()}
    out = {k: nc.dram_tensor("out_" + k, s, F32, kind="ExternalOutput").ap() for k, s in _OUTS.items()}
    scratch = nc.dram_tensor("scratch", (NT, P, T), F32, kind="Internal").ap()
    hymba_step(nc, a, out, scratch)
    r = run_bass_kernel_spmd(nc, [{"in_" + k: v for k, v in arrays.items()}], core_ids=[0])
    return tuple(r.results[0]["out_" + k] for k in _OUTS)
```
